# Optimizing a Trainium2 kernel written in Bass

```python
import math
import jax, jax.numpy as jnp
from jax import lax
import numpy as np

D_MODEL = 1024
BATCH = 1
SEQ = 256
DEPTH = 2
DEC_BATCH = 8
DEC_SEQ = 4
PAST_LEN = 2048
PAGE_SIZE = 128

D_MIX = 2 * D_MODEL
D_POOL = D_MIX // 4
POOL_WINDOWS = (2, 4, 8, 16)
POOL_GROUPS = len(POOL_WINDOWS)
POOL_GROUP = D_POOL // POOL_GROUPS
POOL_BUF = max(POOL_WINDOWS) - 1
D_SSM = D_MIX - D_POOL
HEAD_DIM = 64
N_HEADS = D_SSM // HEAD_DIM
N_GROUPS = 4
HEADS_PER_GROUP = N_HEADS // N_GROUPS
D_STATE = 128
CONV_W = 4
CHUNK = 128
D_XBC = D_SSM + 2 * N_GROUPS * D_STATE
D_IN_PROJ = D_POOL + D_SSM + D_XBC + N_HEADS
D_FF = 2816
N_EXPERTS = 8
TOP_K = 2
D_FF_EXPERT = 2816
N_DENSE = (DEPTH + 1) // 2
N_MOE = DEPTH // 2
ALPHA = (2.0 * DEPTH) ** 0.25
BETA = (8.0 * DEPTH) ** -0.25
LN_EPS = 1e-5
RMS_EPS = 1e-6

kernel_name = "pool_ssd_hybrid_decode_step"

def layer_norm(x, g, b):
    xf = x.astype(jnp.float32)
    mu = jnp.mean(xf, -1, keepdims=True)
    var = jnp.mean(jnp.square(xf - mu), -1, keepdims=True)
    return ((xf - mu) * lax.rsqrt(var + LN_EPS) * g + b).astype(x.dtype)

def pool_mixer(u, buf, start, w, scale):
    bsz, L, _ = u.shape
    up = jnp.concatenate([buf.astype(u.dtype), u], axis=1).astype(jnp.float32)
    cs = jnp.concatenate([jnp.zeros_like(up[:, :1]), jnp.cumsum(up, axis=1)], axis=1)
    hi = cs[:, POOL_BUF + 1:]
    pos = start + jnp.arange(L, dtype=jnp.int32)
    means = []
    for g, win in enumerate(POOL_WINDOWS):
        sl = slice(g * POOL_GROUP, (g + 1) * POOL_GROUP)
        lo = cs[:, POOL_BUF + 1 - win:POOL_BUF + 1 - win + L, sl]
        cnt = jnp.minimum(pos + 1, win).astype(jnp.float32)
        means.append((hi[:, :, sl] - lo) / cnt[None, :, None])
    mean = jnp.concatenate(means, axis=-1)
    diff = (mean - up[:, POOL_BUF:]).reshape(bsz, L, POOL_GROUPS, POOL_GROUP).astype(u.dtype)
    out = jnp.einsum('blgc,gcd->blgd', diff, w).reshape(bsz, L, D_POOL) * scale
    new_buf = up[:, -POOL_BUF:].astype(buf.dtype)
    return out.astype(u.dtype), new_buf

def ssd_scan(x, dt, A, Bm, Cm, h0):
    bsz, L = x.shape[:2]
    Q = min(CHUNK, L)
    pad = (-L) % Q
    if pad:
        def pw(a):
            return jnp.pad(a, [(0, 0), (0, pad)] + [(0, 0)] * (a.ndim - 2))
        x, dt, Bm, Cm = pw(x), pw(dt), pw(Bm), pw(Cm)
    nc = (L + pad) // Q
    G, R, P, N = N_GROUPS, HEADS_PER_GROUP, HEAD_DIM, D_STATE
    xc = x.reshape(bsz, nc, Q, G, R, P).astype(jnp.float32)
    dtc = dt.reshape(bsz, nc, Q, G, R)
    Bc = Bm.reshape(bsz, nc, Q, G, N).astype(jnp.float32)
    Cc = Cm.reshape(bsz, nc, Q, G, N).astype(jnp.float32)
    cum = jnp.cumsum(dtc * A.reshape(G, R), axis=2)
    seg = cum[:, :, :, None] - cum[:, :, None]
    causal = jnp.tril(jnp.ones((Q, Q), dtype=bool))[:, :, None, None]
    decay = jnp.exp(jnp.where(causal, seg, -jnp.inf))
    cb = jnp.einsum('bcign,bcjgn->bcijg', Cc, Bc)
    mix = cb[..., None] * decay * dtc[:, :, None]
    y_diag = jnp.einsum('bcijgr,bcjgrp->bcigrp', mix, xc)
    wx = (jnp.exp(cum[:, :, -1:] - cum) * dtc)[..., None] * xc
    chunk_states = jnp.einsum('bcjgn,bcjgrp->bcgrpn', Bc, wx)
    chunk_decay = jnp.exp(cum[:, :, -1])

    def step(h, inp):
        s, d = inp
        return h * d[..., None, None] + s, h

    hT, h_starts = lax.scan(step, h0.reshape(bsz, G, R, P, N).astype(jnp.float32),
                            (jnp.moveaxis(chunk_states, 1, 0), jnp.moveaxis(chunk_decay, 1, 0)))
    h_starts = jnp.moveaxis(h_starts, 0, 1)
    y_off = jnp.einsum('bcign,bcgrpn->bcigrp', Cc, h_starts) * jnp.exp(cum)[..., None]
    y = (y_diag + y_off).reshape(bsz, nc * Q, N_HEADS, P)[:, :L]
    return y, hT.reshape(bsz, N_HEADS, P, N)

def ssd_mixer(z, xbc, dt_raw, conv_buf, h0, conv_w, conv_b, dt_bias, A_log, D_skip, norm_w):
    bsz, L, _ = xbc.shape
    xpad = jnp.concatenate([conv_buf.astype(xbc.dtype), xbc], axis=1)
    acc = conv_b + xpad[:, 0:L] * conv_w[0]
    for k in range(1, CONV_W):
        acc = acc + xpad[:, k:k + L] * conv_w[k]
    xbc_act = jax.nn.silu(acc)
    xs, Bm, Cm = jnp.split(xbc_act, [D_SSM, D_SSM + N_GROUPS * D_STATE], axis=-1)
    xs = xs.reshape(bsz, L, N_HEADS, HEAD_DIM)
    dt = jax.nn.softplus(dt_raw.astype(jnp.float32) + dt_bias.astype(jnp.float32))
    A = -jnp.exp(A_log.astype(jnp.float32))
    y, hT = ssd_scan(xs, dt, A, Bm.reshape(bsz, L, N_GROUPS, D_STATE),
                     Cm.reshape(bsz, L, N_GROUPS, D_STATE), h0)
    y = y + xs.astype(jnp.float32) * D_skip.astype(jnp.float32)[:, None]
    g = y.reshape(bsz, L, D_SSM) * jax.nn.silu(z.astype(jnp.float32))
    g = g.reshape(bsz, L, N_GROUPS, D_SSM // N_GROUPS)
    g = g * lax.rsqrt(jnp.mean(jnp.square(g), -1, keepdims=True) + RMS_EPS)
    out = (g.reshape(bsz, L, D_SSM) * norm_w).astype(z.dtype)
    new_conv = xpad[:, -(CONV_W - 1):].astype(conv_buf.dtype)
    return out, new_conv, hT.astype(h0.dtype)

def swiglu(h, wg, wu, wd):
    return (jax.nn.silu(h @ wg) * (h @ wu)) @ wd

def moe_swiglu(h, rw, rb, wg, wu, wd):
    logits = (h @ rw).astype(jnp.float32) + rb
    top_v, top_i = lax.top_k(logits, TOP_K)
    gates = jax.nn.softmax(top_v, axis=-1)
    out = jnp.zeros_like(h)
    for e in range(N_EXPERTS):
        ge = jnp.sum(jnp.where(top_i == e, gates, 0.0), axis=-1)
        out = out + ge[..., None].astype(h.dtype) * swiglu(h, wg[e], wu[e], wd[e])
    return out

def trunk(x, start, pool_bufs, conv_bufs, ssm_states, params):
    (w_in, conv_w, conv_b, dt_bias, A_log, D_skip, ssm_norm_w, pool_w, pool_scale, w_out,
     ln1_g, ln1_b, ln2_g, ln2_b, ffn_w_gate, ffn_w_up, ffn_w_down,
     router_w, router_b, moe_w_gate, moe_w_up, moe_w_down) = params
    new_pool, new_conv, new_ssm = [], [], []
    for l in range(DEPTH):
        proj = x @ w_in[l]
        u, z, xbc, dt_raw = jnp.split(proj, [D_POOL, D_POOL + D_SSM, D_POOL + D_SSM + D_XBC], axis=-1)
        pool_out, pb = pool_mixer(u, pool_bufs[l], start, pool_w[l], pool_scale[l])
        ssd_out, cbuf, sh = ssd_mixer(z, xbc, dt_raw, conv_bufs[l], ssm_states[l], conv_w[l], conv_b[l],
                                      dt_bias[l], A_log[l], D_skip[l], ssm_norm_w[l])
        mixed = jnp.concatenate([pool_out, ssd_out], axis=-1) @ w_out[l]
        x = layer_norm(ALPHA * x + mixed, ln1_g[l], ln1_b[l])
        j = l // 2
        if l % 2 == 0:
            f = swiglu(x, ffn_w_gate[j], ffn_w_up[j], ffn_w_down[j])
        else:
            f = moe_swiglu(x, router_w[j], router_b[j], moe_w_gate[j], moe_w_up[j], moe_w_down[j])
        x = layer_norm(ALPHA * x + f, ln2_g[l], ln2_b[l])
        new_pool.append(pb)
        new_conv.append(cbuf)
        new_ssm.append(sh)
    return x, jnp.stack(new_pool), jnp.stack(new_conv), jnp.stack(new_ssm)

def setup_inputs(seed: int = 0) -> dict:
    key = jax.random.key(seed)
    ks = jax.random.split(key, 32)
    f32 = jnp.float32

    def nrm(k, shape, scale):
        return jax.random.normal(k, shape, f32) * scale

    dt0 = jnp.exp(jax.random.uniform(ks[8], (DEPTH, N_HEADS), f32, math.log(1e-3), math.log(1e-1)))
    return {
        "x_prompt": nrm(ks[0], (BATCH, SEQ, D_MODEL), 1.0),
        "x_sample": nrm(ks[1], (DEC_BATCH, DEC_SEQ, D_MODEL), 1.0),
        "state_pool": nrm(ks[2], (DEPTH, DEC_BATCH, POOL_BUF, D_POOL), 1.0),
        "state_conv": nrm(ks[3], (DEPTH, DEC_BATCH, CONV_W - 1, D_XBC), 1.0),
        "state_ssm": nrm(ks[4], (DEPTH, DEC_BATCH, N_HEADS, HEAD_DIM, D_STATE), 0.5),
        "w_in": nrm(ks[5], (DEPTH, D_MODEL, D_IN_PROJ), D_MODEL ** -0.5),
        "conv_w": nrm(ks[6], (DEPTH, CONV_W, D_XBC), CONV_W ** -0.5),
        "conv_b": nrm(ks[7], (DEPTH, D_XBC), 0.01),
        "dt_bias": dt0 + jnp.log(-jnp.expm1(-dt0)),
        "A_log": jnp.log(jax.random.uniform(ks[9], (DEPTH, N_HEADS), f32, 1.0, 16.0)),
        "D_skip": 1.0 + nrm(ks[10], (DEPTH, N_HEADS), 0.1),
        "ssm_norm_w": 1.0 + nrm(ks[11], (DEPTH, D_SSM), 0.02),
        "pool_w": nrm(ks[12], (DEPTH, POOL_GROUPS, POOL_GROUP, POOL_GROUP), POOL_GROUP ** -0.5),
        "pool_scale": 1.0 + nrm(ks[13], (DEPTH, D_POOL), 0.02),
        "w_out": nrm(ks[14], (DEPTH, D_MIX, D_MODEL), BETA * D_MIX ** -0.5),
        "ln1_g": 1.0 + nrm(ks[15], (DEPTH, D_MODEL), 0.02),
        "ln1_b": nrm(ks[16], (DEPTH, D_MODEL), 0.01),
        "ln2_g": 1.0 + nrm(ks[17], (DEPTH, D_MODEL), 0.02),
        "ln2_b": nrm(ks[18], (DEPTH, D_MODEL), 0.01),
        "ffn_w_gate": nrm(ks[19], (N_DENSE, D_MODEL, D_FF), D_MODEL ** -0.5),
        "ffn_w_up": nrm(ks[20], (N_DENSE, D_MODEL, D_FF), D_MODEL ** -0.5),
        "ffn_w_down": nrm(ks[21], (N_DENSE, D_FF, D_MODEL), BETA * D_FF ** -0.5),
        "router_w": nrm(ks[22], (N_MOE, D_MODEL, N_EXPERTS), D_MODEL ** -0.5),
        "router_b": nrm(ks[23], (N_MOE, N_EXPERTS), 0.01),
        "moe_w_gate": nrm(ks[24], (N_MOE, N_EXPERTS, D_MODEL, D_FF_EXPERT), D_MODEL ** -0.5),
        "moe_w_up": nrm(ks[25], (N_MOE, N_EXPERTS, D_MODEL, D_FF_EXPERT), D_MODEL ** -0.5),
        "moe_w_down": nrm(ks[26], (N_MOE, N_EXPERTS, D_FF_EXPERT, D_MODEL), BETA * D_FF_EXPERT ** -0.5),
    }

def reference(x_prompt, x_sample, state_pool, state_conv, state_ssm, w_in, conv_w, conv_b, dt_bias,
              A_log, D_skip, ssm_norm_w, pool_w, pool_scale, w_out, ln1_g, ln1_b, ln2_g, ln2_b,
              ffn_w_gate, ffn_w_up, ffn_w_down, router_w, router_b, moe_w_gate, moe_w_up, moe_w_down):
    params = (w_in, conv_w, conv_b, dt_bias, A_log, D_skip, ssm_norm_w, pool_w, pool_scale, w_out,
              ln1_g, ln1_b, ln2_g, ln2_b, ffn_w_gate, ffn_w_up, ffn_w_down,
              router_w, router_b, moe_w_gate, moe_w_up, moe_w_down)
    bp = x_prompt.shape[0]
    dtype = x_prompt.dtype
    pool0 = jnp.zeros((DEPTH, bp, POOL_BUF, D_POOL), dtype)
    conv0 = jnp.zeros((DEPTH, bp, CONV_W - 1, D_XBC), dtype)
    ssm0 = jnp.zeros((DEPTH, bp, N_HEADS, HEAD_DIM, D_STATE), dtype)
    y_prompt, pool_p, conv_p, ssm_p = trunk(x_prompt, 0, pool0, conv0, ssm0, params)
    y_sample, pool_s, conv_s, ssm_s = trunk(x_sample, PAST_LEN, state_pool, state_conv, state_ssm, params)
    return (y_prompt, y_sample, pool_p, conv_p, ssm_p, pool_s, conv_s, ssm_s)


_drawn_inputs = setup_inputs


def setup_inputs(seed=0):
    import zlib

    import numpy as np

    out = dict(_drawn_inputs(seed))
    spreads = {}
    factors = {'conv_b': 2.904,
     'ssm_norm_w': 4.182,
     'ln1_b': 3.189,
     'ln2_b': 2.971,
     'pool_scale': 8.0,
     'router_b': 5.805}
    for name, (base, spread) in spreads.items():
        noise = np.random.default_rng([zlib.crc32(name.encode()), seed]).standard_normal(out[name].shape)
        drawn = base * np.exp(spread * noise) if base else spread * noise
        out[name] = __import__('jax').numpy.asarray(drawn.astype(out[name].dtype))
    for name, factor in factors.items():
        out[name] = (out[name] * factor).astype(out[name].dtype)
    return out
```

```python
from contextlib import ExitStack

import numpy as np

import concourse.bass as bass
from concourse import mybir

F32 = mybir.dt.float32
F32R = mybir.dt.float32r
I32 = mybir.dt.int32
ALU = mybir.AluOpType
ACT = mybir.ActivationFunctionType
AX = mybir.AxisListType

P = 128
D = 1024
SEQ = 256
NB, DL = 8, 4
NS = NB * DL
T = SEQ + NS
KD = D // P
D_POOL, D_SSM, N_STATE, N_GRP, NH, HD = 512, 1536, 128, 4, 24, 64
D_XBC = D_SSM + 2 * N_GRP * N_STATE
D_IN = D_POOL + D_SSM + D_XBC + NH
CW = 4
HIST = CW - 1
PB = 15
WINDOWS = (2, 4, 8, 16)
D_FF = 2816
NE = 8
DEPTH = 2
ALPHA = (2.0 * DEPTH) ** 0.25
LN_EPS, RMS_EPS = 1e-5, 1e-6

XT = D_XBC // P
ST = D_SSM // P
GT = ST // N_GRP
MT = (D_POOL + D_SSM) // P
FT = D_FF // P
HG = NH // N_GRP

CSEG = HIST + DL
CLINE = HIST + SEQ + NB * CSEG + 1
CS0 = HIST + SEQ
COUT = CLINE - 1 - HIST
PSEG = PB + DL
PLINE = PB + SEQ + NB * PSEG
PS0 = PB + SEQ

UNIT = 2048
RING = 3
AHEAD = 2
FFN_SET = 3 * [0, 1, 0] + [1, 0]
U_WIN, U_WOUT, U_GU, U_DN = 18, 8, 22, 11
L_BASE = (0, U_WIN + U_WOUT + U_GU + U_DN)
TILE_BANKS = 6
TAIL = (7, 1, 3, 4, 7, 1)
U_MOE = L_BASE[1] + U_WIN + U_WOUT
FCH = [(c * 512, min(512, D_FF - c * 512)) for c in range(6)]


def expert_units():
    out = []

    def down(c):
        f0, w = FCH[c]
        if w == 512:
            out.extend([("d", c, 0), ("d", c, 1)])
        else:
            out.append(("d", c, 2))

    for c, (f0, w) in enumerate(FCH):
        for kind in "gu":
            if w == 512:
                out.extend([(kind, c, 0), (kind, c, 1)])
            else:
                out.append((kind, c, 2))
        if c:
            down(c - 1)
    down(len(FCH) - 1)
    return out


EXPERT = expert_units()
U_EXP = len(EXPERT)
J_OUT = 1
J_SCATTER = 2
J_BACK = 10
J_PICK = 12
J_GATHER = EXPERT.index(("u", 5, 2))
assert U_EXP % RING == 0

C_ID, C_TRI, C_TRI2, C_ONES, C_BLK2, C_STRI, C_IOTA = (i * P for i in range(7))
C_REV = 7 * P
C_INVC = C_REV + NE
C_BM = C_INVC + 4 * 16
C_VAL = C_BM + NB
C_N = C_VAL + 3


def shape_constants():
    c = np.zeros((P, C_N), np.float32)
    i = np.arange(P)
    c[:, C_ID:C_ID + P] = np.eye(P)
    c[:, C_TRI:C_TRI + P] = i[:, None] <= i[None, :]
    same = (i[:, None] // DL == i[None, :] // DL) & (i[:, None] < NS) & (i[None, :] < NS)
    c[:, C_TRI2:C_TRI2 + P] = same & (i[:, None] <= i[None, :])
    c[:, C_ONES:C_ONES + P] = 1.0
    c[:, C_BLK2:C_BLK2 + P] = same
    c[:, C_STRI:C_STRI + P] = i[:, None] < i[None, :]
    c[:, C_IOTA:C_IOTA + P] = i[None, :]
    c[:, C_REV:C_REV + NE] = NE - np.arange(NE)[None, :]
    for g, w in enumerate(WINDOWS):
        c[:, C_INVC + 16 * g:C_INVC + 16 * g + 16] = 1.0 / np.minimum(np.arange(16) + 1, w)
    c[:, C_BM:C_BM + NB] = i[:, None] // DL == np.arange(NB)[None, :]
    c[:, C_VAL:C_VAL + 2] = 1.0
    c[:NS, C_VAL + 2] = 1.0
    return c


R_CW, R_CB, R_NW, R_PS, R_A = 0, CW * XT, CW * XT + XT, CW * XT + XT + ST, CW * XT + XT + ST + N_GRP
R_L1G, R_L1B, R_L2G, R_L2B, R_B = 0, KD, 2 * KD, 3 * KD, 4 * KD



class Unit:

    def __init__(self, k, it=0, per=0):
        assert per % RING == 0
        self.slot = k % RING
        self.n = k + per * it if per else k
        self.round = k // RING + (per // RING) * it if per else k // RING

    @property
    def multiplied(self):
        return self.n + RING + 1


class Count:

    def __init__(self, sem):
        self.sem, self.n, self.it, self.per = sem, 0, 0, 0

    def value(self):
        return self.n + self.per * self.it if self.per else self.n

    def loop(self, it, per, times):
        return _Loop(self, it, per, times)


class _Loop:
    def __init__(self, count, it, per, times):
        self.c, self.new, self.times = count, (it, per), times

    def __enter__(self):
        c = self.c
        self.start = c.n
        c.it, c.per = self.new
        return c

    def __exit__(self, *error):
        c = self.c
        if error[0] is None:
            assert c.n - self.start == self.new[1], (c.n - self.start, self.new[1])
        c.n = self.start + self.new[1] * self.times
        c.it, c.per = 0, 0


class Order:

    def __init__(self, engine, sem):
        self.engine, self.own, self.last = engine, Count(sem), None

    def did(self, ins, event=None):
        c = event or self.own
        ins.then_inc(c.sem, 1)
        c.n += 1
        self.last = c
        return ins

    def sync(self):
        self.engine.wait_ge(self.last.sem, self.last.value())


def trunk(nc, x_prompt, x_sample, state_pool, state_conv, state_ssm, w_in, conv_w, conv_b, dt_bias, A_log, D_skip,
          ssm_norm_w, pool_w, pool_scale, w_out, ln1_g, ln1_b, ln2_g, ln2_b, ffn_w_gate, ffn_w_up, ffn_w_down,
          router_w, router_b, moe_w_gate, moe_w_up, moe_w_down, consts,
          y_prompt, y_sample, pool_p, conv_p, ssm_p, pool_s, conv_s, ssm_s):
    with ExitStack() as ctx:
        base = -(-nc.sbuf_base // 64) * 64
        end = nc.sbuf_usable_end

        def at(name, shape, offset, dt=F32):
            size = 4 * int(np.prod(shape[1:]))
            assert offset % 32 == 0, name
            assert base + offset + size <= end, (name, base + offset + size, end)
            return nc.alloc_sbuf_tensor_at(name, shape, dt, offset=base + offset)

        sems = {}

        def sem(name):
            if name not in sems:
                sems[name] = ctx.enter_context(nc.semaphore(name))
            return sems[name]

        class Memory:

            def __init__(self, o):
                self.o = o

            def take(self, name, shape, dt=F32):
                t = at(name, shape, self.o, dt)
                self.o += -(-4 * int(np.prod(shape[1:])) // 32) * 32
                return t

        m = Memory(0)
        raw = [m.take(f"raw{i}", [P, UNIT]) for i in range(RING)]
        hi = [m.take(f"hi{i}", [P, UNIT], F32R) for i in range(RING)]
        lo = [m.take(f"lo{i}", [P, UNIT], F32R) for i in range(RING)]
        xT = m.take("xT", [P, KD, T])
        m2 = Memory(m.o)
        xh = m.take("xh", [P, KD, T], F32R)
        xl = m.take("xl", [P, KD, T], F32R)
        y = m2.take("y", [P, ST, T])
        ctail = m2.take("ctail", [P, XT, (NB + 1) * HIST])
        utail = m2.take("utail", [P, N_GRP, (NB + 1) * PB])
        assert m2.o <= m.o
        cst = m.take("cst", [P, C_N])
        par_a = [m.take(f"par_a{l}", [P, R_A]) for l in range(DEPTH)]
        par_b = [m.take(f"par_b{l}", [P, R_B]) for l in range(DEPTH)]
        bias_h = [m.take(f"bias_h{l}", [P, NH]) for l in range(DEPTH)]
        alog = [m.take(f"alog{l}", [P, NH]) for l in range(DEPTH)]
        dsk = [m.take(f"dsk{l}", [P, ST]) for l in range(DEPTH)]
        dskb = [m.take(f"dskb{l}", [P, NH]) for l in range(DEPTH)]
        wdt = [m.take(f"wdt{l}", [P, KD, NH]) for l in range(DEPTH)]
        plw = m.take("plw", [P, N_GRP, P])
        rw = m.take("rw", [P, KD, NE])
        rb = m.take("rb", [P, NE])
        dts = {n: m.take("dt_" + n, [P, 3, NH]) for n in
               ("v", "a", "e", "s", "s2", "p", "dt", "dtA", "cum", "tot", "ew", "etot")}
        expA = m.take("expA", [P, NH])
        cumT = m.take("cumT", [NH, T])
        cumTh = m.take("cumTh", [NH, T], F32R)
        cumTl = m.take("cumTl", [NH, T], F32R)
        selc = m.take("selc", [NH, NH], F32R)
        zer = m.take("zer", [P, T], F32R)
        arena = m.o

        def ar(o):
            return Memory(arena + o)

        m = ar(0)
        zs = m.take("zs", [P, ST, T])
        o_conv = m.o - arena
        conv = m.take("conv", [P, XT, CLINE])
        o_pad = m.o - arena
        xpad = m.take("xpad", [P, XT, CLINE])
        o_u = m.o - arena
        upad = m.take("upad", [P, N_GRP, PLINE])
        o_h = m.o - arena
        histc = ar(o_h).take("histc", [NB * HIST, D_XBC])
        win_a = m.take("win_a", [P, N_GRP, PLINE])
        win_b = m.take("win_b", [P, N_GRP, PLINE])
        histp = ar(m.o - arena).take("histp", [NB * PB, D_POOL])
        pdiff = m.take("pdiff", [P, N_GRP, T])
        xact = ar(o_pad).take("xact", [P, XT, T])
        m = ar(o_conv)
        ecp = m.take("ecp", [P, ST, P + NS])
        h0T = ar(m.o - arena).take("h0T", [P, NB, P])
        hT = m.take("hT", [P, D_SSM])
        bblk = ar(m.o - arena).take("bblk", [NS, NB, P])
        xdt = m.take("xdt", [P, D_SSM])
        btok = m.take("btok", [P, N_GRP, P])
        cbT = m.take("cbT", [P, N_GRP, P])
        assert m.o - arena <= o_pad
        m = ar(o_pad + 4 * XT * T)
        wx = m.take("wx", [P, D_SSM])
        o_dec = m.o - arena
        dec = [m.take(f"dec{i}", [P, HG, P]) for i in range(2)]
        m3 = ar(o_dec)
        tailp_s = m3.take("tailp_s", [NB * PB, D_POOL])
        tailp_p = m3.take("tailp_p", [PB, D_POOL])
        hout = ar(o_dec).take("hout", [P, ST, P])
        plo = m.take("plo", [P, N_GRP, T])
        tailc = ar(m.o - arena).take("tailc", [HIST * (NB + 1), D_XBC])
        h0 = [m.take(f"h0_{i}", [P, NB, P]) for i in range(3)]
        ytmp = m.take("ytmp", [P, GT * P])
        sq = ar(0).take("sq", [P, ST, T])
        rms = ar(o_conv).take("rms", [P, N_GRP, T])
        m = ar(0)
        mixh = m.take("mixh", [P, MT, T], F32R)
        mixl = m.take("mixl", [P, MT, T], F32R)
        lsq = m.take("lsq", [P, KD, T])
        lnt = m.take("lnt", [P, 2, T])
        m = ar(0)
        hh = m.take("hh", [P, FT, T], F32R)
        hl = m.take("hl", [P, FT, T], F32R)
        sg = [m.take(f"sg{i}", [P, 2, T]) for i in range(2)]
        hf = [m.take(f"hf{i}", [P, 2, T]) for i in range(2)]
        res = m.take("res", [P, KD, T])
        assert m.o - arena <= o_h
        m = ar(0)
        xin = m.take("xin", [P, 3, D])
        prow = [m.take(f"prow{l}", [P, 2, P]) for l in range(DEPTH)]
        m = ar(0)
        xtokh = m.take("xtokh", [P, 3, D], F32R)
        xtokl = m.take("xtokl", [P, 3, D], F32R)
        acc = m.take("acc", [P, 3, D])
        xgh = m.take("xgh", [P, KD, P], F32R)
        xgl = m.take("xgl", [P, KD, P], F32R)
        pick = m.take("pick", [P, 3, P], F32R)
        back = m.take("back", [P, 3 * P], F32R)
        gsl = [m.take(f"gsl{i}", [P, 512]) for i in range(2)]
        hex_ = [m.take(f"hex{i}", [P, 512]) for i in range(2)]
        hTh = [m.take(f"hTh{i}", [P, 4, P], F32R) for i in range(2)]
        hTl = [m.take(f"hTl{i}", [P, 4, P], F32R) for i in range(2)]
        yh = m.take("yh", [P, D], F32R)
        yl = m.take("yl", [P, D], F32R)
        gbc = m.take("gbc", [P, D])
        bbc = m.take("bbc", [P, D])
        gslot = m.take("gslot", [P, 8])
        rt = {n: m.take("rt_" + n, [P, 3, NE]) for n in ("lg", "c1", "oh1", "lg2", "c2", "oh2", "G", "M", "t")}
        posm = m.take("posm", [P, 3, NE + 1])
        r3 = {n: m.take("r3_" + n, [P, 8]) for n in ("v1", "r1", "v2", "r2", "d", "e", "g1", "g2", "st0", "st1", "mv", "rs")}
        cnti = m.take("cnti", [P, 8], I32)
        stat = m.take("stat", [P, 12])

        bank = [ctx.enter_context(nc.psum_tensor(f"bank{i}", [P, 512], F32)) for i in range(8)]

        ident = cst[:, C_ID:C_ID + P]
        tri = cst[:, C_TRI:C_TRI + P]
        tri2 = cst[:, C_TRI2:C_TRI2 + P]
        ones = cst[:, C_ONES:C_ONES + P]
        blk2 = cst[:, C_BLK2:C_BLK2 + P]
        stri = cst[:, C_STRI:C_STRI + P]
        iota = cst[:, C_IOTA:C_IOTA + P]

        def csamples(line, k0=0, n=DL):
            return line.rearrange("p (b k) -> p b k", k=CSEG)[:, :, k0:k0 + n]

        def by_sample(ap):
            return ap.rearrange("p (b k) -> p b k", k=DL)

        landed = [sem(f"landed{i}") for i in range(RING)]
        split_done = sem("split_done")
        hi_done = sem("hi_done")
        used = sem("used")

        def split_hi(act, u):
            act.wait_ge(landed[u.slot], 16 * u.round + 16)
            act.wait_ge(used, u.n + 1)
            nc.scalar.copy(hi[u.slot][:, :], raw[u.slot][:, :]).then_inc(hi_done, 1)

        def split_lo(dve, u):
            dve.wait_ge(hi_done, u.n + 1)
            nc.vector.tensor_tensor(lo[u.slot][:, :], raw[u.slot][:, :], hi[u.slot][:, :].bitcast(F32),
                                    ALU.subtract).then_inc(split_done, 1)

        def three(out, wh, wl, mh, ml, start, stop):
            nc.tensor.matmul(out, wh, mh, start=start, stop=False, skip_group_check=True)
            nc.tensor.matmul(out, wh, ml, start=False, stop=False, skip_group_check=True)
            return nc.tensor.matmul(out, wl, mh, start=False, stop=stop, skip_group_check=True)

        def three_t(out, xh_, xl_, wh, wl, start, stop):
            nc.tensor.matmul(out, xh_, wh, start=start, stop=False, skip_group_check=True)
            nc.tensor.matmul(out, xl_, wh, start=False, stop=False, skip_group_check=True)
            return nc.tensor.matmul(out, xh_, wl, start=False, stop=stop, skip_group_check=True)

        def zero(out, n, m_=P):
            nc.tensor.matmul(out, zer[:, 0:m_], zer[:, 0:n], start=True, stop=False, skip_group_check=True)

        def add(out, a, b, stop=False):
            return nc.tensor.matmul(out, a, b, start=False, stop=stop, skip_group_check=True)

        def view(t, w):
            return t[:, :].rearrange("p (k c) -> p k c", c=w)

        wv = [w_in[l].rearrange("(k p) c -> p k c", p=P) for l in range(DEPTH)]
        gv = ffn_w_gate[0].rearrange("(k p) c -> p k c", p=P)
        uv = ffn_w_up[0].rearrange("(k p) c -> p k c", p=P)
        ov = [w_out[l].rearrange("(k p) c -> p k c", p=P) for l in range(DEPTH)]
        dv = ffn_w_down[0].rearrange("(k p) c -> p k c", p=P)
        egv = moe_w_gate[0].rearrange("e (k p) c -> e p k c", p=P)
        euv = moe_w_up[0].rearrange("e (k p) c -> e p k c", p=P)
        edv = moe_w_down[0].rearrange("e (k p) c -> e p k c", p=P)
        XCOL = D_POOL + D_SSM
        NL = 3 + DEPTH * 12 + 3

        block = ctx.enter_context(nc.Block())

        @block.sync
        def _(sp):
            q = sem("in_loaded")
            loads = 0

            def first(out, src):
                nonlocal loads
                sp.dma_start(out, src).then_inc(q, 16)
                loads += 1

            first(cst[:, :], consts)
            first(xin[:, 0:2, :], x_prompt[0].rearrange("(a p) d -> p a d", p=P))
            first(xin[0:NS, 2, :], x_sample.rearrange("b t d -> (b t) d"))
            for l in range(DEPTH):
                for row, src, n in ((R_CW, conv_w[l].rearrange("k (t p) -> (k t) p", p=P), CW * XT),
                                    (R_CB, conv_b[l].rearrange("(t p) -> t p", p=P), XT),
                                    (R_NW, ssm_norm_w[l].rearrange("(t p) -> t p", p=P), ST),
                                    (R_PS, pool_scale[l].rearrange("(t p) -> t p", p=P), N_GRP)):
                    first(prow[l][row:row + n, 0, :], src)
                for row, src in ((R_L1G, ln1_g), (R_L1B, ln1_b), (R_L2G, ln2_g), (R_L2B, ln2_b)):
                    first(prow[l][row:row + KD, 1, :], src[l].rearrange("(t p) -> t p", p=P))
                first(bias_h[l][:, :], dt_bias[l:l + 1, :].to_broadcast([P, NH]))
                first(alog[l][:, :], A_log[l:l + 1, :].to_broadcast([P, NH]))
                first(dskb[l][:, :], D_skip[l:l + 1, :].to_broadcast([P, NH]))
                first(wdt[l][:, :, :], wv[l][:, :, D_IN - NH:D_IN])
            first(rw[:, :, :], router_w[0].rearrange("(k p) e -> p k e", p=P))
            first(rb[:, :], router_b[0:1, :].to_broadcast([P, NE]))
            first(plw[:, :, :], pool_w[0].rearrange("g c d -> c g d"))
            assert loads == NL, loads

            def load(u, w, src):
                sp.wait_ge(split_done, u.n + 1)
                sp.dma_start(view(raw[u.slot], w), src).then_inc(landed[u.slot], 16)

            for l in range(DEPTH):
                b = L_BASE[l]
                with sp.Fori(0, 3) as i:
                    for j in range(3):
                        load(Unit(b + j, i, 3), 256, wv[l][:, :, bass.ds(XCOL + 256 * j + 768 * i, 256)])
                load(Unit(b + 9), 256, wv[l][:, :, XCOL + 2304:XCOL + 2560])
                for j in range(2):
                    load(Unit(b + 10 + j), 256, wv[l][:, :, 256 * j:256 * j + 256])
                with sp.Fori(0, 2) as i:
                    for j in range(3):
                        load(Unit(b + 12 + j, i, 3), 256, wv[l][:, :, bass.ds(D_POOL + 256 * j + 768 * i, 256)])
                b += U_WIN
                for j in range(U_WOUT):
                    load(Unit(b + j), D, ov[l][:, 2 * j:2 * j + 2, :])
                b += U_WOUT
                if l == 0:
                    with sp.Fori(0, 3) as i:
                        for j in range(6):
                            load(Unit(b + j, i, 6), 256,
                                 (gv, uv)[j % 2][:, :, bass.ds(768 * i + 256 * (j // 2), 256)])
                    for j in range(18, U_GU):
                        load(Unit(b + j), 256, (gv, uv)[j % 2][:, :, 256 * (j // 2):256 * (j // 2) + 256])
                    b += U_GU
                    with sp.Fori(0, 3) as i:
                        for j in range(3):
                            load(Unit(b + j, i, 3), D, dv[:, bass.ds(2 * j + 6 * i, 2), :])
                    for j in range(9, U_DN):
                        load(Unit(b + j), D, dv[:, 2 * j:2 * j + 2, :])

            def expert(j, u, e):
                kind, c, h = EXPERT[j]
                f0, w = FCH[c]
                if isinstance(e, int):
                    e = slice(e, e + 1)
                else:
                    e = bass.ds(e, 1)
                if kind == "d":
                    src = (edv[e, :, f0 // P:f0 // P + 4, 512 * h:512 * h + 512] if h < 2 else
                           edv[e, :, f0 // P:f0 // P + 2, :])
                    load(u, 512 if h < 2 else D, src.rearrange("e p k c -> p (e k) c"))
                else:
                    v = egv if kind == "g" else euv
                    src = v[e, :, 4 * h:4 * h + 4, f0:f0 + w] if h < 2 else v[e, :, :, f0:f0 + w]
                    load(u, w, src.rearrange("e p k c -> p (e k) c"))

            with sp.Fori(0, NE) as e:
                for j in range(U_EXP):
                    expert(j, Unit(U_MOE + j, e, U_EXP), e)
            for j in range(AHEAD):
                expert(j, Unit(U_MOE + NE * U_EXP + j), 0)
            sp.wait_ge(sem("count_ready"), 1)
            over = sp.value_load(cnti[0:1, 0:1], min_val=0, max_val=T)
            with sp.If(over > P):
                for r in range(2):
                    b = U_MOE + NE * U_EXP * (1 + r)
                    with sp.Fori(0, NE - 1) as e:
                        for j in range(AHEAD, U_EXP + AHEAD):
                            expert(j % U_EXP, Unit(b + j, e, U_EXP), e + j // U_EXP)
                    for j in range(AHEAD, U_EXP + AHEAD):
                        expert(j % U_EXP, Unit(b + (NE - 1) * U_EXP + j), (NE - 1 + j // U_EXP) % NE)
            for a in range(3):
                sp.wait_ge(sem("out_ready"), a + 1)
                if a < 2:
                    sp.dma_start(y_prompt[0, P * a:P * a + P, :], acc[:, a, :]).then_inc(sem("y_stored"), 16)
                else:
                    sp.dma_start(y_sample.rearrange("b t d -> (b t) d"), acc[0:NS, 2, :])\
                      .then_inc(sem("y_stored"), 16)
            sp.wait_ge(sem("y_stored"), 48)

        def tile_out(l, n):
            return TILE_BANKS + 2 * U_WIN * l + n

        @block.gpsimd
        def _(pool):
            ev = Order(pool, sem("pool_did"))
            mem = Count(sem("padded"))
            tails = Count(sem("tails_packed"))
            decm = Count(sem("decay_masked"))
            wxm = Count(sem("wx_ready"))
            blkm = Count(sem("bblk_ready"))
            for l in range(DEPTH):
                if l:
                    pool.wait_ge(sem("x_ready"), 16 + KD)
                else:
                    ev.did(nc.gpsimd.memset(zer[:, :].bitcast(F32), 0.0), mem)
                pool.dma_start(histc[:, :], state_conv[l].rearrange("b k c -> (b k) c")).then_inc(sem("hist_in"), 16)
                pool.dma_start(histp[:, :], state_pool[l].rearrange("b k c -> (b k) c")).then_inc(sem("hist_in"), 16)
                if l:
                    pool.wait_ge(sem("plo_done"), N_GRP)
                    pool.dma_start(plw[:, :, :], pool_w[l].rearrange("g c d -> c g d")).then_inc(sem("plw_in"), 16)
                else:
                    pool.wait_ge(sem("params_ready"), 1)
                ev.did(nc.gpsimd.memset(xpad[:, :, 0:HIST], 0.0), mem)
                ev.did(nc.gpsimd.memset(upad[:, :, 0:PB], 0.0), mem)
                pool.wait_ge(used, L_BASE[l] + U_WIN + RING)
                pool.wait_ge(sem("tile_out"), tile_out(l, XT))
                ev.did(nc.gpsimd.tensor_copy(
                    ctail[:, :, 0:HIST], xpad[:, :, SEQ:SEQ + HIST]), tails)
                for b in range(NB):
                    o = CS0 + CSEG * b + DL
                    ev.did(nc.gpsimd.tensor_copy(ctail[:, :, HIST * (b + 1):HIST * (b + 2)],
                                                 xpad[:, :, o:o + HIST]), tails)
                pool.wait_ge(sem("tile_out"), tile_out(l, XT + N_GRP))
                ev.did(nc.gpsimd.tensor_copy(utail[:, :, 0:PB], upad[:, :, SEQ:SEQ + PB]), tails)
                for b in range(NB):
                    o = PS0 + PSEG * b + DL
                    ev.did(nc.gpsimd.tensor_copy(utail[:, :, PB * (b + 1):PB * (b + 2)],
                                                 upad[:, :, o:o + PB]), tails)
                pool.wait_ge(sem("tail_out"), 7 * (l + 1))
                pool.dma_start(conv_p[l, 0], tailc[0:HIST, :]).then_inc(sem("tail_stored"), 16)
                pool.dma_start(conv_s[l].rearrange("b k c -> (b k) c"), tailc[HIST:HIST * (NB + 1), :])\
                    .then_inc(sem("tail_stored"), 16)
                pool.dma_start(pool_p[l, 0], tailp_p[:, :]).then_inc(sem("tail_stored"), 16)
                pool.dma_start(pool_s[l].rearrange("b k c -> (b k) c"), tailp_s[:, :]).then_inc(sem("tail_stored"), 16)
                pool.wait_ge(sem("tail_stored"), 64 * (l + 1))
                for t in range(3):
                    pool.dma_start(h0[t][:, :, :],
                                   state_ssm[l].rearrange("b h p n -> (h p) b n")[P * t:P * t + P])\
                        .then_inc(sem(f"state_in{t}"), 16)
                for b in range(3):
                    n = P if b < 2 else NS
                    q = 3 * l + b
                    pool.wait_ge(sem("ew_ready"), l + 1)
                    pool.wait_ge(sem("xdt_ready"), 3 * (q + 1))
                    if b:
                        pool.wait_ge(sem("state_mm"), 8 * l + 4 * b)
                    ev.did(nc.gpsimd.tensor_tensor(
                        wx[0:n, :].rearrange("p (h d) -> p h d", d=HD), xdt[0:n, :].rearrange("p (h d) -> p h d", d=HD),
                        dts["ew"][0:n, b, :].unsqueeze(2).to_broadcast([n, NH, HD]), ALU.mult), wxm)
                    pool.wait_ge(sem("cb_ready"), q + 1)
                    for g in range(N_GRP):
                        k = 4 * q + g
                        pool.wait_ge(sem("decay_exp"), k + 1)
                        ev.did(nc.gpsimd.tensor_tensor(
                            dec[g % 2][0:n, :, 0:n], dec[g % 2][0:n, :, 0:n],
                            cbT[0:n, g:g + 1, 0:n].to_broadcast([n, HG, n]), ALU.mult), decm)
                pool.wait_ge(sem("hout_ready"), 3 * (l + 1))
                pool.dma_start(ssm_p[l, 0].rearrange("h p n -> (h p) n").rearrange("(t q) n -> q t n", q=P),
                               hout[:, :, :]).then_inc(sem("hout_stored"), 16)
                for t in range(ST):
                    if t % GT == 0:
                        k = N_GRP * l + t // GT
                        if t:
                            pool.wait_ge(sem("update_mm"), GT * k)
                        else:
                            pool.wait_ge(sem("ydiag_mm"), 12 * (l + 1))
                        ev.did(nc.gpsimd.tensor_tensor(
                            bblk[:, :, :], btok[0:NS, t // GT:t // GT + 1, :].to_broadcast([NS, NB, P]),
                            cst[0:NS, C_BM:C_BM + NB].unsqueeze(2).to_broadcast([NS, NB, P]), ALU.mult), blkm)
                    pool.wait_ge(sem("state_new"), ST * l + t + 1)
                    pool.dma_start(ssm_s[l].rearrange("b h p n -> (h p) b n")[P * t:P * t + P], h0[t % 3][:, :, :])\
                        .then_inc(sem(f"state_out{t % 3}"), 16)
                    pool.wait_ge(sem(f"state_out{t % 3}"), 16 * (4 * l + t // 3 + 1))
                    if t + 3 < ST:
                        pool.dma_start(h0[t % 3][:, :, :],
                                       state_ssm[l].rearrange("b h p n -> (h p) b n")[P * (t + 3):P * (t + 3) + P])\
                            .then_inc(sem(f"state_in{t % 3}"), 16)
                pool.wait_ge(sem("hout_stored"), 16 * (l + 1))
            pool.wait_ge(sem("x_ready"), 32)
            pool.dma_start(gbc[:, :], ln2_g[1:2, :].to_broadcast([P, D])).then_inc(sem("ln_bc"), 16)
            pool.dma_start(bbc[:, :], ln2_b[1:2, :].to_broadcast([P, D])).then_inc(sem("ln_bc"), 16)

        @block.scalar
        def _(act):
            A = nc.scalar
            ev = Order(act, sem("act_did"))
            C = {}

            def did(ins, name=None):
                if name is None:
                    return ev.did(ins)
                if name not in C:
                    C[name] = Count(sem(name))
                return ev.did(ins, C[name])

            for name, n in (("tile_out", TILE_BANKS),):
                A.sem_inc(sem(name), n)
                C[name] = Count(sem(name))
                C[name].n = n

            act.wait_ge(sem("in_loaded"), 16 * NL)
            did(A.copy(selc[:, :], cst[0:NH, C_ID:C_ID + NH]))
            for k in range(KD):
                act.wait_ge(sem("xt_turned"), k + 1)
                did(A.copy(xT[:, k, :], bank[k][:, 0:T]))
                did(A.copy(xh[:, k, :], bank[k][:, 0:T]), "x_done")
            for l in range(DEPTH):
                act.wait_ge(sem("par_turned"), 2 * l + 2)
                did(A.copy(par_a[l][:, :], bank[2 * l][:, 0:R_A]))
                did(A.copy(par_b[l][:, :], bank[2 * l + 1][:, 0:R_B]), "params_done")
                for h in range(2):
                    w = slice(HD * h, HD * h + HD)
                    did(A.copy(dsk[l][w, :], dskb[l][w, h:NH:2]))
            did(A.activation(expA[:, :], alog[0][:, :], ACT.Exp), "params_ready")

            for l in range(DEPTH):
                b = L_BASE[l]
                if l == 0:
                    for j in range(AHEAD):
                        split_hi(act, Unit(j))
                act.wait_ge(sem("padded"), 1 + 2 * (l + 1))
                for c in range(XT):
                    if c % 4 == 0:
                        act.wait_ge(sem("hist_turned"), 6 * l + c // 4 + 1)
                    did(A.copy(csamples(xpad[:, c, CS0:CS0 + NB * CSEG], 0, HIST),
                               bank[c // 4][:, 24 * (c % 4):24 * (c % 4) + 24].rearrange("p (b k) -> p b k", k=HIST)),
                        "hist_done" if c == XT - 1 else None)
                act.wait_ge(sem("hist_turned"), 6 * l + 6)
                for g in range(N_GRP):
                    did(A.copy(upad[:, g, PS0:PS0 + NB * PSEG].rearrange("p (b k) -> p b k", k=PSEG)[:, :, 0:PB],
                               bank[6][:, 120 * g:120 * g + 120].rearrange("p (b k) -> p b k", k=PB)),
                        "hist_done" if g == N_GRP - 1 else None)

                def conv_in(u, j, c):
                    act.wait_ge(used, u.multiplied)
                    for h in range(2):
                        o = bank[2 * j + h]
                        cc = bass.ds(c + h, 1)
                        did(A.copy(xpad[:, cc, HIST:HIST + SEQ], o[:, 0:SEQ]))
                        did(A.copy(xpad[:, cc, CS0:CS0 + NB * CSEG].rearrange(
                            "p a (b k) -> p (a b) k", k=CSEG)[:, :, HIST:CSEG], by_sample(o[:, SEQ:T])), "tile_out")

                with act.Fori(0, 3) as i:
                    with C["tile_out"].loop(i, 6, 3), ev.own.loop(i, 6, 3):
                        for j in range(3):
                            split_hi(act, Unit(b + j + AHEAD, i, 3))
                            conv_in(Unit(b + j, i, 3), j, 6 * i + 2 * j)
                split_hi(act, Unit(b + 9 + AHEAD))
                conv_in(Unit(b + 9), 0, 18)
                for j in range(2):
                    split_hi(act, Unit(b + 10 + j + AHEAD))
                    act.wait_ge(used, Unit(b + 10 + j).multiplied)
                    for h in range(2):
                        o = bank[2 * j + 2 + h]
                        g = 2 * j + h
                        did(A.copy(upad[:, g, PB:PB + SEQ], o[:, 0:SEQ]))
                        did(A.copy(upad[:, g, PS0:PS0 + NB * PSEG].rearrange("p (b k) -> p b k", k=PSEG)[:, :, PB:],
                                   by_sample(o[:, SEQ:T])), "tile_out")
                with act.Fori(0, 2) as i:
                    with C["tile_out"].loop(i, 6, 2):
                        for j in range(3):
                            split_hi(act, Unit(b + 12 + j + AHEAD, i, 3))
                            act.wait_ge(used, Unit(b + 12 + j, i, 3).multiplied)
                            for h in range(2):
                                did(A.activation(zs[:, bass.ds(6 * i + 2 * j + h, 1), :], bank[2 * j + h][:, 0:T],
                                                 ACT.Silu), "tile_out")
                act.wait_ge(sem("conv_done"), XT * (l + 1))
                act.wait_ge(sem("tails_packed"), 18 * (l + 1))
                for c in range(XT):
                    did(A.activation(xact[:, c, 0:SEQ], conv[:, c, 0:SEQ], ACT.Silu))
                    did(A.activation(by_sample(xact[:, c, SEQ:T]), csamples(conv[:, c, CS0:CS0 + NB * CSEG]),
                                     ACT.Silu), "xact_done")
                for g in range(N_GRP):
                    act.wait_ge(sem("pool_mm"), N_GRP * l + g + 1)
                    did(A.activation(plo[:, g, :], bank[g][:, 0:T], ACT.Copy,
                                     scale=par_a[l][:, R_PS + g:R_PS + g + 1]), "plo_done")
                for c in range(5):
                    act.wait_ge(sem("tail_turned"), 7 * l + c + 1)
                    did(A.copy(tailc[:, 512 * c:512 * c + 512], bank[c][0:HIST * (NB + 1), :]), "tail_out")
                act.wait_ge(sem("tail_turned"), 7 * l + 7)
                did(A.copy(tailp_s[:, :], bank[5][0:NB * PB, :]), "tail_out")
                did(A.copy(tailp_p[:, :], bank[6][0:PB, :]), "tail_out")
                act.wait_ge(sem("dt_a"), l + 1)
                did(A.activation(dts["e"][:, :, :], dts["a"][:, :, :], ACT.Exp, scale=-1.0), "dt_e")
                if l:
                    did(A.activation(expA[:, :], alog[l][:, :], ACT.Exp), "dt_e")
                act.wait_ge(sem("cum_mm"), l + 1)
                did(A.copy(cumT[:, :], bank[6][0:NH, 0:T]))
                did(A.copy(cumTh[:, :], bank[6][0:NH, 0:T]), "cumh")
                act.wait_ge(sem("ew_arg"), l + 1)
                did(A.activation(dts["ew"][:, :, :], dts["ew"][:, :, :], ACT.Exp))
                did(A.activation(dts["etot"][:, :, :], dts["tot"][:, :, :], ACT.Exp), "ew_ready")
                for j in range(4):
                    act.wait_ge(sem("ecp_mm"), 4 * l + j + 1)
                    did(A.activation(ecp[:, 3 * j:3 * j + 3, :],
                                     bank[j][:, 0:480].rearrange("p (t c) -> p t c", t=3), ACT.Exp), "ecp_done")
                for bl in range(3):
                    n = P if bl < 2 else NS
                    q = 3 * l + bl
                    act.wait_ge(sem("b_turned"), q + 1)
                    if bl:
                        act.wait_ge(sem("state_mm"), 8 * l + 4 * bl)
                    did(A.copy(btok[0:n, :, :], bank[3][0:n, :].rearrange("p (g c) -> p g c", g=N_GRP)), "btok_ready")
                    for g in range(N_GRP):
                        k = 4 * q + g
                        act.wait_ge(sem("seg_ready"), k + 1)
                        did(A.activation(dec[g % 2][0:n, :, 0:n], dec[g % 2][0:n, :, 0:n], ACT.Exp), "decay_exp")
                        act.wait_ge(sem("ydiag_mm"), k + 1)
                        did(A.copy(y[:, GT * g:GT * g + GT, P * bl:P * bl + n],
                                   bank[5][:, 0:GT * n].rearrange("p (t c) -> p t c", t=GT)), "y_diag")
                    if bl == 0:
                        for g in range(N_GRP):
                            act.wait_ge(sem("state_mm"), 8 * l + g + 1)
                            did(A.copy(hT[:, 384 * g:384 * g + 384], bank[g][:, 0:384]), "h1_done")
                for j in range(3):
                    act.wait_ge(sem("h_turned"), 3 * l + j + 1)
                    did(A.copy(hout[:, 4 * j:4 * j + 4, :], bank[4 + j][:, :].rearrange("p (t c) -> p t c", t=4)),
                        "hout_ready")
                for t in range(ST):
                    act.wait_ge(sem("h0_turned"), ST * l + t + 1)
                    if t:
                        act.wait_ge(sem("yoff_mm"), ST * l + t)
                    did(A.copy(h0T[:, 0:4, :], bank[0][:, :].rearrange("p (b c) -> p b c", b=4)))
                    did(A.copy(h0T[:, 4:8, :], bank[1][:, :].rearrange("p (b c) -> p b c", b=4)), "h0T_ready")
                for g in range(N_GRP):
                    act.wait_ge(sem("gated"), N_GRP * l + g + 1)
                    did(A.activation(sq[:, GT * g:GT * g + GT, :], y[:, GT * g:GT * g + GT, :], ACT.Square), "sq_done")
                act.wait_ge(sem("rms_in"), l + 1)
                did(A.activation(rms[:, :, :], rms[:, :, :], ACT.Sqrt), "rms_sqrt")
                act.wait_ge(sem("normed"), l + 1)
                did(A.copy(mixh[:, 0:N_GRP, :], plo[:, :, :]), "mixh_done")
                for g in range(N_GRP):
                    did(A.copy(mixh[:, N_GRP + GT * g:N_GRP + GT * g + GT, :], y[:, GT * g:GT * g + GT, :]),
                        "mixh_done")
                b += U_WIN
                for j in range(U_WOUT):
                    split_hi(act, Unit(b + j + AHEAD))

                def norm(v):
                    act.wait_ge(sem("ln_cent"), v + 1)
                    for h in range(2):
                        did(A.activation(lsq[:, 4 * h:4 * h + 4, :], res[:, 4 * h:4 * h + 4, :], ACT.Square), "ln_sq")
                    act.wait_ge(sem("ln_var"), v + 1)
                    did(A.activation(lnt[:, 0, :], lnt[:, 0, :], ACT.Sqrt), "ln_sqrt")
                    off = R_L2B if v % 2 else R_L1B
                    for d in range(KD):
                        act.wait_ge(sem("ln_scaled"), KD * v + d + 1)
                        bias = par_b[l][:, off + d:off + d + 1]
                        did(A.activation(xT[:, d, :], res[:, d, :], ACT.Identity, bias=bias))
                        did(A.activation(xh[:, d, :], res[:, d, :], ACT.Identity, bias=bias), "x_done")

                norm(2 * l)
                b += U_WOUT
                if l == 0:
                    def silus(up, s):
                        act.wait_ge(used, up.n + RING)
                        did(A.activation(sg[s][:, 0, :], bank[4 * s][:, 0:T], ACT.Silu))
                        did(A.activation(sg[s][:, 1, :], bank[4 * s + 1][:, 0:T], ACT.Silu), "silu_done")

                    def upper(s, f, nth):
                        act.wait_ge(sem("hf_done"), nth + 2)
                        did(A.copy(hh[:, f, :], hf[s][:, :, :]), "hh_done")

                    with act.Fori(0, 3) as i:
                        with ev.own.loop(i, 3, 3), C.setdefault("silu_done", Count(sem("silu_done"))).loop(i, 3, 3), \
                                C.setdefault("hh_done", Count(sem("hh_done"))).loop(i, 3, 3):
                            for j in range(3):
                                split_hi(act, Unit(b + 2 * j + AHEAD, i, 6))
                                silus(Unit(b + 2 * j + 1, i, 6), FFN_SET[j])
                                split_hi(act, Unit(b + 2 * j + 1 + AHEAD, i, 6))
                                upper(FFN_SET[j], bass.ds(6 * i + 2 * j, 2), 3 * i + j)
                    for j in range(9, 11):
                        split_hi(act, Unit(b + 2 * j + AHEAD))
                        silus(Unit(b + 2 * j + 1), FFN_SET[j])
                        split_hi(act, Unit(b + 2 * j + 1 + AHEAD))
                        upper(FFN_SET[j], slice(2 * j, 2 * j + 2), j)
                    b += U_GU
                    with act.Fori(0, 3) as i:
                        for j in range(3):
                            split_hi(act, Unit(b + j + AHEAD, i, 3))
                    for j in range(9, U_DN):
                        split_hi(act, Unit(b + j + AHEAD))
                    norm(1)

            for a in range(3):
                n = P if a < 2 else NS
                for h in range(2):
                    act.wait_ge(sem("tok_turned"), 2 * a + h + 1)
                    o = bank[2 * a + h][0:n, :]
                    did(A.copy(xtokh[0:n, a, 512 * h:512 * h + 512], o), "xtokh_done")
                    did(A.mul(acc[0:n, a, 512 * h:512 * h + 512], o, ALPHA), "acc_begun")
            act.wait_ge(sem("rt_diff"), 1)
            did(A.activation(r3["e"][:, 0:3], r3["d"][:, 0:3], ACT.Exp), "rt_exp")

            def gathered(it):
                for h in range(2):
                    act.wait_ge(sem("xg_mm"), 2 * it + h + 1)
                    did(A.copy(xgh[:, 4 * h:4 * h + 4, :], bank[2 * h][:, :].rearrange("p (k s) -> p k s", k=4)),
                        "xgh_done")

            def outputs(last):
                act.wait_ge(used, last)
                for h in range(2):
                    did(A.activation(yh[:, 512 * h:512 * h + 512], bank[5 + h][:, :], ACT.Copy,
                                     scale=gslot[:, 0:1]), "yh_done")

            def item(it, b, e, per):
                def unit(j):
                    return Unit(b + j, e, per)

                def turned(c):
                    n = FCH[c][1] // P
                    act.wait_ge(sem("hT_mm"), 6 * it + c + 1)
                    did(A.copy(hTh[c % 2][:, 0:n, :], bank[4][:, 0:P * n].rearrange("p (f s) -> p f s", s=P)),
                        "hTh_done")

                for j in range(U_EXP):
                    split_hi(act, unit(j + AHEAD))
                    kind, c, h = EXPERT[j]
                    if j == J_OUT:
                        outputs(unit(0).multiplied)
                    if kind == "g" and h:
                        act.wait_ge(used, unit(j).multiplied)
                        w = FCH[c][1]
                        did(A.activation(gsl[c % 2][:, 0:w], bank[c % 2][:, 0:w], ACT.Silu), "gate_done")
                        if c:
                            turned(c - 1)
                    if j == J_BACK:
                        act.wait_ge(sem("back_mm"), it + 1)
                        did(A.copy(back[:, 0:T], bank[7][:, 0:T]), "back_done")
                        did(A.copy(gslot[:, 0:1], bank[7][:, T:T + 1]), "back_done")
                    if j == J_GATHER + 1:
                        gathered(it + 1)
                    if (kind, c, h) == ("d", 4, 0):
                        turned(5)

            def items(base):
                names = dict(xgh_done=2, back_done=2, hTh_done=6, gate_done=6, yh_done=2)
                with act.Fori(0, NE) as e:
                    with ExitStack() as loops:
                        for name, per in names.items():
                            loops.enter_context(C.setdefault(name, Count(sem(name))).loop(e, per, NE))
                        item(e + base, U_MOE + base * U_EXP, e, U_EXP)
                outputs(Unit(U_MOE + (base + NE) * U_EXP - 1).multiplied)

            gathered(0)
            items(0)
            act.wait_ge(sem("count_ready"), 1)
            over = act.value_load(cnti[0:1, 0:1], min_val=0, max_val=T)
            with act.If(over > P):
                for r in range(2):
                    items(NE * (r + 1))
            for a in range(3):
                n = P if a < 2 else NS
                act.wait_ge(sem("fin_var"), a + 1)
                did(A.activation(r3["rs"][0:n, a:a + 1], r3["rs"][0:n, a:a + 1], ACT.Sqrt), "fin_sqrt")

        @block.vector
        def _(dve):
            V = nc.vector
            ev = Order(dve, sem("dve_did"))
            C = {}

            def did(ins, name=None):
                if name is None:
                    return ev.did(ins)
                if name not in C:
                    C[name] = Count(sem(name))
                return ev.did(ins, C[name])

            def loop(it, times, **names):
                stack = ExitStack()
                for name, per in names.items():
                    stack.enter_context(C.setdefault(name, Count(sem(name))).loop(it, per, times))
                return stack

            V.sem_inc(split_done, RING)
            for name, n in (("hf_done", 1), ("hl_done", 1), ("acc_added", 1)):
                V.sem_inc(sem(name), n)
                C[name] = Count(sem(name))
                C[name].n = n
            for k in range(KD):
                dve.wait_ge(sem("x_done"), k + 1)
                did(V.tensor_tensor(xl[:, k, :], xT[:, k, :], xh[:, k, :].bitcast(F32), ALU.subtract), "x_ready")
            for j in range(AHEAD):
                split_lo(dve, Unit(j))
            for l in range(DEPTH):
                b = L_BASE[l]
                pa = par_a[l]
                dve.wait_ge(sem("hist_done"), 2 * (l + 1))
                dve.wait_ge(sem("padded"), 1 + 2 * (l + 1))
                dve.wait_ge(sem("params_ready"), 1)

                def conv_tile(c, cc, nth):
                    dve.wait_ge(sem("tile_out"), tile_out(l, nth + 1))
                    did(V.tensor_scalar(conv[:, c, 0:COUT], xpad[:, c, 0:COUT], pa[:, cc(R_CW)], pa[:, cc(R_CB)],
                                        ALU.mult, ALU.add))
                    for k in range(1, CW):
                        ev.sync()
                        did(V.scalar_tensor_tensor(conv[:, c, 0:COUT], xpad[:, c, k:k + COUT],
                                                   pa[:, cc(R_CW + XT * k)], conv[:, c, 0:COUT], ALU.mult, ALU.add),
                            "conv_done" if k == CW - 1 else None)

                with dve.Fori(0, 3) as i:
                    with loop(i, 3, conv_done=6), ev.own.loop(i, 18, 3):
                        for j in range(3):
                            split_lo(dve, Unit(b + j + AHEAD, i, 3))
                            for h in range(2):
                                c = 6 * i + 2 * j + h
                                conv_tile(bass.ds(c, 1), lambda r, c=c: bass.ds(c + r, 1), c)
                split_lo(dve, Unit(b + 9 + AHEAD))
                for c in range(18, 20):
                    conv_tile(slice(c, c + 1), lambda r, c=c: slice(c + r, c + r + 1), c)
                for j in range(2):
                    split_lo(dve, Unit(b + 10 + j + AHEAD))
                with dve.Fori(0, 2) as i:
                    for j in range(3):
                        split_lo(dve, Unit(b + 12 + j + AHEAD, i, 3))
                dve.wait_ge(sem("tile_out"), tile_out(l, XT + N_GRP))
                src, L = upad, PLINE
                for step, w in enumerate(WINDOWS):
                    out = (win_a, win_b)[step % 2]
                    lo_ = w - 1
                    half = w // 2
                    did(V.tensor_tensor(out[:, step:N_GRP, lo_:L], src[:, step:N_GRP, lo_:L],
                                        src[:, step:N_GRP, lo_ - half:L - half], ALU.add))
                    ev.sync()
                    src = out
                for g, w in enumerate(WINDOWS):
                    s_ = (win_a, win_b)[g % 2]
                    did(V.tensor_scalar(pdiff[:, g, 0:SEQ], s_[:, g, PB:PB + SEQ], 1.0 / w, None, ALU.mult))
                    did(V.tensor_scalar(by_sample(pdiff[:, g, SEQ:T]),
                                        s_[:, g, PS0:].rearrange("p (b k) -> p b k", k=PSEG)[:, :, PB:],
                                        1.0 / w, None, ALU.mult))
                    ev.sync()
                    did(V.tensor_tensor(pdiff[:, g, 0:16], s_[:, g, PB:PB + 16],
                                        cst[:, C_INVC + 16 * g:C_INVC + 16 * g + 16], ALU.mult))
                    ev.sync()
                    did(V.tensor_tensor(pdiff[:, g, 0:SEQ], pdiff[:, g, 0:SEQ], upad[:, g, PB:PB + SEQ],
                                        ALU.subtract))
                    did(V.tensor_tensor(by_sample(pdiff[:, g, SEQ:T]), by_sample(pdiff[:, g, SEQ:T]),
                                        upad[:, g, PS0:].rearrange("p (b k) -> p b k", k=PSEG)[:, :, PB:],
                                        ALU.subtract), "pdiff_done")
                D3 = {k: t[:, :, :] for k, t in dts.items()}
                dve.wait_ge(sem("dt_mm"), l + 1)
                did(V.tensor_tensor(D3["v"], bank[7][:, 0:72].rearrange("p (b h) -> p b h", b=3),
                                    bias_h[l][:, :].unsqueeze(1).to_broadcast([P, 3, NH]), ALU.add))
                ev.sync()
                did(V.tensor_scalar(D3["a"], D3["v"], -1.0, None, ALU.mult))
                ev.sync()
                did(V.tensor_tensor(D3["a"], D3["a"], D3["v"], ALU.max), "dt_a")
                dve.wait_ge(sem("dt_e"), 2 * l + 1)
                did(V.tensor_scalar(D3["s2"], D3["e"], 2.0, None, ALU.add))
                ev.sync()
                did(V.reciprocal(D3["s"], D3["s2"]))
                ev.sync()
                did(V.tensor_tensor(D3["s"], D3["s"], D3["e"], ALU.mult))
                ev.sync()
                did(V.tensor_tensor(D3["s2"], D3["s"], D3["s"], ALU.mult))
                ev.sync()
                did(V.tensor_scalar(D3["p"], D3["s2"], 1.0 / 17, None, ALU.mult))
                for k in (15, 13, 11, 9, 7, 5, 3):
                    ev.sync()
                    did(V.scalar_tensor_tensor(D3["p"], D3["p"], 1.0 / k, D3["s2"], ALU.add, ALU.mult))
                ev.sync()
                did(V.scalar_tensor_tensor(D3["p"], D3["p"], 1.0, D3["s"], ALU.add, ALU.mult))
                did(V.tensor_scalar(D3["a"], D3["v"], 0.0, None, ALU.max))
                ev.sync()
                did(V.scalar_tensor_tensor(D3["dt"], D3["p"], 2.0, D3["a"], ALU.mult, ALU.add))
                ev.sync()
                did(V.scalar_tensor_tensor(D3["dtA"], D3["dt"], -1.0,
                                           expA[:, :].unsqueeze(1).to_broadcast([P, 3, NH]), ALU.mult, ALU.mult),
                    "dtA_ready")
                dve.wait_ge(sem("cum_mm"), l + 1)
                did(V.tensor_copy(D3["cum"], bank[7][:, 128:200].rearrange("p (b h) -> p b h", b=3)))
                did(V.tensor_copy(D3["tot"], bank[7][:, 256:328].rearrange("p (b h) -> p b h", b=3)))
                ev.sync()
                did(V.tensor_tensor(D3["ew"], D3["tot"], D3["cum"], ALU.subtract), "ew_arg")
                dve.wait_ge(sem("cumh"), l + 1)
                did(V.tensor_tensor(cumTl[:, :], cumT[:, :], cumTh[:, :].bitcast(F32), ALU.subtract), "cuml")

                dve.wait_ge(sem("tail_stored"), 64 * (l + 1))
                for bl in range(3):
                    n = P if bl < 2 else NS
                    q = 3 * l + bl
                    if bl:
                        dve.wait_ge(sem("wx_ready"), q)
                        dve.wait_ge(sem("ydiag_mm"), 4 * q)
                    for j in range(3):
                        dve.wait_ge(sem("x_turned"), 3 * q + j + 1)
                        did(V.tensor_tensor(xdt[0:n, 512 * j:512 * j + 512].rearrange("p (h d) -> p h d", d=HD),
                                            bank[j][0:n, :].rearrange("p (h d) -> p h d", d=HD),
                                            dts["dt"][0:n, bl, 8 * j:8 * j + 8].unsqueeze(2)
                                            .to_broadcast([n, 8, HD]), ALU.mult), "xdt_ready")
                    dve.wait_ge(sem("cb_mm"), q + 1)
                    if bl:
                        dve.wait_ge(sem("decay_masked"), 4 * q)
                    did(V.tensor_tensor(cbT[0:n, :, 0:n], bank[4][0:n, 0:4 * n].rearrange("p (g c) -> p g c", g=4),
                                        (tri if bl < 2 else tri2)[0:n, 0:n].unsqueeze(1).to_broadcast([n, 4, n]),
                                        ALU.mult), "cb_ready")
                    for g in range(N_GRP):
                        k = 4 * q + g
                        dve.wait_ge(sem("bc_mm"), k + 1)
                        if g >= 2 or bl:
                            dve.wait_ge(sem("ydiag_mm"), k - 1)
                        for x in range(HG):
                            h = HG * g + x
                            src = bank[2 * (g % 2) + x // 4][0:n, n * (x % 4):n * (x % 4) + n]
                            did(V.tensor_scalar(dec[g % 2][0:n, x, 0:n], src, dts["cum"][0:n, bl, h:h + 1], 0.0,
                                                ALU.subtract, ALU.min), "seg_ready" if x == HG - 1 else None)
                    if bl == 1:
                        for g in range(N_GRP):
                            dve.wait_ge(sem("yoff1_mm"), N_GRP * l + g + 1)
                            dve.wait_ge(sem("y_diag"), 4 * q + g + 1)
                            yy = y[:, GT * g:GT * g + GT, P:2 * P]
                            yt = ytmp[:, :].rearrange("p (t c) -> p t c", t=GT)
                            did(V.tensor_tensor(yt, bank[6][:, 0:GT * P].rearrange("p (t c) -> p t c", t=GT),
                                                ecp[:, GT * g:GT * g + GT, 0:P], ALU.mult), "yoff1_done")
                            ev.sync()
                            did(V.tensor_tensor(yy, yy, yt, ALU.add))
                            ev.sync()
                        hv = hT[:, :].rearrange("p (h d) -> p h d", d=HD)
                        did(V.tensor_tensor(hv, hv, dts["etot"][:, 1, :].unsqueeze(2).to_broadcast([P, NH, HD]),
                                            ALU.mult))
                        ev.sync()
                        for g in range(N_GRP):
                            dve.wait_ge(sem("state_mm"), 8 * l + 4 + g + 1)
                            hg = hT[:, 384 * g:384 * g + 384]
                            did(V.tensor_tensor(hg, hg, bank[g][:, 0:384], ALU.add), "h2_done")
                for t in range(ST):
                    dve.wait_ge(sem("h0_turned"), ST * l + t + 1)
                    hv = h0[t % 3][:, :, :]
                    did(V.tensor_tensor(hv, hv, ecp[:, t, P + DL - 1:P + NS:DL].unsqueeze(2)
                                        .to_broadcast([P, NB, P]), ALU.mult))
                    dve.wait_ge(sem("update_mm"), ST * l + t + 1)
                    ev.sync()
                    for h in range(2):
                        hv = h0[t % 3][:, 4 * h:4 * h + 4, :]
                        did(V.tensor_tensor(hv, hv, bank[2 + h][:, :].rearrange("p (b c) -> p b c", b=4), ALU.add),
                            "state_new" if h else None)
                yt = ytmp[:, :].rearrange("p (t c) -> p t c", t=ST)
                dve.wait_ge(sem("yoff_mm"), ST * (l + 1))
                did(V.tensor_tensor(yt, bank[7][:, 0:ST * NS].rearrange("p (t c) -> p t c", t=ST),
                                    ecp[:, :, P:P + NS], ALU.mult))
                ev.sync()
                dve.wait_ge(sem("y_diag"), 12 * (l + 1))
                did(V.tensor_tensor(y[:, :, SEQ:T], y[:, :, SEQ:T], yt, ALU.add))
                ev.sync()
                for g in range(N_GRP):
                    for t in range(GT * g, GT * g + GT):
                        did(V.scalar_tensor_tensor(y[:, t, :], xact[:, t, :], dsk[l][:, t:t + 1], y[:, t, :],
                                                   ALU.mult, ALU.add))
                    ev.sync()
                    yy = y[:, GT * g:GT * g + GT, :]
                    did(V.tensor_tensor(yy, yy, zs[:, GT * g:GT * g + GT, :], ALU.mult), "gated")
                for g in range(N_GRP):
                    dve.wait_ge(sem("rms_mm"), N_GRP * l + g + 1)
                    did(V.tensor_scalar(rms[:, g, :], bank[g][:, 0:T], 1.0 / (GT * P), RMS_EPS, ALU.mult, ALU.add),
                        "rms_in" if g == N_GRP - 1 else None)
                dve.wait_ge(sem("rms_sqrt"), l + 1)
                did(V.reciprocal(rms[:, :, :], rms[:, :, :]))
                ev.sync()
                for t in range(ST):
                    did(V.scalar_tensor_tensor(y[:, t, :], y[:, t, :], pa[:, R_NW + t:R_NW + t + 1],
                                               rms[:, t // GT, :], ALU.mult, ALU.mult),
                        "normed" if t == ST - 1 else None)
                ev.sync()
                for g in range(N_GRP + 1):
                    dve.wait_ge(sem("mixh_done"), 5 * l + g + 1)
                    if g == 0:
                        did(V.tensor_tensor(mixl[:, 0:N_GRP, :], plo[:, :, :], mixh[:, 0:N_GRP, :].bitcast(F32),
                                            ALU.subtract), "mix_ready")
                    else:
                        a0 = N_GRP + GT * (g - 1)
                        did(V.tensor_tensor(mixl[:, a0:a0 + GT, :], y[:, GT * (g - 1):GT * g, :],
                                            mixh[:, a0:a0 + GT, :].bitcast(F32), ALU.subtract), "mix_ready")
                b += U_WIN
                for j in range(U_WOUT):
                    split_lo(dve, Unit(b + j + AHEAD))
                b += U_WOUT

                def norm(v, end_unit):
                    dve.wait_ge(used, end_unit.multiplied)
                    for d in range(KD):
                        did(V.scalar_tensor_tensor(res[:, d, :], xT[:, d, :], ALPHA, bank[d][:, 0:T], ALU.mult,
                                                   ALU.add), "ln_res")
                    ev.sync()
                    dve.wait_ge(sem("ln_mean"), v + 1)
                    did(V.scalar_tensor_tensor(res[:, :, :], bank[0][:, 0:T].unsqueeze(1).to_broadcast([P, KD, T]),
                                               -1.0 / D, res[:, :, :], ALU.mult, ALU.add), "ln_cent")
                    dve.wait_ge(sem("ln_varmm"), v + 1)
                    did(V.tensor_scalar(lnt[:, 0, :], bank[1][:, 0:T], 1.0 / D, LN_EPS, ALU.mult, ALU.add), "ln_var")
                    dve.wait_ge(sem("ln_sqrt"), v + 1)
                    did(V.reciprocal(lnt[:, 1, :], lnt[:, 0, :]))
                    ev.sync()
                    off = R_L2G if v % 2 else R_L1G

                    def low(d):
                        dve.wait_ge(sem("x_done"), KD * (v + 1) + d + 1)
                        did(V.tensor_tensor(xl[:, d, :], xT[:, d, :], xh[:, d, :].bitcast(F32), ALU.subtract),
                            "x_ready")

                    for d in range(KD):
                        did(V.scalar_tensor_tensor(res[:, d, :], res[:, d, :], par_b[l][:, off + d:off + d + 1],
                                                   lnt[:, 1, :], ALU.mult, ALU.mult), "ln_scaled")
                        if d:
                            low(d - 1)
                    low(KD - 1)

                norm(2 * l, Unit(b - 1))
                if l == 0:
                    def product(up, s, nth):
                        dve.wait_ge(used, up.multiplied)
                        dve.wait_ge(sem("hl_done"), nth + 1)
                        for h in range(2):
                            did(V.tensor_tensor(hf[s][:, h, :], sg[s][:, h, :], bank[4 * s + 2 + h][:, 0:T],
                                                ALU.mult), "hf_done" if h else None)

                    def lower(s, f, nth):
                        dve.wait_ge(sem("hh_done"), nth + 1)
                        did(V.tensor_tensor(hl[:, f, :], hf[s][:, :, :], hh[:, f, :].bitcast(F32), ALU.subtract),
                            "hl_done")

                    with dve.Fori(0, 3) as i:
                        with loop(i, 3, hf_done=3, hl_done=3), ev.own.loop(i, 3, 3):
                            for j in range(3):
                                split_lo(dve, Unit(b + 2 * j + AHEAD, i, 6))
                                dve.wait_ge(sem("silu_done"), 3 * i + j + 1)
                                product(Unit(b + 2 * j + 1, i, 6), FFN_SET[j], 3 * i + j)
                                split_lo(dve, Unit(b + 2 * j + 1 + AHEAD, i, 6))
                                lower(FFN_SET[j], bass.ds(6 * i + 2 * j, 2), 3 * i + j)
                    for j in range(9, 11):
                        split_lo(dve, Unit(b + 2 * j + AHEAD))
                        dve.wait_ge(sem("silu_done"), j + 1)
                        product(Unit(b + 2 * j + 1), FFN_SET[j], j)
                        split_lo(dve, Unit(b + 2 * j + 1 + AHEAD))
                        lower(FFN_SET[j], slice(2 * j, 2 * j + 2), j)
                    b += U_GU
                    with dve.Fori(0, 3) as i:
                        for j in range(3):
                            split_lo(dve, Unit(b + j + AHEAD, i, 3))
                    for j in range(9, U_DN):
                        split_lo(dve, Unit(b + j + AHEAD))
                    norm(1, Unit(b + U_DN - 1))

            R = {k: t[:, :, :] for k, t in rt.items()}

            def col(name):
                return r3[name][:, 0:3]

            def wide(name):
                return r3[name][:, 0:3].unsqueeze(2).to_broadcast([P, 3, NE])

            for j in range(3):
                dve.wait_ge(sem(f"state_out{j}"), 16 * (ST // 3) * DEPTH)
            dve.wait_ge(sem("logit_mm"), 1)
            did(V.tensor_tensor(R["lg"], bank[6][:, 0:3 * NE].rearrange("p (a e) -> p a e", a=3),
                                rb[:, :].unsqueeze(1).to_broadcast([P, 3, NE]), ALU.add))
            rev = cst[:, C_REV:C_REV + NE].unsqueeze(1).to_broadcast([P, 3, NE])
            for logits, v, c, r, oh in (("lg", "v1", "c1", "r1", "oh1"), ("lg2", "v2", "c2", "r2", "oh2")):
                ev.sync()
                did(V.tensor_reduce(col(v), R[logits], AX.X, ALU.max))
                ev.sync()
                did(V.tensor_tensor(R[c], R[logits], wide(v), ALU.is_equal))
                ev.sync()
                did(V.tensor_tensor(R[c], R[c], rev, ALU.mult))
                ev.sync()
                did(V.tensor_reduce(col(r), R[c], AX.X, ALU.max))
                ev.sync()
                did(V.tensor_tensor(R[oh], R[c], wide(r), ALU.is_equal))
                if oh == "oh1":
                    ev.sync()
                    did(V.scalar_tensor_tensor(R["lg2"], R["oh1"], -3e38, R["lg"], ALU.mult, ALU.add))
            ev.sync()
            did(V.tensor_tensor(col("d"), col("v2"), col("v1"), ALU.subtract), "rt_diff")
            dve.wait_ge(sem("rt_exp"), 1)
            did(V.tensor_scalar(col("g2"), col("e"), 1.0, None, ALU.add))
            ev.sync()
            did(V.reciprocal(col("g1"), col("g2")))
            ev.sync()
            did(V.tensor_tensor(col("g2"), col("e"), col("g1"), ALU.mult))
            did(V.tensor_tensor(R["t"], R["oh1"], wide("g1"), ALU.mult))
            ev.sync()
            did(V.tensor_tensor(R["G"], R["oh2"], wide("g2"), ALU.mult))
            ev.sync()
            did(V.tensor_tensor(R["G"], R["G"], R["t"], ALU.add))
            did(V.tensor_tensor(R["M"], R["oh1"], R["oh2"], ALU.add))
            ev.sync()
            did(V.tensor_tensor(R["M"], R["M"], cst[:, C_VAL:C_VAL + 3].unsqueeze(2).to_broadcast([P, 3, NE]),
                                ALU.mult), "marks_ready")
            dve.wait_ge(sem("pos_mm"), 1)
            did(V.scalar_tensor_tensor(posm[:, :, 0:NE], bank[7][:, 0:3 * NE].rearrange("p (a e) -> p a e", a=3), 1.0,
                                       R["M"], ALU.add, ALU.mult))
            did(V.tensor_reduce(r3["r1"][:, 3:4], bank[7][:, 64:64 + NE], AX.X, ALU.max))
            ev.sync()
            did(V.tensor_scalar(posm[:, :, NE:NE + 1], posm[:, :, 0:1], -1.0 - P, None, ALU.add))
            ev.sync()
            did(V.tensor_scalar(posm[:, :, 0:NE], posm[:, :, 0:NE], -1.0, None, ALU.add))
            did(V.tensor_copy(cnti[:, 0:1], r3["r1"][:, 3:4]), "count_ready")
            for a in range(3):
                n = P if a < 2 else NS
                for h in range(2):
                    dve.wait_ge(sem("xtokh_done"), 2 * a + h + 1)
                    w = slice(512 * h, 512 * h + 512)
                    did(V.tensor_tensor(xtokl[0:n, a, w], bank[2 * a + h][0:n, :], xtokh[0:n, a, w].bitcast(F32),
                                        ALU.subtract), "xtokl_done")
            did(V.memset(gslot[:, :], 0.0))
            did(V.memset(back[:, :].bitcast(F32), 0.0), "xtokl_done")
            ev.sync()

            def choose(e):
                for a in range(3):
                    did(V.tensor_scalar(pick[:, a, :], iota, posm[:, a, e], None, ALU.is_equal), "pick_ready")

            def gathered(it):
                for h in range(2):
                    dve.wait_ge(sem("xgh_done"), 2 * it + h + 1)
                    did(V.tensor_tensor(xgl[:, 4 * h:4 * h + 4, :], bank[2 * h][:, :].rearrange("p (k s) -> p k s", k=4),
                                        xgh[:, 4 * h:4 * h + 4, :].bitcast(F32), ALU.subtract), "xgl_done")

            def outputs(s):
                for h in range(2):
                    dve.wait_ge(sem("yh_done"), 2 * s + h + 1)
                    w = slice(512 * h, 512 * h + 512)
                    did(V.scalar_tensor_tensor(yl[:, w], bank[5 + h][:, :], gslot[:, 0:1], yh[:, w].bitcast(F32),
                                               ALU.mult, ALU.subtract), "yl_done")

            def scattered(s, r, o):
                a, h = r // 2, r % 2
                n = P if a < 2 else NS
                w = slice(512 * h, 512 * h + 512)
                dve.wait_ge(sem("scat_mm"), 6 * s + r + 1)
                did(V.tensor_tensor(acc[0:n, a, w], acc[0:n, a, w], o[0:n, :], ALU.add), "acc_added")

            def item(it, s, b, e, per):
                def unit(j):
                    return Unit(b + j, e, per)

                def turned(c):
                    n = FCH[c][1] // P
                    dve.wait_ge(sem("hTh_done"), 6 * it + c + 1)
                    did(V.tensor_tensor(hTl[c % 2][:, 0:n, :], bank[4][:, 0:P * n].rearrange("p (f s) -> p f s", s=P),
                                        hTh[c % 2][:, 0:n, :].bitcast(F32), ALU.subtract), "hTl_done")

                for j in range(U_EXP):
                    split_lo(dve, unit(j + AHEAD))
                    kind, c, h = EXPERT[j]
                    if j == J_OUT:
                        outputs(s)
                    if j == J_PICK:
                        dve.wait_ge(sem("back_mm"), it + 1)
                        choose(bass.ds(e + 1, 1))
                    if j == J_GATHER + 1:
                        gathered(it + 1)
                    if kind == "g" and h and c:
                        turned(c - 1)
                    if kind == "u" and h:
                        w = FCH[c][1]
                        dve.wait_ge(used, unit(j).multiplied)
                        dve.wait_ge(sem("gate_done"), 6 * it + c + 1)
                        if c >= 2:
                            dve.wait_ge(sem("hT_mm"), 6 * it + c - 1)
                        did(V.tensor_tensor(hex_[c % 2][:, 0:w], gsl[c % 2][:, 0:w], bank[2 + c % 2][:, 0:w],
                                            ALU.mult), "h_ready")
                    if (kind, c, h) == ("d", 4, 0):
                        turned(5)
                    if J_SCATTER <= j < J_SCATTER + 6:
                        scattered(s, j - J_SCATTER, bank[7])

            def items(base, r):
                with dve.Fori(0, NE) as e:
                    with loop(e, NE, pick_ready=3, xgl_done=2, hTl_done=6, h_ready=6, yl_done=2, acc_added=6):
                        item(e + base, e + base + r, U_MOE + base * U_EXP, e, U_EXP)
                s = base + NE + r
                outputs(s)
                for k in range(6):
                    scattered(s, k, bank[TAIL[k]])
                ev.sync()

            choose(slice(0, 1))
            gathered(0)
            dve.wait_ge(sem("acc_begun"), 6)
            items(0, 0)
            over = dve.value_load(cnti[0:1, 0:1], min_val=0, max_val=T)
            with dve.If(over > P):
                for r in range(2):
                    did(V.tensor_scalar(posm[:, :, :], posm[:, :, :], -float(P), None, ALU.add), "posm_next")
                    ev.sync()
                    items(NE * (r + 1), r + 1)

            dve.wait_ge(sem("ln_bc"), 32)
            for a in range(3):
                n = P if a < 2 else NS
                for h in range(2):
                    did(V.bn_stats(r3[f"st{h}"][0:n, 0:6], acc[0:n, a, 512 * h:512 * h + 512]))
                    ev.sync()
                    did(V.tensor_copy(stat[0:n, 6 * h:6 * h + 6], r3[f"st{h}"][0:n, 0:6]))
                ev.sync()
                did(V.bn_aggr(r3["mv"][0:n, 0:2], stat[0:n, :]))
                ev.sync()
                did(V.tensor_scalar(r3["rs"][0:n, a:a + 1], r3["mv"][0:n, 1:2], LN_EPS, None, ALU.add), "fin_var")
                dve.wait_ge(sem("fin_sqrt"), a + 1)
                did(V.reciprocal(r3["rs"][0:n, a:a + 1], r3["rs"][0:n, a:a + 1]))
                ev.sync()
                did(V.tensor_scalar(acc[0:n, a, :], acc[0:n, a, :], r3["mv"][0:n, 0:1], r3["rs"][0:n, a:a + 1],
                                    ALU.subtract, ALU.mult))
                ev.sync()
                did(V.tensor_tensor(acc[0:n, a, :], acc[0:n, a, :], gbc[0:n, :], ALU.mult))
                ev.sync()
                did(V.tensor_tensor(acc[0:n, a, :], acc[0:n, a, :], bbc[0:n, :], ALU.add), "out_ready")

        @block.tensor
        def _(pe):
            M = nc.tensor

            def mm(out, a, b_, start=True, stop=True):
                return M.matmul(out, a, b_, start=start, stop=stop, skip_group_check=True)

            def turn(out, in_, k=P):
                return M.transpose(out, in_, ident[0:k, 0:k])

            M.sem_inc(used, RING)
            pe.wait_ge(sem("in_loaded"), 16 * NL)
            for k in range(KD):
                for a in range(3):
                    n = P if a < 2 else NS
                    last = turn(bank[k][:, P * a:P * a + n], xin[0:n, a, P * k:P * k + P], n)
                last.then_inc(sem("xt_turned"), 1)
            for l in range(DEPTH):
                pe.wait_ge(sem("x_done"), 2 * l + 2)
                turn(bank[2 * l][:, 0:R_A], prow[l][0:R_A, 0, :], R_A).then_inc(sem("par_turned"), 1)
                turn(bank[2 * l + 1][:, 0:R_B], prow[l][0:R_B, 1, :], R_B).then_inc(sem("par_turned"), 1)
            pe.wait_ge(sem("params_ready"), 1)
            pe.wait_ge(sem("padded"), 1)

            for l in range(DEPTH):
                b = L_BASE[l]
                pe.wait_ge(sem("hist_in"), 32 * (l + 1))
                pe.wait_ge(sem("x_ready"), KD * (2 * l + 1))
                for c in range(XT):
                    last = turn(bank[c // 4][:, 24 * (c % 4):24 * (c % 4) + 24], histc[:, P * c:P * c + P], 24)
                    if c % 4 == 3:
                        last.then_inc(sem("hist_turned"), 1)
                for g in range(N_GRP):
                    last = turn(bank[6][:, 120 * g:120 * g + 120], histp[:, P * g:P * g + P], 120)
                last.then_inc(sem("hist_turned"), 1)
                pe.wait_ge(sem("hist_done"), 2 * (l + 1))

                def columns(u, j, free):
                    pe.wait_ge(split_done, u.n + RING + 1)
                    free()
                    for h in range(2):
                        for k in range(KD):
                            wh = view(hi[u.slot], 256)[:, k, P * h:P * h + P]
                            wl = view(lo[u.slot], 256)[:, k, P * h:P * h + P]
                            last = three(bank[j + h][:, 0:T], wh, wl, xh[:, k, :], xl[:, k, :], k == 0, k == KD - 1)
                    last.then_inc(used, 1)

                with pe.Fori(0, 6) as i:
                    for j in range(3):
                        columns(Unit(b + j, i, 3), 2 * j,
                                lambda: pe.wait_ge(sem("tile_out"), tile_out(l, 6 * i + 2 * j - 4)))
                zero(bank[7][:, 0:72], 72)
                for a in range(3):
                    n = P if a < 2 else NS
                    for k in range(KD):
                        last = add(bank[7][0:n, NH * a:NH * a + NH], xT[:, k, P * a:P * a + n], wdt[l][:, k, :],
                                   stop=(a == 2 and k == KD - 1))
                last.then_inc(sem("dt_mm"), 1)
                pe.wait_ge(sem("pdiff_done"), N_GRP * (l + 1))
                pe.wait_ge(sem("tile_out"), tile_out(l, 2 * U_WIN))
                if l:
                    pe.wait_ge(sem("plw_in"), 16)
                for g in range(N_GRP):
                    mm(bank[g][:, 0:T], plw[:, g, :], pdiff[:, g, :]).then_inc(sem("pool_mm"), 1)
                pe.wait_ge(sem("tails_packed"), 18 * (l + 1))
                for c in range(XT):
                    if c % 4 == 0:
                        pe.wait_ge(sem("plo_done"), N_GRP * l + min(c // 4 + 1, N_GRP))
                    last = turn(bank[c // 4][0:27, P * (c % 4):P * (c % 4) + P], ctail[:, c, :])
                    if c % 4 == 3:
                        last.then_inc(sem("tail_turned"), 1)
                for g in range(N_GRP):
                    last = turn(bank[5][0:NB * PB, P * g:P * g + P], utail[:, g, PB:PB * (NB + 1)])
                last.then_inc(sem("tail_turned"), 1)
                for g in range(N_GRP):
                    last = turn(bank[6][0:PB, P * g:P * g + P], utail[:, g, 0:PB])
                last.then_inc(sem("tail_turned"), 1)
                pe.wait_ge(sem("dtA_ready"), l + 1)
                pe.wait_ge(sem("tail_out"), 7 * (l + 1))
                dA = dts["dtA"]
                for a in range(3):
                    mm(bank[7][:, 128 + NH * a:128 + NH * a + NH], tri if a < 2 else tri2, dA[:, a, :])
                    mm(bank[7][:, 256 + NH * a:256 + NH * a + NH], ones if a < 2 else blk2, dA[:, a, :])
                    n = P if a < 2 else NS
                    last = mm(bank[6][0:NH, P * a:P * a + n], dA[:, a, :], (tri if a < 2 else tri2)[:, 0:n])
                last.then_inc(sem("cum_mm"), 1)
                pe.wait_ge(sem("cumh"), l + 1)
                for t in range(ST):
                    for h in range(2):
                        o = bank[t // 3][HD * h:HD * h + HD, 160 * (t % 3):160 * (t % 3) + 160]
                        last = mm(o, cst[0:NH, C_ID + 2 * t + h:C_ID + 2 * t + h + 1].to_broadcast([NH, HD]),
                                  cumT[:, P:T])
                    if t % 3 == 2:
                        last.then_inc(sem("ecp_mm"), 1)
                pe.wait_ge(sem("xact_done"), XT * (l + 1))
                pe.wait_ge(sem("cuml"), l + 1)
                pe.wait_ge(sem("ecp_done"), 4 * (l + 1))
                for bl in range(3):
                    n = P if bl < 2 else NS
                    q = 3 * l + bl
                    w = slice(P * bl, P * bl + n)
                    if bl == 1:
                        pe.wait_ge(sem("h1_done"), 4 * (l + 1))
                    if bl == 2:
                        pe.wait_ge(sem("h2_done"), 4 * (l + 1))
                    for t in range(ST):
                        last = turn(bank[t // 4][0:n, P * (t % 4):P * (t % 4) + P], xact[:, t, w])
                        if t % 4 == 3:
                            last.then_inc(sem("x_turned"), 1)
                    for g in range(N_GRP):
                        last = turn(bank[3][0:n, P * g:P * g + P], xact[:, ST + g, w])
                    last.then_inc(sem("b_turned"), 1)
                    for g in range(N_GRP):
                        last = mm(bank[4][0:n, n * g:n * g + n], xact[:, ST + g, w], xact[:, ST + N_GRP + g, w])
                    last.then_inc(sem("cb_mm"), 1)
                    pe.wait_ge(sem("xdt_ready"), 3 * (q + 1))
                    pe.wait_ge(sem("btok_ready"), q + 1)

                    def sums(g):
                        if g >= 2:
                            pe.wait_ge(sem("seg_ready"), 4 * q + g - 1)
                        for x in range(HG):
                            o = bank[2 * (g % 2) + x // 4][:, n * (x % 4):n * (x % 4) + n]
                            s_ = selc[:, HG * g + x:HG * g + x + 1].to_broadcast([NH, P])
                            mm(o, s_, cumTh[:, w], True, False)
                            last = mm(o, s_, cumTl[:, w], False, True)
                        last.then_inc(sem("bc_mm"), 1)

                    def inside(g):
                        k = 4 * q + g
                        pe.wait_ge(sem("decay_masked"), k + 1)
                        pe.wait_ge(sem("y_diag"), k)
                        for x in range(HG):
                            h = HG * g + x
                            last = mm(bank[5][HD * (x % 2):HD * (x % 2) + HD, n * (x // 2):n * (x // 2) + n],
                                      xdt[0:n, HD * h:HD * h + HD], dec[g % 2][0:n, x, 0:n])
                        last.then_inc(sem("ydiag_mm"), 1)

                    sums(0)
                    for g in range(N_GRP):
                        if g + 1 < N_GRP:
                            sums(g + 1)
                        inside(g)
                    if bl == 1:
                        for g in range(N_GRP):
                            if g or l:
                                pe.wait_ge(sem("yoff1_done"), N_GRP * l + g)
                            for t in range(GT):
                                last = mm(bank[6][:, P * t:P * t + P], hT[:, P * (GT * g + t):P * (GT * g + t) + P],
                                          xact[:, ST + N_GRP + g, w])
                            last.then_inc(sem("yoff1_mm"), 1)
                    if bl < 2:
                        pe.wait_ge(sem("wx_ready"), q + 1)
                        pe.wait_ge(sem("seg_ready"), 4 * q + 4)
                        for g in range(N_GRP):
                            mm(bank[g][:, 0:384], btok[:, g, :], wx[:, 384 * g:384 * g + 384])\
                                .then_inc(sem("state_mm"), 1)
                pe.wait_ge(sem("y_diag"), 12 * (l + 1))
                for t in range(ST):
                    last = turn(bank[4 + t // 4][:, P * (t % 4):P * (t % 4) + P], hT[:, P * t:P * t + P])
                    if t % 4 == 3:
                        last.then_inc(sem("h_turned"), 1)
                pe.wait_ge(sem("seg_ready"), 12 * (l + 1))
                pe.wait_ge(sem("wx_ready"), 3 * (l + 1))
                for t in range(ST):
                    pe.wait_ge(sem(f"state_in{t % 3}"), 16 * (4 * l + t // 3 + 1))
                    if t:
                        pe.wait_ge(sem("h0T_ready"), ST * l + t)
                    for i in range(NB):
                        last = turn(bank[i // 4][:, P * (i % 4):P * (i % 4) + P], h0[t % 3][:, i, :])
                    last.then_inc(sem("h0_turned"), 1)
                    pe.wait_ge(sem("bblk_ready"), N_GRP * l + t // GT + 1)
                    if t:
                        pe.wait_ge(sem("state_new"), ST * l + t)
                    for h in range(2):
                        last = mm(bank[2 + h][:, :], wx[0:NS, P * t:P * t + P], bblk[:, 4 * h:4 * h + 4, :])
                    last.then_inc(sem("update_mm"), 1)
                    pe.wait_ge(sem("h0T_ready"), ST * l + t + 1)
                    for i in range(NB):
                        last = mm(bank[7][:, NS * t + DL * i:NS * t + DL * i + DL], h0T[:, i, :],
                                  xact[:, ST + N_GRP + t // GT, SEQ + DL * i:SEQ + DL * i + DL])
                    last.then_inc(sem("yoff_mm"), 1)
                for g in range(N_GRP):
                    pe.wait_ge(sem("sq_done"), N_GRP * l + g + 1)
                    for t in range(GT):
                        last = mm(bank[g][:, 0:T], ones, sq[:, GT * g + t, :], t == 0, t == GT - 1)
                    last.then_inc(sem("rms_mm"), 1)
                b += U_WIN

                def rows(u, mh, ml, k0, start, stop):
                    pe.wait_ge(split_done, u.n + RING + 1)
                    for kk in range(2):
                        for d in range(KD):
                            wh = view(hi[u.slot], D)[:, kk, P * d:P * d + P]
                            wl = view(lo[u.slot], D)[:, kk, P * d:P * d + P]
                            kx = bass.ds(k0 + kk, 1) if not isinstance(k0, int) else slice(k0 + kk, k0 + kk + 1)
                            last = three(bank[d][:, 0:T], wh, wl, mh[:, kx, :], ml[:, kx, :],
                                         start and kk == 0, stop and kk == 1)
                    last.then_inc(used, 1)

                pe.wait_ge(sem("rms_in"), l + 1)
                for j in range(U_WOUT):
                    if j in (0, 2, 3, 5, 6):
                        pe.wait_ge(sem("mix_ready"), 5 * (l + 1))
                    rows(Unit(b + j), mixh, mixl, 2 * j, j == 0, j == U_WOUT - 1)
                b += U_WOUT

                def norm(v):
                    for d in range(KD):
                        pe.wait_ge(sem("ln_res"), KD * v + d + 1)
                        last = mm(bank[0][:, 0:T], ones, res[:, d, :], d == 0, d == KD - 1)
                    last.then_inc(sem("ln_mean"), 1)
                    for d in range(KD):
                        pe.wait_ge(sem("ln_sq"), 2 * v + d // 4 + 1)
                        last = mm(bank[1][:, 0:T], ones, lsq[:, d, :], d == 0, d == KD - 1)
                    last.then_inc(sem("ln_varmm"), 1)
                    pe.wait_ge(sem("x_ready"), KD * (v + 2))

                norm(2 * l)
                if l == 0:
                    def pair(un, s, need):
                        pe.wait_ge(sem("hf_done"), need)
                        for x in range(2):
                            columns(un(x), 4 * s + 2 * x, lambda: None)

                    with pe.Fori(0, 3) as i:
                        for j in range(3):
                            pair(lambda x: Unit(b + 2 * j + x, i, 6), FFN_SET[j], 3 * i + (1, 0, 2)[j])
                    for j in range(9, 11):
                        pair(lambda x: Unit(b + 2 * j + x), FFN_SET[j], j)
                    b += U_GU
                    pe.wait_ge(sem("hl_done"), 12)
                    for d in range(KD):
                        zero(bank[d][:, 0:T], T)
                    with pe.Fori(0, 3) as i:
                        for j in range(3):
                            rows(Unit(b + j, i, 3), hh, hl, 6 * i + 2 * j, False, False)
                    for j in range(9, U_DN):
                        rows(Unit(b + j), hh, hl, 2 * j, False, j == U_DN - 1)
                    norm(1)

            for a in range(3):
                n = P if a < 2 else NS
                for k in range(KD):
                    last = turn(bank[2 * a + k // 4][0:n, P * (k % 4):P * (k % 4) + P], xT[:, k, P * a:P * a + n])
                    if k % 4 == 3:
                        last.then_inc(sem("tok_turned"), 1)
            zero(bank[6][:, 0:3 * NE], 3 * NE)
            for a in range(3):
                n = P if a < 2 else NS
                for k in range(KD):
                    last = add(bank[6][0:n, NE * a:NE * a + NE], xT[:, k, P * a:P * a + n], rw[:, k, :],
                               stop=(a == 2 and k == KD - 1))
            last.then_inc(sem("logit_mm"), 1)
            pe.wait_ge(sem("marks_ready"), 1)
            Mk = rt["M"]
            zero(bank[7][:, 0:64 + NE], 64 + NE)
            for a in range(3):
                for b_ in range(a):
                    add(bank[7][:, NE * a:NE * a + NE], ones, Mk[:, b_, :])
                add(bank[7][:, NE * a:NE * a + NE], stri, Mk[:, a, :])
                last = add(bank[7][:, 64:64 + NE], ones, Mk[:, a, :], stop=(a == 2))
            last.then_inc(sem("pos_mm"), 1)
            pe.wait_ge(sem("xtokl_done"), 7)
            pe.wait_ge(sem("acc_begun"), 6)
            pe.wait_ge(sem("count_ready"), 1)

            def gather(it):
                pe.wait_ge(sem("pick_ready"), 3 * it + 3)
                for h in range(2):
                    for k in range(4 * h, 4 * h + 4):
                        for a in range(3):
                            n = P if a < 2 else NS
                            for x in (xtokh, xtokl):
                                last = mm(bank[2 * h][:, P * (k % 4):P * (k % 4) + P], x[0:n, a, P * k:P * k + P],
                                          pick[0:n, a, :], a == 0 and x is xtokh, a == 2 and x is xtokl)
                    last.then_inc(sem("xg_mm"), 1)

            def scatter(s, r, o):
                a, h = r // 2, r % 2
                w = slice(512 * h, 512 * h + 512)
                mm(o[:, :], back[:, P * a:P * a + P], yh[:, w], True, False)
                mm(o[:, :], back[:, P * a:P * a + P], yl[:, w], False, True).then_inc(sem("scat_mm"), 1)

            def clear_outputs():
                for h in range(2):
                    for w in range(2):
                        mm(bank[5 + h][:, 256 * w:256 * w + 256], zer[:, 0:P], zer[:, 0:256])

            def item(it, s, b, e, per):
                def unit(j):
                    return Unit(b + j, e, per)

                pe.wait_ge(sem("xgh_done"), 2 * it + 2)
                pe.wait_ge(sem("xgl_done"), 2 * it + 2)

                def turns(c):
                    pe.wait_ge(sem("h_ready"), 6 * it + c + 1)
                    if c:
                        pe.wait_ge(sem("hTl_done"), 6 * it + c)
                    for f in range(FCH[c][1] // P):
                        last = turn(bank[4][:, P * f:P * f + P], hex_[c % 2][:, P * f:P * f + P])
                    last.then_inc(sem("hT_mm"), 1)

                for j in range(U_EXP):
                    u = unit(j)
                    kind, c, h = EXPERT[j]
                    pe.wait_ge(split_done, u.n + RING + 1)
                    w = FCH[c][1]
                    if kind in "gu":
                        if kind == "g" and c >= 2 and h != 1:
                            pe.wait_ge(sem("h_ready"), 6 * it + c - 1)
                        o = bank[c % 2 + (0 if kind == "g" else 2)][:, 0:w]
                        ks = range(4 * h, 4 * h + 4) if h < 2 else range(KD)
                        for i, k in enumerate(ks):
                            last = three_t(o, xgh[:, k, :], xgl[:, k, :], view(hi[u.slot], w)[:, i, :],
                                           view(lo[u.slot], w)[:, i, :], k == 0, k == KD - 1)
                    else:
                        if h != 1:
                            pe.wait_ge(sem("hTl_done"), 6 * it + c + 1)
                        nf = w // P
                        for y_ in ((h,) if h < 2 else (0, 1)):
                            vw = 512 if h < 2 else D
                            x0 = 0 if h < 2 else 512 * y_
                            for f in range(nf):
                                last = three_t(bank[5 + y_][:, :], hTh[c % 2][:, f, :], hTl[c % 2][:, f, :],
                                               view(hi[u.slot], vw)[:, f, x0:x0 + 512],
                                               view(lo[u.slot], vw)[:, f, x0:x0 + 512],
                                               c == 0 and f == 0, c == 5 and f == nf - 1)
                    last.then_inc(used, 1)
                    if kind == "g" and h and c:
                        turns(c - 1)
                    if (kind, c, h) == ("d", 4, 0):
                        turns(5)
                    if J_SCATTER <= j < J_SCATTER + 6:
                        r = j - J_SCATTER
                        if r == 0:
                            pe.wait_ge(sem("yl_done"), 2 * s + 2)
                        pe.wait_ge(sem("acc_added"), 6 * s + r + 1)
                        scatter(s, r, bank[7])
                    if j == J_BACK:
                        pe.wait_ge(sem("acc_added"), 6 * s + 7)
                        for a in range(3):
                            n = P if a < 2 else NS
                            turn(bank[7][:, P * a:P * a + n], pick[0:n, a, :].bitcast(F32), n)
                        for a in range(3):
                            last = mm(bank[7][:, T:T + 1], pick[:, a, :].bitcast(F32), rt["G"][:, a, bass.ds(e, 1)],
                                      a == 0, a == 2)
                        last.then_inc(sem("back_mm"), 1)
                    if j == J_GATHER:
                        pe.wait_ge(sem("h_ready"), 6 * it + 5)
                        gather(it + 1)

            def items(base, r):
                with pe.Fori(0, NE) as e:
                    item(e + base, e + base + r, U_MOE + base * U_EXP, e, U_EXP)
                s = base + NE + r
                pe.wait_ge(sem("yl_done"), 2 * s + 2)
                for k in range(6):
                    pe.wait_ge(sem("acc_added"), 6 * s + max(k - 4, -1) + 2)
                    scatter(s, k, bank[TAIL[k]])

            gather(0)
            clear_outputs()
            items(0, 0)
            over = pe.value_load(cnti[0:1, 0:1], min_val=0, max_val=T)
            with pe.If(over > P):
                for r in range(2):
                    clear_outputs()
                    items(NE * (r + 1), r + 1)


_INS = ['x_prompt', 'x_sample', 'state_pool', 'state_conv', 'state_ssm', 'w_in', 'conv_w', 'conv_b', 'dt_bias',
        'A_log', 'D_skip', 'ssm_norm_w', 'pool_w', 'pool_scale', 'w_out', 'ln1_g', 'ln1_b', 'ln2_g', 'ln2_b',
        'ffn_w_gate', 'ffn_w_up', 'ffn_w_down', 'router_w', 'router_b', 'moe_w_gate', 'moe_w_up', 'moe_w_down']
_OUTS = [(1, SEQ, D), (NB, DL, D), (DEPTH, 1, PB, D_POOL), (DEPTH, 1, HIST, D_XBC), (DEPTH, 1, NH, HD, N_STATE),
         (DEPTH, NB, PB, D_POOL), (DEPTH, NB, HIST, D_XBC), (DEPTH, NB, NH, HD, N_STATE)]


def kernel(**inputs):
    import concourse.bacc as _bacc
    from concourse.bass_utils import run_bass_kernel_spmd as _run

    nc = _bacc.Bacc("TRN2", target_bir_lowering=False, num_devices=1)
    arrays, args = {}, []
    for name in _INS + ["consts"]:
        a = shape_constants() if name == "consts" else np.ascontiguousarray(inputs[name])
        arrays[f"in_{name}_dram"] = a
        args.append(nc.dram_tensor(f"in_{name}_dram", a.shape, mybir.dt.from_np(a.dtype), kind="ExternalInput").ap())
    for i, shape in enumerate(_OUTS):
        args.append(nc.dram_tensor(f"out_{i}_dram", shape, F32, kind="ExternalOutput").ap())
    trunk(nc, *args)
    r = _run(nc, [arrays], core_ids=[0])
    return tuple(r.results[0][f"out_{i}_dram"] for i in range(len(_OUTS)))
```

```python
from contextlib import ExitStack

import numpy as np

import concourse.bass as bass
from concourse import mybir

F32 = mybir.dt.float32
F32R = mybir.dt.float32r
I32 = mybir.dt.int32
ALU = mybir.AluOpType
ACT = mybir.ActivationFunctionType
AX = mybir.AxisListType

P = 128
D = 1024
SEQ = 256
NB, DL = 8, 4
NS = NB * DL
T = SEQ + NS
KD = D // P
D_POOL, D_SSM, N_STATE, N_GRP, NH, HD = 512, 1536, 128, 4, 24, 64
D_XBC = D_SSM + 2 * N_GRP * N_STATE
D_IN = D_POOL + D_SSM + D_XBC + NH
CW = 4
HIST = CW - 1
PB = 15
WINDOWS = (2, 4, 8, 16)
D_FF = 2816
NE = 8
DEPTH = 2
ALPHA = (2.0 * DEPTH) ** 0.25
LN_EPS, RMS_EPS = 1e-5, 1e-6

XT = D_XBC // P
ST = D_SSM // P
GT = ST // N_GRP
MT = (D_POOL + D_SSM) // P
FT = D_FF // P
HG = NH // N_GRP

CSEG = HIST + DL
CLINE = HIST + SEQ + NB * CSEG + 1
CS0 = HIST + SEQ
COUT = CLINE - 1 - HIST
PSEG = PB + DL
PLINE = PB + SEQ + NB * PSEG
PS0 = PB + SEQ

UNIT = 2048
RING = 3
AHEAD = 2
FFN_SET = 3 * [0, 1, 0] + [1, 0]
U_WIN, U_WOUT, U_GU, U_DN = 18, 8, 22, 11
L_BASE = (0, U_WIN + U_WOUT + U_GU + U_DN)
TILE_BANKS = 6
TAIL = (7, 1, 3, 4, 7, 1)
U_MOE = L_BASE[1] + U_WIN + U_WOUT
FCH = [(c * 512, min(512, D_FF - c * 512)) for c in range(6)]


def expert_units():
    out = []

    def down(c):
        f0, w = FCH[c]
        if w == 512:
            out.extend([("d", c, 0), ("d", c, 1)])
        else:
            out.append(("d", c, 2))

    for c, (f0, w) in enumerate(FCH):
        for kind in "gu":
            if w == 512:
                out.extend([(kind, c, 0), (kind, c, 1)])
            else:
                out.append((kind, c, 2))
        if c:
            down(c - 1)
    down(len(FCH) - 1)
    return out


EXPERT = expert_units()
U_EXP = len(EXPERT)
J_OUT = 1
J_SCATTER = range(2, 14, 2)
J_BACK = 14
J_PICK = 16
J_COPY = EXPERT.index(("u", 5, 2))
J_GATHER = (19, 22, J_COPY - 2, J_COPY)
XG = (7, 0)
assert U_EXP % RING == 0

C_ID, C_TRI, C_TRI2, C_ONES, C_BLK2, C_STRI, C_IOTA = (i * P for i in range(7))
C_REV = 7 * P
C_INVC = C_REV + NE
C_BM = C_INVC + 4 * 16
C_VAL = C_BM + NB
C_N = C_VAL + 3


def shape_constants():
    c = np.zeros((P, C_N), np.float32)
    i = np.arange(P)
    c[:, C_ID:C_ID + P] = np.eye(P)
    c[:, C_TRI:C_TRI + P] = i[:, None] <= i[None, :]
    same = (i[:, None] // DL == i[None, :] // DL) & (i[:, None] < NS) & (i[None, :] < NS)
    c[:, C_TRI2:C_TRI2 + P] = same & (i[:, None] <= i[None, :])
    c[:, C_ONES:C_ONES + P] = 1.0
    c[:, C_BLK2:C_BLK2 + P] = same
    c[:, C_STRI:C_STRI + P] = i[:, None] < i[None, :]
    c[:, C_IOTA:C_IOTA + P] = i[None, :]
    c[:, C_REV:C_REV + NE] = NE - np.arange(NE)[None, :]
    for g, w in enumerate(WINDOWS):
        c[:, C_INVC + 16 * g:C_INVC + 16 * g + 16] = 1.0 / np.minimum(np.arange(16) + 1, w)
    c[:, C_BM:C_BM + NB] = i[:, None] // DL == np.arange(NB)[None, :]
    c[:, C_VAL:C_VAL + 2] = 1.0
    c[:NS, C_VAL + 2] = 1.0
    return c


R_CW, R_CB, R_NW, R_PS, R_A = 0, CW * XT, CW * XT + XT, CW * XT + XT + ST, CW * XT + XT + ST + N_GRP
R_L1G, R_L1B, R_L2G, R_L2B, R_B = 0, KD, 2 * KD, 3 * KD, 4 * KD


class Unit:

    def __init__(self, k, it=0, per=0):
        assert per % RING == 0
        self.slot = k % RING
        self.n = k + per * it if per else k
        self.round = k // RING + (per // RING) * it if per else k // RING

    @property
    def multiplied(self):
        return self.n + RING + 1


class Count:

    def __init__(self, sem):
        self.sem, self.n, self.it, self.per = sem, 0, 0, 0

    def value(self):
        return self.n + self.per * self.it if self.per else self.n

    def loop(self, it, per, times):
        return _Loop(self, it, per, times)


class _Loop:
    def __init__(self, count, it, per, times):
        self.c, self.new, self.times = count, (it, per), times

    def __enter__(self):
        c = self.c
        self.start = c.n
        c.it, c.per = self.new
        return c

    def __exit__(self, *error):
        c = self.c
        if error[0] is None:
            assert c.n - self.start == self.new[1], (c.n - self.start, self.new[1])
        c.n = self.start + self.new[1] * self.times
        c.it, c.per = 0, 0


class Order:

    def __init__(self, engine, sem):
        self.engine, self.own, self.last = engine, Count(sem), None

    def did(self, ins, event=None):
        c = event or self.own
        ins.then_inc(c.sem, 1)
        c.n += 1
        self.last = c
        return ins

    def sync(self):
        self.engine.wait_ge(self.last.sem, self.last.value())


def trunk(nc, x_prompt, x_sample, state_pool, state_conv, state_ssm, w_in, conv_w, conv_b, dt_bias, A_log, D_skip,
          ssm_norm_w, pool_w, pool_scale, w_out, ln1_g, ln1_b, ln2_g, ln2_b, ffn_w_gate, ffn_w_up, ffn_w_down,
          router_w, router_b, moe_w_gate, moe_w_up, moe_w_down, consts,
          y_prompt, y_sample, pool_p, conv_p, ssm_p, pool_s, conv_s, ssm_s):
    with ExitStack() as ctx:
        base = -(-nc.sbuf_base // 64) * 64
        end = nc.sbuf_usable_end

        def at(name, shape, offset, dt=F32):
            size = 4 * int(np.prod(shape[1:]))
            assert offset % 32 == 0, name
            assert base + offset + size <= end, (name, base + offset + size, end)
            return nc.alloc_sbuf_tensor_at(name, shape, dt, offset=base + offset)

        sems = {}

        def sem(name):
            if name not in sems:
                sems[name] = ctx.enter_context(nc.semaphore(name))
            return sems[name]

        class Memory:

            def __init__(self, o):
                self.o = o

            def take(self, name, shape, dt=F32):
                t = at(name, shape, self.o, dt)
                self.o += -(-4 * int(np.prod(shape[1:])) // 32) * 32
                return t

        m = Memory(0)
        raw = [m.take(f"raw{i}", [P, UNIT]) for i in range(RING)]
        hi = [m.take(f"hi{i}", [P, UNIT], F32R) for i in range(RING)]
        lo = [m.take(f"lo{i}", [P, UNIT], F32R) for i in range(RING)]
        xT = m.take("xT", [P, KD, T])
        m2 = Memory(m.o)
        xh = m.take("xh", [P, KD, T], F32R)
        xl = m.take("xl", [P, KD, T], F32R)
        y = m2.take("y", [P, ST, T])
        utail = m2.take("utail", [P, N_GRP, (NB + 1) * PB])
        assert m2.o <= m.o
        cst = m.take("cst", [P, C_N])
        par_a = [m.take(f"par_a{l}", [P, R_A]) for l in range(DEPTH)]
        par_b = [m.take(f"par_b{l}", [P, R_B]) for l in range(DEPTH)]
        bias_h = [m.take(f"bias_h{l}", [P, NH]) for l in range(DEPTH)]
        alog = [m.take(f"alog{l}", [P, NH]) for l in range(DEPTH)]
        dsk = [m.take(f"dsk{l}", [P, ST]) for l in range(DEPTH)]
        dskb = [m.take(f"dskb{l}", [P, NH]) for l in range(DEPTH)]
        wdt = [m.take(f"wdt{l}", [P, KD, NH]) for l in range(DEPTH)]
        plw = m.take("plw", [P, N_GRP, P])
        rw = m.take("rw", [P, KD, NE])
        rb = m.take("rb", [P, NE])
        dts = {n: m.take("dt_" + n, [P, 3, NH]) for n in
               ("v", "a", "e", "s", "s2", "p", "dt", "dtA", "cum", "tot", "ew", "etot")}
        expA = m.take("expA", [P, NH])
        cumT = m.take("cumT", [P, T])
        cumTh = m.take("cumTh", [P, T], F32R)
        cumTl = m.take("cumTl", [P, T], F32R)
        selc = m.take("selc", [P, NH], F32R)
        zer = m.take("zer", [P, P], F32R)
        arena = m.o

        def ar(o):
            return Memory(arena + o)

        m = ar(0)
        zs = m.take("zs", [P, ST, T])
        o_conv = m.o - arena
        conv = m.take("conv", [P, XT, CLINE])
        o_pad = m.o - arena
        xpad = m.take("xpad", [P, XT, CLINE])
        upad = m.take("upad", [P, N_GRP, PLINE])
        o_h = m.o - arena
        histc = ar(o_h).take("histc", [NB * HIST, D_XBC])
        win_a = m.take("win_a", [P, N_GRP, PLINE])
        win_b = m.take("win_b", [P, N_GRP, PLINE])
        histp = ar(m.o - arena).take("histp", [NB * PB, D_POOL])
        pdiff = m.take("pdiff", [P, N_GRP, T])
        ctail = m.take("ctail", [P, XT, (NB + 1) * HIST])
        xact = ar(o_pad).take("xact", [P, XT, T])
        m = ar(o_conv)
        ecp = m.take("ecp", [P, ST, P + NS])
        m3 = ar(m.o - arena)
        h0T = [m3.take(f"h0T{i}", [P, NB, P]) for i in range(2)]
        bblk = m3.take("bblk", [P, NB, P])
        m4 = ar(m.o - arena)
        tailp_s = m4.take("tailp_s", [NB * PB, D_POOL])
        tailp_p = m4.take("tailp_p", [PB, D_POOL])
        hT = m.take("hT", [P, D_SSM])
        assert m4.o <= m.o
        xdt = m.take("xdt", [P, D_SSM])
        assert m3.o <= m.o
        btok = m.take("btok", [P, N_GRP, P])
        m3 = ar(m.o - arena)
        yst = [m3.take(f"yst{i}", [NS, GT * P]) for i in range(2)]
        cbT = m.take("cbT", [P, N_GRP, P])
        assert m3.o - arena <= o_pad
        assert m.o - arena <= o_pad
        m = ar(o_pad + 4 * XT * T)
        wx = m.take("wx", [P, D_SSM])
        o_dec = m.o - arena
        dec = [m.take(f"dec{i}", [P, HG, P]) for i in range(2)]
        hout = ar(o_dec).take("hout", [P, ST, P])
        plo = m.take("plo", [P, N_GRP, T])
        tailc = ar(m.o - arena).take("tailc", [HIST * (NB + 1), D_XBC])
        h0 = [m.take(f"h0_{i}", [P, NB, P]) for i in range(3)]
        ytmp = m.take("ytmp", [P, GT * P])
        calone = m.take("calone", [P, NB * (NS + DL)])
        sq = ar(0).take("sq", [P, ST, T])
        rms = ar(o_pad).take("rms", [P, N_GRP, T])
        m = ar(0)
        mixh = m.take("mixh", [P, MT, T], F32R)
        mixl = m.take("mixl", [P, MT, T], F32R)
        lsq = m.take("lsq", [P, KD, T])
        lnt = m.take("lnt", [P, 2, T])
        m = ar(0)
        hh = m.take("hh", [P, FT, T], F32R)
        hl = m.take("hl", [P, FT, T], F32R)
        sg = [m.take(f"sg{i}", [P, 2, T]) for i in range(2)]
        hf = [m.take(f"hf{i}", [P, 2, T]) for i in range(2)]
        res = m.take("res", [P, KD, T])
        assert m.o - arena <= o_h
        m = ar(0)
        xin = m.take("xin", [P, 3, D])
        prow = [m.take(f"prow{l}", [P, 2, P]) for l in range(DEPTH)]
        m = ar(0)
        xtokh = m.take("xtokh", [P, 3, D], F32R)
        xtokl = m.take("xtokl", [P, 3, D], F32R)
        acc = m.take("acc", [P, 3, D])
        xgh = m.take("xgh", [P, KD, P], F32R)
        xgl = m.take("xgl", [P, KD, P], F32R)
        pick = m.take("pick", [P, 3, P], F32R)
        back = m.take("back", [P, 3 * P], F32R)
        gsl = [m.take(f"gsl{i}", [P, 512]) for i in range(2)]
        hex_ = [m.take(f"hex{i}", [P, 512]) for i in range(2)]
        hTh = [m.take(f"hTh{i}", [P, 4, P], F32R) for i in range(2)]
        hTl = [m.take(f"hTl{i}", [P, 4, P], F32R) for i in range(2)]
        yh = m.take("yh", [P, D], F32R)
        yl = m.take("yl", [P, D], F32R)
        gbc = m.take("gbc", [P, D])
        bbc = m.take("bbc", [P, D])
        gslot = m.take("gslot", [P, 8])
        rt = {n: m.take("rt_" + n, [P, 3, NE]) for n in ("lg", "c1", "oh1", "lg2", "c2", "oh2", "G", "M", "t")}
        posm = m.take("posm", [P, 3, NE + 1])
        r3 = {n: m.take("r3_" + n, [P, 8]) for n in
              ("v1", "r1", "v2", "r2", "d", "e", "g1", "g2", "st0", "st1", "mv", "rs")}
        cnti = m.take("cnti", [P, 8], I32)
        stat = m.take("stat", [P, 12])

        bank = [ctx.enter_context(nc.psum_tensor(f"bank{i}", [P, 512], F32)) for i in range(8)]

        ident = cst[:, C_ID:C_ID + P]
        tri = cst[:, C_TRI:C_TRI + P]
        tri2 = cst[:, C_TRI2:C_TRI2 + P]
        ones = cst[:, C_ONES:C_ONES + P]
        blk2 = cst[:, C_BLK2:C_BLK2 + P]
        stri = cst[:, C_STRI:C_STRI + P]
        iota = cst[:, C_IOTA:C_IOTA + P]

        def csamples(line, k0=0, n=DL):
            return line.rearrange("p (b k) -> p b k", k=CSEG)[:, :, k0:k0 + n]

        def by_sample(ap):
            return ap.rearrange("p (b k) -> p b k", k=DL)

        landed = [sem(f"landed{i}") for i in range(RING)]
        split_done = sem("split_done")
        hi_done = sem("hi_done")
        used = sem("used")

        HALVES = (slice(0, UNIT // 2), slice(UNIT // 2, UNIT))

        def split_hi(act, u):
            act.wait_ge(landed[u.slot], 16 * u.round + 16)
            act.wait_ge(used, u.n + 1)
            for w in HALVES:
                nc.scalar.copy(hi[u.slot][:, w], raw[u.slot][:, w]).then_inc(hi_done, 1)

        def split_lo(dve, u):
            for i, w in enumerate(HALVES):
                dve.wait_ge(hi_done, 2 * u.n + i + 1)
                last = nc.vector.tensor_tensor(lo[u.slot][:, w], raw[u.slot][:, w], hi[u.slot][:, w].bitcast(F32),
                                               ALU.subtract)
            last.then_inc(split_done, 1)

        def three(out, wh, wl, mh, ml, start, stop):
            nc.tensor.matmul(out, wh, mh, start=start, stop=False, skip_group_check=True)
            nc.tensor.matmul(out, wh, ml, start=False, stop=False, skip_group_check=True)
            return nc.tensor.matmul(out, wl, mh, start=False, stop=stop, skip_group_check=True)

        def three_t(out, xh_, xl_, wh, wl, start, stop):
            nc.tensor.matmul(out, xh_, wh, start=start, stop=False, skip_group_check=True)
            nc.tensor.matmul(out, xl_, wh, start=False, stop=False, skip_group_check=True)
            return nc.tensor.matmul(out, xh_, wl, start=False, stop=stop, skip_group_check=True)

        def zero(out, n, m_=P):
            nc.tensor.matmul(out, zer[:, 0:m_], zer[:, 0:1].to_broadcast([P, n]), start=True, stop=False,
                             skip_group_check=True)

        def add(out, a, b, stop=False):
            return nc.tensor.matmul(out, a, b, start=False, stop=stop, skip_group_check=True)

        def view(t, w):
            return t[:, :].rearrange("p (k c) -> p k c", c=w)

        wv = [w_in[l].rearrange("(k p) c -> p k c", p=P) for l in range(DEPTH)]
        gv = ffn_w_gate[0].rearrange("(k p) c -> p k c", p=P)
        uv = ffn_w_up[0].rearrange("(k p) c -> p k c", p=P)
        ov = [w_out[l].rearrange("(k p) c -> p k c", p=P) for l in range(DEPTH)]
        dv = ffn_w_down[0].rearrange("(k p) c -> p k c", p=P)
        egv = moe_w_gate[0].rearrange("e (k p) c -> e p k c", p=P)
        euv = moe_w_up[0].rearrange("e (k p) c -> e p k c", p=P)
        edv = moe_w_down[0].rearrange("e (k p) c -> e p k c", p=P)
        XCOL = D_POOL + D_SSM
        NL = DEPTH * 12 + 3

        block = ctx.enter_context(nc.Block())

        @block.sync
        def _(sp):
            q = sem("x_loaded")
            sp.dma_start(cst[:, :], consts).then_inc(q, 16)
            sp.dma_start(xin[:, 0:2, :], x_prompt[0].rearrange("(a p) d -> p a d", p=P)).then_inc(q, 16)
            sp.dma_start(xin[0:NS, 2, :], x_sample.rearrange("b t d -> (b t) d")).then_inc(q, 16)

            def small_parameters():
                q = sem("in_loaded")
                loads = 0

                def first(out, src):
                    nonlocal loads
                    sp.dma_start(out, src).then_inc(q, 16)
                    loads += 1

                for l in range(DEPTH):
                    for row, src, n in ((R_CW, conv_w[l].rearrange("k (t p) -> (k t) p", p=P), CW * XT),
                                        (R_CB, conv_b[l].rearrange("(t p) -> t p", p=P), XT),
                                        (R_NW, ssm_norm_w[l].rearrange("(t p) -> t p", p=P), ST),
                                        (R_PS, pool_scale[l].rearrange("(t p) -> t p", p=P), N_GRP)):
                        first(prow[l][row:row + n, 0, :], src)
                    for row, src in ((R_L1G, ln1_g), (R_L1B, ln1_b), (R_L2G, ln2_g), (R_L2B, ln2_b)):
                        first(prow[l][row:row + KD, 1, :], src[l].rearrange("(t p) -> t p", p=P))
                    first(bias_h[l][:, :], dt_bias[l:l + 1, :].to_broadcast([P, NH]))
                    first(alog[l][:, :], A_log[l:l + 1, :].to_broadcast([P, NH]))
                    first(dskb[l][:, :], D_skip[l:l + 1, :].to_broadcast([P, NH]))
                    first(wdt[l][:, :, :], wv[l][:, :, D_IN - NH:D_IN])
                first(rw[:, :, :], router_w[0].rearrange("(k p) e -> p k e", p=P))
                first(rb[:, :], router_b[0:1, :].to_broadcast([P, NE]))
                first(plw[:, :, :], pool_w[0].rearrange("g c d -> c g d"))
                assert loads == NL, loads

            def load(u, w, src):
                sp.wait_ge(split_done, u.n + 1)
                sp.dma_start(view(raw[u.slot], w), src).then_inc(landed[u.slot], 16)

            for l in range(DEPTH):
                b = L_BASE[l]
                for j in range(3):
                    load(Unit(b + j), 256, wv[l][:, :, XCOL + 256 * j:XCOL + 256 * j + 256])
                if l == 0:
                    small_parameters()
                with sp.Fori(0, 2) as i:
                    for j in range(3):
                        load(Unit(b + 3 + j, i, 3), 256, wv[l][:, :, bass.ds(XCOL + 256 * (3 + j) + 768 * i, 256)])
                load(Unit(b + 9), 256, wv[l][:, :, XCOL + 2304:XCOL + 2560])
                for j in range(2):
                    load(Unit(b + 10 + j), 256, wv[l][:, :, 256 * j:256 * j + 256])
                with sp.Fori(0, 2) as i:
                    for j in range(3):
                        load(Unit(b + 12 + j, i, 3), 256, wv[l][:, :, bass.ds(D_POOL + 256 * j + 768 * i, 256)])
                b += U_WIN
                for j in range(U_WOUT):
                    if j == RING:
                        sp.wait_ge(sem("tail_stored"), 64 * (l + 1))
                        for t in range(ST):
                            if t >= 3:
                                sp.wait_ge(sem(f"state_out{t % 3}"), 16 * (4 * l + t // 3))
                            sp.dma_start(h0[t % 3][:, :, :],
                                         state_ssm[l].rearrange("b h p n -> (h p) b n")[P * t:P * t + P])\
                                .then_inc(sem(f"state_in{t % 3}"), 16)
                    load(Unit(b + j), D, ov[l][:, 2 * j:2 * j + 2, :])
                b += U_WOUT
                if l == 0:
                    with sp.Fori(0, 3) as i:
                        for j in range(6):
                            load(Unit(b + j, i, 6), 256,
                                 (gv, uv)[j % 2][:, :, bass.ds(768 * i + 256 * (j // 2), 256)])
                    for j in range(18, U_GU):
                        load(Unit(b + j), 256, (gv, uv)[j % 2][:, :, 256 * (j // 2):256 * (j // 2) + 256])
                    b += U_GU
                    with sp.Fori(0, 3) as i:
                        for j in range(3):
                            load(Unit(b + j, i, 3), D, dv[:, bass.ds(2 * j + 6 * i, 2), :])
                    for j in range(9, U_DN):
                        load(Unit(b + j), D, dv[:, 2 * j:2 * j + 2, :])

            def expert(j, u, e):
                kind, c, h = EXPERT[j]
                f0, w = FCH[c]
                if isinstance(e, int):
                    e = slice(e, e + 1)
                else:
                    e = bass.ds(e, 1)
                if kind == "d":
                    src = (edv[e, :, f0 // P:f0 // P + 4, 512 * h:512 * h + 512] if h < 2 else
                           edv[e, :, f0 // P:f0 // P + 2, :])
                    load(u, 512 if h < 2 else D, src.rearrange("e p k c -> p (e k) c"))
                else:
                    v = egv if kind == "g" else euv
                    src = v[e, :, 4 * h:4 * h + 4, f0:f0 + w] if h < 2 else v[e, :, :, f0:f0 + w]
                    load(u, w, src.rearrange("e p k c -> p (e k) c"))

            with sp.Fori(0, NE) as e:
                for j in range(U_EXP):
                    expert(j, Unit(U_MOE + j, e, U_EXP), e)
            for j in range(AHEAD):
                expert(j, Unit(U_MOE + NE * U_EXP + j), 0)
            sp.wait_ge(sem("count_ready"), 1)
            over = sp.value_load(cnti[0:1, 0:1], min_val=0, max_val=T)
            with sp.If(over > P):
                for r in range(2):
                    b = U_MOE + NE * U_EXP * (1 + r)
                    with sp.Fori(0, NE - 1) as e:
                        for j in range(AHEAD, U_EXP + AHEAD):
                            expert(j % U_EXP, Unit(b + j, e, U_EXP), e + j // U_EXP)
                    for j in range(AHEAD, U_EXP + AHEAD):
                        expert(j % U_EXP, Unit(b + (NE - 1) * U_EXP + j), (NE - 1 + j // U_EXP) % NE)
            for a in range(3):
                sp.wait_ge(sem("out_ready"), a + 1)
                if a < 2:
                    sp.dma_start(y_prompt[0, P * a:P * a + P, :], acc[:, a, :]).then_inc(sem("y_stored"), 16)
                else:
                    sp.dma_start(y_sample.rearrange("b t d -> (b t) d"), acc[0:NS, 2, :])\
                      .then_inc(sem("y_stored"), 16)
            sp.wait_ge(sem("y_stored"), 48)

        def tile_out(l, n):
            return TILE_BANKS + 2 * U_WIN * l + n

        @block.gpsimd
        def _(pool):
            ev = Order(pool, sem("pool_did"))
            mem = Count(sem("padded"))
            tails = Count(sem("tails_packed"))
            decm = Count(sem("decay_masked"))
            alm = Count(sem("calone_ready"))
            sqm = Count(sem("sq_summed"))
            wxz = Count(sem("wx_padded"))
            blkm = Count(sem("bblk_ready"))
            for l in range(DEPTH):
                if l:
                    pool.wait_ge(sem("mix_ready"), 5 * l)
                else:
                    for t in (calone[:, :], cumT[:, :], cumTh[:, :].bitcast(F32), cumTl[:, :].bitcast(F32)):
                        ev.did(nc.gpsimd.memset(t, 0.0))
                    ev.did(nc.gpsimd.memset(zer[:, :].bitcast(F32), 0.0), mem)
                pool.dma_start(histc[:, :], state_conv[l].rearrange("b k c -> (b k) c")).then_inc(sem("hist_in"), 16)
                pool.dma_start(histp[:, :], state_pool[l].rearrange("b k c -> (b k) c")).then_inc(sem("hist_in"), 16)
                if l:
                    pool.wait_ge(sem("plo_done"), N_GRP)
                    pool.dma_start(plw[:, :, :], pool_w[l].rearrange("g c d -> c g d")).then_inc(sem("plw_in"), 16)
                else:
                    pool.wait_ge(sem("params_ready"), 1)
                if l:
                    pool.wait_ge(sem("x_ready"), 16 + KD)
                ev.did(nc.gpsimd.memset(xpad[:, :, 0:HIST], 0.0), mem)
                ev.did(nc.gpsimd.memset(upad[:, :, 0:PB], 0.0), mem)
                pool.wait_ge(sem("tile_out"), tile_out(l, XT))
                ev.did(nc.gpsimd.tensor_copy(
                    ctail[:, :, 0:HIST], xpad[:, :, SEQ:SEQ + HIST]), tails)
                for b in range(NB):
                    o = CS0 + CSEG * b + DL
                    ev.did(nc.gpsimd.tensor_copy(ctail[:, :, HIST * (b + 1):HIST * (b + 2)],
                                                 xpad[:, :, o:o + HIST]), tails)
                pool.wait_ge(used, L_BASE[l] + U_WIN + RING)
                pool.wait_ge(sem("tile_out"), tile_out(l, XT + N_GRP))
                ev.did(nc.gpsimd.tensor_copy(utail[:, :, 0:PB], upad[:, :, SEQ:SEQ + PB]), tails)
                for b in range(NB):
                    o = PS0 + PSEG * b + DL
                    ev.did(nc.gpsimd.tensor_copy(utail[:, :, PB * (b + 1):PB * (b + 2)],
                                                 upad[:, :, o:o + PB]), tails)
                pool.wait_ge(sem("tail_out"), 7 * (l + 1))
                pool.dma_start(conv_p[l, 0], tailc[0:HIST, :]).then_inc(sem("tail_stored"), 16)
                pool.dma_start(conv_s[l].rearrange("b k c -> (b k) c"), tailc[HIST:HIST * (NB + 1), :])\
                    .then_inc(sem("tail_stored"), 16)
                pool.dma_start(pool_p[l, 0], tailp_p[:, :]).then_inc(sem("tail_stored"), 16)
                pool.dma_start(pool_s[l].rearrange("b k c -> (b k) c"), tailp_s[:, :]).then_inc(sem("tail_stored"), 16)
                pool.wait_ge(sem("tail_stored"), 64 * (l + 1))
                for b in range(3):
                    n = P if b < 2 else NS
                    q = 3 * l + b
                    pool.wait_ge(sem("cb_ready"), q + 1)
                    for g in range(N_GRP):
                        k = 4 * q + g
                        if b == 2 and g == 2:
                            pool.wait_ge(sem("state_mm"), 8 * (l + 1))
                            for r in (NS, 2 * NS):
                                ev.did(nc.gpsimd.memset(wx[r:2 * r, :], 0.0), wxz)
                        pool.wait_ge(sem("decay_exp"), k + 1)
                        ev.did(nc.gpsimd.tensor_tensor(
                            dec[g % 2][0:n, :, 0:n], dec[g % 2][0:n, :, 0:n],
                            cbT[0:n, g:g + 1, 0:n].to_broadcast([n, HG, n]), ALU.mult), decm)
                def blocked(g):
                    if g:
                        pool.wait_ge(sem("update_mm"), ST * l + GT * g)
                    else:
                        pool.wait_ge(sem("ydiag_mm"), 12 * (l + 1))
                        ev.did(nc.gpsimd.memset(bblk[:, :, :], 0.0))
                        ev.sync()
                    ev.did(nc.gpsimd.tensor_tensor(
                        bblk[0:NS, :, :], btok[0:NS, g:g + 1, :].to_broadcast([NS, NB, P]),
                        cst[0:NS, C_BM:C_BM + NB].unsqueeze(2).to_broadcast([NS, NB, P]), ALU.mult), blkm)

                def alone(g):
                    if g:
                        pool.wait_ge(sem("yoff_mm"), ST * l + GT * g)
                    elif l:
                        pool.wait_ge(sem("yoff_mm"), ST * l)
                    ev.did(nc.gpsimd.tensor_copy(calone[:, :].rearrange("p (b x) -> p b x", b=NB)[:, :, 0:DL],
                                                 by_sample(xact[:, ST + N_GRP + g, SEQ:T])), alm)

                def summed(g):
                    pool.wait_ge(sem("sq_done"), 5 * l + g + 1)
                    for t in (1, 2):
                        if t == 2:
                            ev.sync()
                        ev.did(nc.gpsimd.tensor_tensor(sq[:, GT * g, 0:SEQ], sq[:, GT * g, 0:SEQ],
                                                       sq[:, GT * g + t, 0:SEQ], ALU.add), sqm if t == 2 else None)

                for g in range(N_GRP):
                    blocked(g)
                    alone(g)
                    if g:
                        summed(g - 1)
                    else:
                        pool.wait_ge(sem("hout_ready"), 3 * (l + 1))
                        pool.dma_start(ssm_p[l, 0].rearrange("h p n -> (h p) n").rearrange("(t q) n -> q t n", q=P),
                                       hout[:, :, :]).then_inc(sem("hout_stored"), 16)
                summed(N_GRP - 1)
                for j in range(3):
                    pool.wait_ge(sem(f"state_out{j}"), 16 * (ST // 3) * (l + 1))
                pool.wait_ge(sem("hout_stored"), 16 * (l + 1))
            pool.wait_ge(sem("x_ready"), 32)
            pool.dma_start(gbc[:, :], ln2_g[1:2, :].to_broadcast([P, D])).then_inc(sem("ln_bc"), 16)
            pool.dma_start(bbc[:, :], ln2_b[1:2, :].to_broadcast([P, D])).then_inc(sem("ln_bc"), 16)

        @block.scalar
        def _(act):
            A = nc.scalar
            ev = Order(act, sem("act_did"))
            C = {}

            def did(ins, name=None):
                if name is None:
                    return ev.did(ins)
                if name not in C:
                    C[name] = Count(sem(name))
                return ev.did(ins, C[name])

            A.sem_inc(sem("tile_out"), TILE_BANKS)
            C["tile_out"] = Count(sem("tile_out"))
            C["tile_out"].n = TILE_BANKS

            act.wait_ge(sem("x_loaded"), 48)
            did(A.copy(selc[:, :], cst[:, C_ID:C_ID + NH]))
            for k in range(KD):
                act.wait_ge(sem("xt_turned"), k + 1)
                did(A.copy(xT[:, k, :], bank[k][:, 0:T]))
                did(A.copy(xh[:, k, :], bank[k][:, 0:T]), "x_done")
            for j in range(AHEAD):
                split_hi(act, Unit(j))
            act.wait_ge(sem("in_loaded"), 16 * NL)
            for l in range(DEPTH):
                act.wait_ge(sem("par_turned"), l + 1)
                did(A.copy(par_a[l][:, :], bank[6 + l][:, 0:R_A]))
                did(A.copy(par_b[l][:, :], bank[6 + l][:, R_A:R_A + R_B]), "params_done")
                for h in range(2):
                    w = slice(HD * h, HD * h + HD)
                    did(A.copy(dsk[l][w, :], dskb[l][w, h:NH:2]))
            did(A.activation(expA[:, :], alog[0][:, :], ACT.Exp), "params_ready")

            for l in range(DEPTH):
                b = L_BASE[l]
                act.wait_ge(sem("padded"), 1 + 2 * (l + 1))
                act.wait_ge(sem("hist_turned"), 2 * l + 1)
                did(A.copy(xpad[:, :, CS0:CS0 + NB * CSEG].rearrange("p c (b k) -> p c b k", k=CSEG)[:, :, :, 0:HIST],
                           bank[6][:, 0:XT * NB * HIST].rearrange("p (c b k) -> p c b k", b=NB, k=HIST)), "hist_done")
                act.wait_ge(sem("hist_turned"), 2 * l + 2)
                did(A.copy(upad[:, :, PS0:PS0 + NB * PSEG].rearrange("p g (b k) -> p g b k", k=PSEG)[:, :, :, 0:PB],
                           bank[7][:, 0:N_GRP * NB * PB].rearrange("p (g b k) -> p g b k", b=NB, k=PB)), "hist_done")

                def conv_in(u, j, c):
                    act.wait_ge(used, u.multiplied)
                    for h in range(2):
                        o = bank[2 * j + h]
                        cc = bass.ds(c + h, 1)
                        did(A.copy(xpad[:, cc, HIST:HIST + SEQ], o[:, 0:SEQ]))
                        did(A.copy(xpad[:, cc, CS0:CS0 + NB * CSEG].rearrange(
                            "p a (b k) -> p (a b) k", k=CSEG)[:, :, HIST:CSEG], by_sample(o[:, SEQ:T])))
                        ev.sync()
                        did(A.activation(conv[:, cc, 0:COUT], xpad[:, cc, 0:COUT], ACT.Identity,
                                         scale=par_a[l][:, bass.ds(c + h + R_CW, 1)],
                                         bias=par_a[l][:, bass.ds(c + h + R_CB, 1)]), "tile_out")

                with act.Fori(0, 3) as i:
                    with C["tile_out"].loop(i, 6, 3), ev.own.loop(i, 12, 3):
                        for j in range(3):
                            split_hi(act, Unit(b + j + AHEAD, i, 3))
                            conv_in(Unit(b + j, i, 3), j, 6 * i + 2 * j)
                split_hi(act, Unit(b + 9 + AHEAD))
                conv_in(Unit(b + 9), 0, 18)
                for j in range(2):
                    split_hi(act, Unit(b + 10 + j + AHEAD))
                    act.wait_ge(used, Unit(b + 10 + j).multiplied)
                    for h in range(2):
                        o = bank[2 * j + 2 + h]
                        g = 2 * j + h
                        did(A.copy(upad[:, g, PB:PB + SEQ], o[:, 0:SEQ]))
                        did(A.copy(upad[:, g, PS0:PS0 + NB * PSEG].rearrange("p (b k) -> p b k", k=PSEG)[:, :, PB:],
                                   by_sample(o[:, SEQ:T])), "tile_out")

                def packed(c):
                    act.wait_ge(sem("conv_done"), XT * l + c + 1)
                    did(A.activation(xact[:, c, 0:SEQ], conv[:, c, 0:SEQ], ACT.Silu))
                    did(A.activation(by_sample(xact[:, c, SEQ:T]), csamples(conv[:, c, CS0:CS0 + NB * CSEG]),
                                     ACT.Silu), "xact_done")

                def pooled(g):
                    act.wait_ge(sem("pool_mm"), N_GRP * l + g + 1)
                    did(A.activation(plo[:, g, :], bank[6 + g % 2][:, 0:T], ACT.Copy,
                                     scale=par_a[l][:, R_PS + g:R_PS + g + 1]), "plo_done")

                act.wait_ge(sem("tails_packed"), 18 * l + 9)
                for j in range(6):
                    split_hi(act, Unit(b + 12 + j + AHEAD))
                    if j == 0:
                        act.wait_ge(sem("dt_a"), l + 1)
                        did(A.activation(dts["e"][:, :, :], dts["a"][:, :, :], ACT.Exp, scale=-1.0), "dt_e")
                        if l:
                            did(A.activation(expA[:, :], alog[l][:, :], ACT.Exp), "dt_e")
                    for c in range(4 * j, min(4 * j + 4, XT)):
                        packed(c)
                    act.wait_ge(used, Unit(b + 12 + j).multiplied)
                    for h in range(2):
                        did(A.activation(zs[:, 2 * j + h, :], bank[2 * (j % 3) + h][:, 0:T], ACT.Silu), "tile_out")
                    if j == 2:
                        act.wait_ge(sem("cum_mm"), l + 1)
                        did(A.copy(cumT[0:NH, :], bank[6][0:NH, 0:T]))
                        did(A.copy(cumTh[0:NH, :], bank[6][0:NH, 0:T]), "cumh")
                    if j >= 4:
                        pooled(2 * (j - 4))
                        pooled(2 * (j - 4) + 1)
                for c in range(5):
                    act.wait_ge(sem("tail_turned"), 7 * l + c + 1)
                    did(A.copy(tailc[:, 512 * c:512 * c + 512], bank[c][0:HIST * (NB + 1), :]), "tail_out")
                act.wait_ge(sem("tail_turned"), 7 * l + 7)
                did(A.copy(tailp_s[:, :], bank[5][0:NB * PB, :]), "tail_out")
                did(A.copy(tailp_p[:, :], bank[6][0:PB, :]), "tail_out")
                act.wait_ge(sem("ew_arg"), l + 1)
                did(A.activation(dts["ew"][:, :, :], dts["ew"][:, :, :], ACT.Exp))
                did(A.activation(dts["etot"][:, :, :], dts["tot"][:, :, :], ACT.Exp), "ew_ready")
                for bl in range(3):
                    n = P if bl < 2 else NS
                    q = 3 * l + bl
                    act.wait_ge(sem("b_turned"), q + 1)
                    if bl:
                        act.wait_ge(sem("state_mm"), 8 * l + 4 * bl)
                    did(A.copy(btok[0:n, :, :], bank[7][0:n, :].rearrange("p (g c) -> p g c", g=N_GRP)), "btok_ready")
                    for g in range(N_GRP + 1):
                        if g < N_GRP:
                            act.wait_ge(sem("seg_ready"), 4 * q + g + 1)
                            did(A.activation(dec[g % 2][0:n, :, 0:n], dec[g % 2][0:n, :, 0:n], ACT.Exp), "decay_exp")
                        if g:
                            act.wait_ge(sem("ydiag_mm"), 4 * q + g)
                            did(A.copy(y[:, GT * (g - 1):GT * g, P * bl:P * bl + n],
                                       bank[5][:, 0:GT * n].rearrange("p (t c) -> p t c", t=GT)), "y_diag")
                            if bl == 0:
                                act.wait_ge(sem("ecp_mm"), 4 * l + g)
                                did(A.activation(ecp[:, GT * (g - 1):GT * g, :],
                                                 bank[7][:, 0:GT * (P + NS)].rearrange("p (t c) -> p t c", t=GT),
                                                 ACT.Exp), "ecp_done")
                    if bl == 0:
                        act.wait_ge(sem("tail_stored"), 64 * (l + 1))
                        for g in range(N_GRP):
                            act.wait_ge(sem("state_mm"), 8 * l + g + 1)
                            did(A.copy(hT[:, 384 * g:384 * g + 384], bank[g][:, 0:384]), "h1_done")
                for j in range(3):
                    act.wait_ge(sem("h_turned"), 3 * l + j + 1)
                    did(A.copy(hout[:, 4 * j:4 * j + 4, :], bank[4 + j][:, :].rearrange("p (t c) -> p t c", t=4)),
                        "hout_ready")

                def by_token(g):
                    act.wait_ge(sem("yoff_mm"), ST * l + GT * g + GT)
                    if g >= 2:
                        act.wait_ge(sem("yst_turned"), N_GRP * l + g - 1)
                    did(A.copy(yst[g % 2][:, :], bank[6][0:NS, 0:GT * P]), "yst_ready")

                def store(t):
                    act.wait_ge(sem("state_new"), ST * l + t + 1)
                    act.dma_start(ssm_s[l].rearrange("b h p n -> (h p) b n")[P * t:P * t + P], h0[t % 3][:, :, :])\
                        .then_inc(sem(f"state_out{t % 3}"), 16)

                def squares(g):
                    act.wait_ge(sem("gated"), 5 * l + g + 1)
                    did(A.activation(sq[:, GT * g:GT * g + GT, 0:SEQ], y[:, GT * g:GT * g + GT, 0:SEQ], ACT.Square),
                        "sq_done")

                for t in range(ST):
                    act.wait_ge(sem("h0_turned"), ST * l + t + 1)
                    if t >= 2:
                        act.wait_ge(sem("yoff_mm"), ST * l + t - 1)
                    for h in range(2):
                        did(A.copy(h0T[t % 2][:, 4 * h:4 * h + 4, :],
                                   bank[2 * (t % 2) + h][:, :].rearrange("p (b c) -> p b c", b=4)),
                            "h0T_ready" if h else None)
                    if t:
                        store(t - 1)
                    if t % GT == 0 and t:
                        by_token(t // GT - 1)
                        squares(t // GT - 1)
                by_token(N_GRP - 1)
                squares(N_GRP - 1)
                store(ST - 1)
                act.wait_ge(sem("gated"), 5 * l + 5)
                did(A.activation(sq[:, :, SEQ:T], y[:, :, SEQ:T], ACT.Square), "sq_done")
                split_hi(act, Unit(b + U_WIN + AHEAD))
                act.wait_ge(sem("rms_mm"), N_GRP * (l + 1))
                did(A.copy(mixh[:, 0:N_GRP, :], plo[:, :, :]), "mixh_done")
                for g in range(N_GRP):
                    act.wait_ge(sem("rms_in"), N_GRP * l + g + 1)
                    did(A.activation(rms[:, g, :], rms[:, g, :], ACT.Sqrt), "rms_sqrt")
                for g in range(N_GRP):
                    act.wait_ge(sem("normed"), N_GRP * l + g + 1)
                    did(A.copy(mixh[:, N_GRP + GT * g:N_GRP + GT * g + GT, :], y[:, GT * g:GT * g + GT, :]),
                        "mixh_done")
                b += U_WIN
                for j in range(1, U_WOUT):
                    split_hi(act, Unit(b + j + AHEAD))

                def norm(v):
                    for h in range(2):
                        act.wait_ge(sem("ln_cent"), 2 * v + h + 1)
                        did(A.activation(lsq[:, 4 * h:4 * h + 4, :], res[:, 4 * h:4 * h + 4, :], ACT.Square), "ln_sq")
                    act.wait_ge(sem("ln_var"), v + 1)
                    did(A.activation(lnt[:, 0, :], lnt[:, 0, :], ACT.Sqrt), "ln_sqrt")
                    off = R_L2B if v % 2 else R_L1B
                    for d in range(KD):
                        act.wait_ge(sem("ln_scaled"), KD * v + d + 1)
                        bias = par_b[l][:, off + d:off + d + 1]
                        did(A.activation(xT[:, d, :], res[:, d, :], ACT.Identity, bias=bias))
                        did(A.activation(xh[:, d, :], res[:, d, :], ACT.Identity, bias=bias), "x_done")

                norm(2 * l)
                b += U_WOUT
                if l == 0:
                    def silus(up, s):
                        act.wait_ge(used, up.n + RING)
                        did(A.activation(sg[s][:, 0, :], bank[4 * s][:, 0:T], ACT.Silu))
                        did(A.activation(sg[s][:, 1, :], bank[4 * s + 1][:, 0:T], ACT.Silu), "silu_done")

                    def upper(s, f, nth):
                        act.wait_ge(sem("hf_done"), nth + 2)
                        did(A.copy(hh[:, f, :], hf[s][:, :, :]), "hh_done")

                    with act.Fori(0, 3) as i:
                        with ev.own.loop(i, 3, 3), C.setdefault("silu_done", Count(sem("silu_done"))).loop(i, 3, 3), \
                                C.setdefault("hh_done", Count(sem("hh_done"))).loop(i, 3, 3):
                            for j in range(3):
                                split_hi(act, Unit(b + 2 * j + AHEAD, i, 6))
                                silus(Unit(b + 2 * j + 1, i, 6), FFN_SET[j])
                                split_hi(act, Unit(b + 2 * j + 1 + AHEAD, i, 6))
                                upper(FFN_SET[j], bass.ds(6 * i + 2 * j, 2), 3 * i + j)
                    for j in range(9, 11):
                        split_hi(act, Unit(b + 2 * j + AHEAD))
                        silus(Unit(b + 2 * j + 1), FFN_SET[j])
                        split_hi(act, Unit(b + 2 * j + 1 + AHEAD))
                        upper(FFN_SET[j], slice(2 * j, 2 * j + 2), j)
                    b += U_GU
                    with act.Fori(0, 3) as i:
                        for j in range(3):
                            split_hi(act, Unit(b + j + AHEAD, i, 3))
                    for j in range(9, U_DN):
                        split_hi(act, Unit(b + j + AHEAD))
                    norm(1)

            for h in range(2):
                for a in range(3):
                    n = P if a < 2 else NS
                    act.wait_ge(sem("tok_turned"), 3 * h + a + 1)
                    o = bank[2 * a + h][0:n, :]
                    did(A.copy(xtokh[0:n, a, 512 * h:512 * h + 512], o), "xtokh_done")
                    did(A.mul(acc[0:n, a, 512 * h:512 * h + 512], o, ALPHA), "acc_begun")
            act.wait_ge(sem("rt_diff"), 1)
            did(A.activation(r3["e"][:, 0:3], r3["d"][:, 0:3], ACT.Exp), "rt_exp")

            def gathered(it):
                for h in range(2):
                    act.wait_ge(sem("xg_mm"), 2 * it + 2)
                    did(A.copy(xgh[:, 4 * h:4 * h + 4, :], bank[XG[h]][:, :].rearrange("p (k s) -> p k s", k=4)),
                        "xgh_done")

            def outputs(last):
                act.wait_ge(used, last)
                for h in range(2):
                    did(A.activation(yh[:, 512 * h:512 * h + 512], bank[5 + h][:, :], ACT.Copy,
                                     scale=gslot[:, 0:1]), "yh_done")

            def item(it, b, e, per):
                def unit(j):
                    return Unit(b + j, e, per)

                def turned(c):
                    n = FCH[c][1] // P
                    act.wait_ge(sem("hT_mm"), 6 * it + c + 1)
                    did(A.copy(hTh[c % 2][:, 0:n, :], bank[4][:, 0:P * n].rearrange("p (f s) -> p f s", s=P)),
                        "hTh_done")

                for j in range(U_EXP):
                    split_hi(act, unit(j + AHEAD))
                    kind, c, h = EXPERT[j]
                    if j == J_OUT:
                        outputs(unit(0).multiplied)
                    if kind == "g" and h:
                        act.wait_ge(used, unit(j).multiplied)
                        w = FCH[c][1]
                        did(A.activation(gsl[c % 2][:, 0:w], bank[c % 2][:, 0:w], ACT.Silu), "gate_done")
                        if c:
                            turned(c - 1)
                    if j == J_BACK:
                        act.wait_ge(sem("back_mm"), it + 1)
                        did(A.copy(back[:, 0:T], bank[7][:, 0:T]), "back_done")
                        did(A.copy(gslot[:, 0:1], bank[7][:, T:T + 1]), "back_done")
                    if j == J_COPY + 1:
                        gathered(it + 1)
                    if (kind, c, h) == ("d", 4, 0):
                        turned(5)

            def items(base):
                names = dict(xgh_done=2, back_done=2, hTh_done=6, gate_done=6, yh_done=2)
                with act.Fori(0, NE) as e:
                    with ExitStack() as loops:
                        for name, per in names.items():
                            loops.enter_context(C.setdefault(name, Count(sem(name))).loop(e, per, NE))
                        item(e + base, U_MOE + base * U_EXP, e, U_EXP)
                outputs(Unit(U_MOE + (base + NE) * U_EXP - 1).multiplied)

            gathered(0)
            items(0)
            act.wait_ge(sem("count_ready"), 1)
            over = act.value_load(cnti[0:1, 0:1], min_val=0, max_val=T)
            with act.If(over > P):
                for r in range(2):
                    items(NE * (r + 1))
            for a in range(3):
                n = P if a < 2 else NS
                act.wait_ge(sem("fin_var"), a + 1)
                did(A.activation(r3["rs"][0:n, a:a + 1], r3["rs"][0:n, a:a + 1], ACT.Sqrt), "fin_sqrt")

        @block.vector
        def _(dve):
            V = nc.vector
            ev = Order(dve, sem("dve_did"))
            C = {}

            def did(ins, name=None):
                if name is None:
                    return ev.did(ins)
                if name not in C:
                    C[name] = Count(sem(name))
                return ev.did(ins, C[name])

            def loop(it, times, **names):
                stack = ExitStack()
                for name, per in names.items():
                    stack.enter_context(C.setdefault(name, Count(sem(name))).loop(it, per, times))
                return stack

            V.sem_inc(split_done, RING)
            for name, n in (("hf_done", 1), ("hl_done", 1), ("acc_added", 1)):
                V.sem_inc(sem(name), n)
                C[name] = Count(sem(name))
                C[name].n = n
            for k in range(KD):
                dve.wait_ge(sem("x_done"), k + 1)
                did(V.tensor_tensor(xl[:, k, :], xT[:, k, :], xh[:, k, :].bitcast(F32), ALU.subtract), "x_ready")
            for j in range(AHEAD):
                split_lo(dve, Unit(j))
            for l in range(DEPTH):
                b = L_BASE[l]
                pa = par_a[l]
                dve.wait_ge(sem("hist_done"), 2 * (l + 1))
                dve.wait_ge(sem("padded"), 1 + 2 * (l + 1))
                dve.wait_ge(sem("params_ready"), 1)

                def conv_tile(c, cc, nth):
                    dve.wait_ge(sem("tile_out"), tile_out(l, nth + 1))
                    for k in range(1, CW):
                        if k > 1:
                            ev.sync()
                        did(V.scalar_tensor_tensor(conv[:, c, 0:COUT], xpad[:, c, k:k + COUT],
                                                   pa[:, cc(R_CW + XT * k)], conv[:, c, 0:COUT], ALU.mult, ALU.add),
                            "conv_done" if k == CW - 1 else None)

                with dve.Fori(0, 3) as i:
                    with loop(i, 3, conv_done=6), ev.own.loop(i, 12, 3):
                        for j in range(3):
                            split_lo(dve, Unit(b + j + AHEAD, i, 3))
                            for h in range(2):
                                c = 6 * i + 2 * j + h
                                conv_tile(bass.ds(c, 1), lambda r, c=c: bass.ds(c + r, 1), c)
                split_lo(dve, Unit(b + 9 + AHEAD))
                for c in range(18, 20):
                    conv_tile(slice(c, c + 1), lambda r, c=c: slice(c + r, c + r + 1), c)
                for j in range(2):
                    split_lo(dve, Unit(b + 10 + j + AHEAD))
                D3 = {k: t[:, :, :] for k, t in dts.items()}
                dve.wait_ge(sem("dt_mm"), l + 1)
                did(V.tensor_tensor(D3["v"], bank[7][:, 0:72].rearrange("p (b h) -> p b h", b=3),
                                    bias_h[l][:, :].unsqueeze(1).to_broadcast([P, 3, NH]), ALU.add))
                ev.sync()
                did(V.tensor_scalar(D3["a"], D3["v"], -1.0, None, ALU.mult))
                ev.sync()
                did(V.tensor_tensor(D3["a"], D3["a"], D3["v"], ALU.max), "dt_a")
                dve.wait_ge(sem("dt_e"), 2 * l + 1)
                did(V.tensor_scalar(D3["s2"], D3["e"], 2.0, None, ALU.add))
                ev.sync()
                did(V.reciprocal(D3["s"], D3["s2"]))
                ev.sync()
                did(V.tensor_tensor(D3["s"], D3["s"], D3["e"], ALU.mult))
                ev.sync()
                did(V.tensor_tensor(D3["s2"], D3["s"], D3["s"], ALU.mult))
                ev.sync()
                did(V.tensor_scalar(D3["p"], D3["s2"], 1.0 / 17, None, ALU.mult))
                for k in (15, 13, 11, 9, 7, 5, 3):
                    ev.sync()
                    did(V.scalar_tensor_tensor(D3["p"], D3["p"], 1.0 / k, D3["s2"], ALU.add, ALU.mult))
                ev.sync()
                did(V.scalar_tensor_tensor(D3["p"], D3["p"], 1.0, D3["s"], ALU.add, ALU.mult))
                did(V.tensor_scalar(D3["a"], D3["v"], 0.0, None, ALU.max))
                ev.sync()
                did(V.scalar_tensor_tensor(D3["dt"], D3["p"], 2.0, D3["a"], ALU.mult, ALU.add))
                ev.sync()
                did(V.scalar_tensor_tensor(D3["dtA"], D3["dt"], -1.0,
                                           expA[:, :].unsqueeze(1).to_broadcast([P, 3, NH]), ALU.mult, ALU.mult),
                    "dtA_ready")


                def pooling(g, w):
                    s_ = (win_a, win_b)[g % 2]
                    did(V.tensor_scalar(pdiff[:, g, 0:SEQ], s_[:, g, PB:PB + SEQ], 1.0 / w, None, ALU.mult))
                    did(V.tensor_scalar(by_sample(pdiff[:, g, SEQ:T]),
                                        s_[:, g, PS0:].rearrange("p (b k) -> p b k", k=PSEG)[:, :, PB:],
                                        1.0 / w, None, ALU.mult))
                    ev.sync()
                    did(V.tensor_tensor(pdiff[:, g, 0:16], s_[:, g, PB:PB + 16],
                                        cst[:, C_INVC + 16 * g:C_INVC + 16 * g + 16], ALU.mult))
                    ev.sync()
                    did(V.tensor_tensor(pdiff[:, g, 0:SEQ], pdiff[:, g, 0:SEQ], upad[:, g, PB:PB + SEQ],
                                        ALU.subtract))
                    did(V.tensor_tensor(by_sample(pdiff[:, g, SEQ:T]), by_sample(pdiff[:, g, SEQ:T]),
                                        upad[:, g, PS0:].rearrange("p (b k) -> p b k", k=PSEG)[:, :, PB:],
                                        ALU.subtract), "pdiff_done")

                for j in range(6):
                    split_lo(dve, Unit(b + 12 + j + AHEAD))
                    if j == 0:
                        dve.wait_ge(sem("tile_out"), tile_out(l, XT + N_GRP))
                        src, L = upad, PLINE
                        for step, w in enumerate(WINDOWS):
                            out = (win_a, win_b)[step % 2]
                            lo_ = w - 1
                            half = w // 2
                            did(V.tensor_tensor(out[:, step:N_GRP, lo_:L], src[:, step:N_GRP, lo_:L],
                                                src[:, step:N_GRP, lo_ - half:L - half], ALU.add))
                            ev.sync()
                            src = out
                    for g in ((0,), (1,), (2, 3), (), (), ())[j]:
                        pooling(g, WINDOWS[g])
                    if j == 3:
                        dve.wait_ge(sem("cum_mm"), l + 1)
                        did(V.tensor_copy(D3["cum"], bank[7][:, 128:200].rearrange("p (b h) -> p b h", b=3)))
                        did(V.tensor_copy(D3["tot"], bank[7][:, 256:328].rearrange("p (b h) -> p b h", b=3)))
                        ev.sync()
                        did(V.tensor_tensor(D3["ew"], D3["tot"], D3["cum"], ALU.subtract), "ew_arg")
                        dve.wait_ge(sem("cumh"), l + 1)
                        did(V.tensor_tensor(cumTl[0:NH, :], cumT[0:NH, :], cumTh[0:NH, :].bitcast(F32), ALU.subtract),
                            "cuml")
                for bl in range(3):
                    n = P if bl < 2 else NS
                    q = 3 * l + bl

                    def exponents(g):
                        k = 4 * q + g
                        dve.wait_ge(sem("bc_mm"), k + 1)
                        if g >= 2 or bl:
                            dve.wait_ge(sem("ydiag_mm"), k - 1)
                        for x in range(HG):
                            h = HG * g + x
                            src = bank[2 * (g % 2) + x // 4][0:n, n * (x % 4):n * (x % 4) + n]
                            did(V.tensor_scalar(dec[g % 2][0:n, x, 0:n], src, dts["cum"][0:n, bl, h:h + 1], 0.0,
                                                ALU.subtract, ALU.min), "seg_ready" if x == HG - 1 else None)
                    for j in range(3):
                        if bl and j == 0:
                            dve.wait_ge(sem("wx_ready"), q)
                            dve.wait_ge(sem("ydiag_mm"), 4 * q)
                        dve.wait_ge(sem("x_turned"), 3 * q + j + 1)
                        did(V.tensor_tensor(xdt[0:n, 512 * j:512 * j + 512].rearrange("p (h d) -> p h d", d=HD),
                                            bank[4 + j][0:n, :].rearrange("p (h d) -> p h d", d=HD),
                                            dts["dt"][0:n, bl, 8 * j:8 * j + 8].unsqueeze(2)
                                            .to_broadcast([n, 8, HD]), ALU.mult), "xdt_ready")
                    exponents(0)
                    dve.wait_ge(sem("cb_mm"), q + 1)
                    if bl:
                        dve.wait_ge(sem("decay_masked"), 4 * q)
                    did(V.tensor_tensor(cbT[0:n, :, 0:n], bank[4][0:n, 0:4 * n].rearrange("p (g c) -> p g c", g=4),
                                        (tri if bl < 2 else tri2)[0:n, 0:n].unsqueeze(1).to_broadcast([n, 4, n]),
                                        ALU.mult), "cb_ready")
                    exponents(1)
                    dve.wait_ge(sem("ew_ready"), l + 1)
                    dve.wait_ge(sem("xdt_ready"), 3 * (q + 1))
                    if bl:
                        dve.wait_ge(sem("state_mm"), 8 * l + 4 * bl)
                    did(V.tensor_tensor(
                        wx[0:n, :].rearrange("p (h d) -> p h d", d=HD),
                        xdt[0:n, :].rearrange("p (h d) -> p h d", d=HD),
                        dts["ew"][0:n, bl, :].unsqueeze(2).to_broadcast([n, NH, HD]), ALU.mult), "wx_ready")
                    for g in range(2, N_GRP):
                        exponents(g)
                    if bl == 1:
                        for g in range(N_GRP):
                            dve.wait_ge(sem("yoff1_mm"), N_GRP * l + g + 1)
                            dve.wait_ge(sem("y_diag"), 4 * q + g + 1)
                            yy = y[:, GT * g:GT * g + GT, P:2 * P]
                            yt = ytmp[:, :].rearrange("p (t c) -> p t c", t=GT)
                            did(V.tensor_tensor(yt,
                                                bank[(6, 4)[g % 2]][:, 0:GT * P].rearrange("p (t c) -> p t c", t=GT),
                                                ecp[:, GT * g:GT * g + GT, 0:P], ALU.mult), "yoff1_done")
                            ev.sync()
                            did(V.tensor_tensor(yy, yy, yt, ALU.add))
                            ev.sync()
                        hv = hT[:, :].rearrange("p (h d) -> p h d", d=HD)
                        did(V.tensor_tensor(hv, hv, dts["etot"][:, 1, :].unsqueeze(2).to_broadcast([P, NH, HD]),
                                            ALU.mult))
                        ev.sync()
                        for g in range(N_GRP):
                            dve.wait_ge(sem("state_mm"), 8 * l + 4 + g + 1)
                            hg = hT[:, 384 * g:384 * g + 384]
                            did(V.tensor_tensor(hg, hg, bank[g][:, 0:384], ALU.add), "h2_done")
                dve.wait_ge(sem("y_diag"), 12 * (l + 1))
                for t in range(ST):
                    dve.wait_ge(sem("h0_turned"), ST * l + t + 1)
                    dve.wait_ge(sem("update_mm"), ST * l + t + 1)
                    for i in range(NB):
                        hv = h0[t % 3][:, i, :]
                        last_token = P + DL * i + DL - 1
                        did(V.scalar_tensor_tensor(hv, hv, ecp[:, t, last_token:last_token + 1],
                                                   bank[4 + i // 4][:, P * (i % 4):P * (i % 4) + P],
                                                   ALU.mult, ALU.add), "state_new" if i == NB - 1 else None)
                    did(V.scalar_tensor_tensor(y[:, t, 0:SEQ], xact[:, t, 0:SEQ], dsk[l][:, t:t + 1], y[:, t, 0:SEQ],
                                               ALU.mult, ALU.add))
                    ev.sync()
                    did(V.tensor_tensor(y[:, t, 0:SEQ], y[:, t, 0:SEQ], zs[:, t, 0:SEQ], ALU.mult),
                        "gated" if t % GT == GT - 1 else None)
                yt = ytmp[:, :].rearrange("p (t c) -> p t c", t=ST)
                ys = y[:, :, SEQ:T]
                did(V.tensor_tensor(yt, xact[:, 0:ST, SEQ:T], dsk[l][:, :].unsqueeze(2).to_broadcast([P, ST, NS]),
                                    ALU.mult))
                ev.sync()
                did(V.tensor_tensor(ys, ys, yt, ALU.add))
                dve.wait_ge(sem("yst_turned"), N_GRP * (l + 1))
                ev.sync()
                did(V.tensor_tensor(yt, bank[7][:, 0:ST * NS].rearrange("p (t c) -> p t c", t=ST),
                                    ecp[:, :, P:P + NS], ALU.mult))
                ev.sync()
                did(V.tensor_tensor(ys, ys, yt, ALU.add))
                ev.sync()
                did(V.tensor_tensor(ys, ys, zs[:, :, SEQ:T], ALU.mult), "gated")
                dve.wait_ge(sem("sq_done"), 5 * (l + 1))
                sg3 = sq[:, :, SEQ:T].rearrange("p (g t) c -> p g t c", t=GT)
                for t in (1, 2):
                    did(V.tensor_tensor(sg3[:, :, 0, :], sg3[:, :, 0, :], sg3[:, :, t, :], ALU.add),
                        "sq_summed_s" if t == 2 else None)
                    ev.sync()
                split_lo(dve, Unit(b + U_WIN + AHEAD))
                for g in range(N_GRP):
                    dve.wait_ge(sem("rms_mm"), N_GRP * l + g + 1)
                    did(V.tensor_scalar(rms[:, g, :], bank[g][:, 0:T], 1.0 / (GT * P), RMS_EPS, ALU.mult, ALU.add),
                        "rms_in")

                def lower(g):
                    dve.wait_ge(sem("mixh_done"), 5 * l + g + 1)
                    if g == 0:
                        did(V.tensor_tensor(mixl[:, 0:N_GRP, :], plo[:, :, :], mixh[:, 0:N_GRP, :].bitcast(F32),
                                            ALU.subtract), "mix_ready")
                    else:
                        a0 = N_GRP + GT * (g - 1)
                        did(V.tensor_tensor(mixl[:, a0:a0 + GT, :], y[:, GT * (g - 1):GT * g, :],
                                            mixh[:, a0:a0 + GT, :].bitcast(F32), ALU.subtract), "mix_ready")

                lower(0)
                for g in range(N_GRP):
                    dve.wait_ge(sem("rms_sqrt"), N_GRP * l + g + 1)
                    did(V.reciprocal(rms[:, g, :], rms[:, g, :]))
                    ev.sync()
                    for t in range(GT * g, GT * g + GT):
                        did(V.scalar_tensor_tensor(y[:, t, :], y[:, t, :], pa[:, R_NW + t:R_NW + t + 1],
                                                   rms[:, g, :], ALU.mult, ALU.mult),
                            "normed" if t == GT * g + GT - 1 else None)
                    if g:
                        lower(g)
                lower(N_GRP)
                b += U_WIN
                for j in range(1, U_WOUT):
                    split_lo(dve, Unit(b + j + AHEAD))
                b += U_WOUT

                def norm(v, end_unit):
                    for d in range(KD):
                        if d < KD - 1:
                            dve.wait_ge(sem("row_done"), (KD - 1) * v + d + 1)
                        else:
                            dve.wait_ge(used, end_unit.multiplied)
                        did(V.scalar_tensor_tensor(res[:, d, :], xT[:, d, :], ALPHA, bank[d][:, 0:T], ALU.mult,
                                                   ALU.add), "ln_res")
                    ev.sync()
                    dve.wait_ge(sem("ln_mean"), v + 1)
                    for h in range(2):
                        half = res[:, 4 * h:4 * h + 4, :]
                        did(V.scalar_tensor_tensor(half, bank[0][:, 0:T].unsqueeze(1).to_broadcast([P, 4, T]),
                                                   -1.0 / D, half, ALU.mult, ALU.add), "ln_cent")
                    dve.wait_ge(sem("ln_varmm"), v + 1)
                    did(V.tensor_scalar(lnt[:, 0, :], bank[1][:, 0:T], 1.0 / D, LN_EPS, ALU.mult, ALU.add), "ln_var")
                    dve.wait_ge(sem("ln_sqrt"), v + 1)
                    did(V.reciprocal(lnt[:, 1, :], lnt[:, 0, :]))
                    ev.sync()
                    off = R_L2G if v % 2 else R_L1G

                    def low(d):
                        dve.wait_ge(sem("x_done"), KD * (v + 1) + d + 1)
                        did(V.tensor_tensor(xl[:, d, :], xT[:, d, :], xh[:, d, :].bitcast(F32), ALU.subtract),
                            "x_ready")

                    for d in range(KD):
                        did(V.scalar_tensor_tensor(res[:, d, :], res[:, d, :], par_b[l][:, off + d:off + d + 1],
                                                   lnt[:, 1, :], ALU.mult, ALU.mult), "ln_scaled")
                        if d:
                            low(d - 1)
                    low(KD - 1)

                dve.wait_ge(sem("hout_stored"), 16 * (l + 1))
                for j in range(3):
                    dve.wait_ge(sem(f"state_out{j}"), 16 * (ST // 3) * (l + 1))
                norm(2 * l, Unit(b - 1))
                if l == 0:
                    def product(up, s, nth):
                        dve.wait_ge(used, up.multiplied)
                        dve.wait_ge(sem("hl_done"), nth + 1)
                        for h in range(2):
                            did(V.tensor_tensor(hf[s][:, h, :], sg[s][:, h, :], bank[4 * s + 2 + h][:, 0:T],
                                                ALU.mult), "hf_done" if h else None)

                    def lower(s, f, nth):
                        dve.wait_ge(sem("hh_done"), nth + 1)
                        did(V.tensor_tensor(hl[:, f, :], hf[s][:, :, :], hh[:, f, :].bitcast(F32), ALU.subtract),
                            "hl_done")

                    with dve.Fori(0, 3) as i:
                        with loop(i, 3, hf_done=3, hl_done=3), ev.own.loop(i, 3, 3):
                            for j in range(3):
                                split_lo(dve, Unit(b + 2 * j + AHEAD, i, 6))
                                dve.wait_ge(sem("silu_done"), 3 * i + j + 1)
                                product(Unit(b + 2 * j + 1, i, 6), FFN_SET[j], 3 * i + j)
                                split_lo(dve, Unit(b + 2 * j + 1 + AHEAD, i, 6))
                                lower(FFN_SET[j], bass.ds(6 * i + 2 * j, 2), 3 * i + j)
                    for j in range(9, 11):
                        split_lo(dve, Unit(b + 2 * j + AHEAD))
                        dve.wait_ge(sem("silu_done"), j + 1)
                        product(Unit(b + 2 * j + 1), FFN_SET[j], j)
                        split_lo(dve, Unit(b + 2 * j + 1 + AHEAD))
                        lower(FFN_SET[j], slice(2 * j, 2 * j + 2), j)
                    b += U_GU
                    with dve.Fori(0, 3) as i:
                        for j in range(3):
                            split_lo(dve, Unit(b + j + AHEAD, i, 3))
                    for j in range(9, U_DN):
                        split_lo(dve, Unit(b + j + AHEAD))
                    norm(1, Unit(b + U_DN - 1))

            R = {k: t[:, :, :] for k, t in rt.items()}

            def col(name):
                return r3[name][:, 0:3]

            def wide(name):
                return r3[name][:, 0:3].unsqueeze(2).to_broadcast([P, 3, NE])

            for j in range(3):
                dve.wait_ge(sem(f"state_out{j}"), 16 * (ST // 3) * DEPTH)
            for h in range(2):
                for a in range(3):
                    n = P if a < 2 else NS
                    dve.wait_ge(sem("acc_begun"), 3 * h + a + 1)
                    w = slice(512 * h, 512 * h + 512)
                    did(V.tensor_tensor(xtokl[0:n, a, w], bank[2 * a + h][0:n, :], xtokh[0:n, a, w].bitcast(F32),
                                        ALU.subtract), "xtokl_done")
            did(V.memset(gslot[:, :], 0.0))
            did(V.memset(back[:, :].bitcast(F32), 0.0), "xtokl_done")
            dve.wait_ge(sem("logit_mm"), 1)
            did(V.tensor_tensor(R["lg"], bank[6][:, 0:3 * NE].rearrange("p (a e) -> p a e", a=3),
                                rb[:, :].unsqueeze(1).to_broadcast([P, 3, NE]), ALU.add))
            rev = cst[:, C_REV:C_REV + NE].unsqueeze(1).to_broadcast([P, 3, NE])
            for logits, v, c, r, oh in (("lg", "v1", "c1", "r1", "oh1"), ("lg2", "v2", "c2", "r2", "oh2")):
                ev.sync()
                did(V.tensor_reduce(col(v), R[logits], AX.X, ALU.max))
                ev.sync()
                did(V.tensor_tensor(R[c], R[logits], wide(v), ALU.is_equal))
                ev.sync()
                did(V.tensor_tensor(R[c], R[c], rev, ALU.mult))
                ev.sync()
                did(V.tensor_reduce(col(r), R[c], AX.X, ALU.max))
                ev.sync()
                did(V.tensor_tensor(R[oh], R[c], wide(r), ALU.is_equal))
                if oh == "oh1":
                    ev.sync()
                    did(V.scalar_tensor_tensor(R["lg2"], R["oh1"], -3e38, R["lg"], ALU.mult, ALU.add))
            ev.sync()
            did(V.tensor_tensor(col("d"), col("v2"), col("v1"), ALU.subtract), "rt_diff")
            dve.wait_ge(sem("rt_exp"), 1)
            did(V.tensor_scalar(col("g2"), col("e"), 1.0, None, ALU.add))
            ev.sync()
            did(V.reciprocal(col("g1"), col("g2")))
            ev.sync()
            did(V.tensor_tensor(col("g2"), col("e"), col("g1"), ALU.mult))
            did(V.tensor_tensor(R["t"], R["oh1"], wide("g1"), ALU.mult))
            ev.sync()
            did(V.tensor_tensor(R["G"], R["oh2"], wide("g2"), ALU.mult))
            ev.sync()
            did(V.tensor_tensor(R["G"], R["G"], R["t"], ALU.add))
            did(V.tensor_tensor(R["M"], R["oh1"], R["oh2"], ALU.add))
            ev.sync()
            did(V.tensor_tensor(R["M"], R["M"], cst[:, C_VAL:C_VAL + 3].unsqueeze(2).to_broadcast([P, 3, NE]),
                                ALU.mult), "marks_ready")
            dve.wait_ge(sem("pos_mm"), 1)
            did(V.scalar_tensor_tensor(posm[:, :, 0:NE], bank[7][:, 0:3 * NE].rearrange("p (a e) -> p a e", a=3), 1.0,
                                       R["M"], ALU.add, ALU.mult))
            did(V.tensor_reduce(r3["r1"][:, 3:4], bank[7][:, 64:64 + NE], AX.X, ALU.max))
            ev.sync()
            did(V.tensor_scalar(posm[:, :, NE:NE + 1], posm[:, :, 0:1], -1.0 - P, None, ALU.add))
            ev.sync()
            did(V.tensor_scalar(posm[:, :, 0:NE], posm[:, :, 0:NE], -1.0, None, ALU.add))
            did(V.tensor_copy(cnti[:, 0:1], r3["r1"][:, 3:4]), "count_ready")
            ev.sync()

            def choose(e):
                for a in range(3):
                    did(V.tensor_scalar(pick[:, a, :], iota, posm[:, a, e], None, ALU.is_equal), "pick_ready")

            def gathered(it):
                for h in range(2):
                    dve.wait_ge(sem("xgh_done"), 2 * it + h + 1)
                    did(V.tensor_tensor(xgl[:, 4 * h:4 * h + 4, :],
                                        bank[XG[h]][:, :].rearrange("p (k s) -> p k s", k=4),
                                        xgh[:, 4 * h:4 * h + 4, :].bitcast(F32), ALU.subtract), "xgl_done")

            def outputs(s):
                for h in range(2):
                    dve.wait_ge(sem("yh_done"), 2 * s + h + 1)
                    w = slice(512 * h, 512 * h + 512)
                    did(V.scalar_tensor_tensor(yl[:, w], bank[5 + h][:, :], gslot[:, 0:1], yh[:, w].bitcast(F32),
                                               ALU.mult, ALU.subtract), "yl_done")

            def scattered(s, r, o):
                a, h = r // 2, r % 2
                n = P if a < 2 else NS
                w = slice(512 * h, 512 * h + 512)
                dve.wait_ge(sem("scat_mm"), 6 * s + r + 1)
                did(V.tensor_tensor(acc[0:n, a, w], acc[0:n, a, w], o[0:n, :], ALU.add), "acc_added")

            def item(it, s, b, e, per):
                def unit(j):
                    return Unit(b + j, e, per)

                def turned(c):
                    n = FCH[c][1] // P
                    dve.wait_ge(sem("hTh_done"), 6 * it + c + 1)
                    did(V.tensor_tensor(hTl[c % 2][:, 0:n, :], bank[4][:, 0:P * n].rearrange("p (f s) -> p f s", s=P),
                                        hTh[c % 2][:, 0:n, :].bitcast(F32), ALU.subtract), "hTl_done")

                for j in range(U_EXP):
                    split_lo(dve, unit(j + AHEAD))
                    kind, c, h = EXPERT[j]
                    if j == J_OUT:
                        outputs(s)
                    if j == J_PICK:
                        dve.wait_ge(sem("back_mm"), it + 1)
                        choose(bass.ds(e + 1, 1))
                    if j == J_COPY + 1:
                        gathered(it + 1)
                    if kind == "g" and h and c:
                        turned(c - 1)
                    if kind == "u" and h:
                        w = FCH[c][1]
                        dve.wait_ge(used, unit(j).multiplied)
                        dve.wait_ge(sem("gate_done"), 6 * it + c + 1)
                        if c >= 2:
                            dve.wait_ge(sem("hT_mm"), 6 * it + c - 1)
                        did(V.tensor_tensor(hex_[c % 2][:, 0:w], gsl[c % 2][:, 0:w], bank[2 + c % 2][:, 0:w],
                                            ALU.mult), "h_ready")
                    if (kind, c, h) == ("d", 4, 0):
                        turned(5)
                    if j in J_SCATTER:
                        scattered(s, J_SCATTER.index(j), bank[7])

            def items(base, r):
                with dve.Fori(0, NE) as e:
                    with loop(e, NE, pick_ready=3, xgl_done=2, hTl_done=6, h_ready=6, yl_done=2, acc_added=6):
                        item(e + base, e + base + r, U_MOE + base * U_EXP, e, U_EXP)
                s = base + NE + r
                outputs(s)
                for k in range(6):
                    scattered(s, k, bank[TAIL[k]])
                ev.sync()

            choose(slice(0, 1))
            gathered(0)
            dve.wait_ge(sem("acc_begun"), 6)
            items(0, 0)
            over = dve.value_load(cnti[0:1, 0:1], min_val=0, max_val=T)
            with dve.If(over > P):
                for r in range(2):
                    did(V.tensor_scalar(posm[:, :, :], posm[:, :, :], -float(P), None, ALU.add), "posm_next")
                    ev.sync()
                    items(NE * (r + 1), r + 1)

            dve.wait_ge(sem("ln_bc"), 32)
            for a in range(3):
                n = P if a < 2 else NS
                for h in range(2):
                    did(V.bn_stats(r3[f"st{h}"][0:n, 0:6], acc[0:n, a, 512 * h:512 * h + 512]))
                    ev.sync()
                    did(V.tensor_copy(stat[0:n, 6 * h:6 * h + 6], r3[f"st{h}"][0:n, 0:6]))
                ev.sync()
                did(V.bn_aggr(r3["mv"][0:n, 0:2], stat[0:n, :]))
                ev.sync()
                did(V.tensor_scalar(r3["rs"][0:n, a:a + 1], r3["mv"][0:n, 1:2], LN_EPS, None, ALU.add), "fin_var")
                dve.wait_ge(sem("fin_sqrt"), a + 1)
                did(V.reciprocal(r3["rs"][0:n, a:a + 1], r3["rs"][0:n, a:a + 1]))
                ev.sync()
                did(V.scalar_tensor_tensor(acc[0:n, a, :], acc[0:n, a, :], r3["mv"][0:n, 0:1], gbc[0:n, :],
                                           ALU.subtract, ALU.mult))
                ev.sync()
                did(V.scalar_tensor_tensor(acc[0:n, a, :], acc[0:n, a, :], r3["rs"][0:n, a:a + 1], bbc[0:n, :],
                                           ALU.mult, ALU.add), "out_ready")

        @block.tensor
        def _(pe):
            M = nc.tensor

            def mm(out, a, b_, start=True, stop=True):
                return M.matmul(out, a, b_, start=start, stop=stop, skip_group_check=True)

            def turn(out, in_, k=P):
                return M.transpose(out, in_, ident[0:k, 0:k])

            M.sem_inc(used, RING)
            pe.wait_ge(sem("x_loaded"), 48)
            for k in range(KD):
                for a in range(3):
                    n = P if a < 2 else NS
                    last = turn(bank[k][:, P * a:P * a + n], xin[0:n, a, P * k:P * k + P], n)
                last.then_inc(sem("xt_turned"), 1)
            for l in range(DEPTH):
                b = L_BASE[l]
                def columns(u, j, free, x0=KD * 2 * l):
                    pe.wait_ge(split_done, u.n + RING + 1)
                    free()
                    for h in range(2):
                        for k in range(KD):
                            wh = view(hi[u.slot], 256)[:, k, P * h:P * h + P]
                            wl = view(lo[u.slot], 256)[:, k, P * h:P * h + P]
                            if h == 0:
                                pe.wait_ge(sem("x_ready"), x0 + k + 1)
                            last = three(bank[j + h][:, 0:T], wh, wl, xh[:, k, :], xl[:, k, :], k == 0, k == KD - 1)
                    last.then_inc(used, 1)

                for j in range(3):
                    columns(Unit(b + j), 2 * j, lambda: pe.wait_ge(sem("tile_out"), tile_out(l, 2 * j - 4)))
                    if j == 0:
                        if l == 0:
                            pe.wait_ge(sem("in_loaded"), 16 * NL)
                            pe.wait_ge(sem("x_done"), KD)
                            for i in range(DEPTH):
                                turn(bank[6 + i][:, 0:R_A], prow[i][0:R_A, 0, :], R_A)
                                turn(bank[6 + i][:, R_A:R_A + R_B], prow[i][0:R_B, 1, :], R_B)\
                                    .then_inc(sem("par_turned"), 1)
                            pe.wait_ge(sem("params_done"), DEPTH)
                            pe.wait_ge(sem("padded"), 1)
                        pe.wait_ge(sem("hist_in"), 32 * (l + 1))
                        for c in range(XT):
                            last = turn(bank[6][:, 24 * c:24 * c + 24], histc[:, P * c:P * c + P], 24)
                        last.then_inc(sem("hist_turned"), 1)
                        for g in range(N_GRP):
                            last = turn(bank[7][:, 120 * g:120 * g + 120], histp[:, P * g:P * g + P], 120)
                        last.then_inc(sem("hist_turned"), 1)
                with pe.Fori(0, 2) as i:
                    for j in range(3):
                        columns(Unit(b + 3 + j, i, 3), 2 * j,
                                lambda: pe.wait_ge(sem("tile_out"), tile_out(l, 6 * i + 2 * j + 2)))
                pe.wait_ge(sem("hist_done"), 2 * (l + 1))
                zero(bank[7][:, 0:72], 72)
                for a in range(3):
                    n = P if a < 2 else NS
                    for k in range(KD):
                        last = add(bank[7][0:n, NH * a:NH * a + NH], xT[:, k, P * a:P * a + n], wdt[l][:, k, :],
                                   stop=(a == 2 and k == KD - 1))
                last.then_inc(sem("dt_mm"), 1)
                with pe.Fori(0, 2) as i:
                    for j in range(3):
                        columns(Unit(b + 9 + j, i, 3), 2 * j,
                                lambda: pe.wait_ge(sem("tile_out"), tile_out(l, 18 + 6 * i + 2 * j - 4)))
                pe.wait_ge(sem("dtA_ready"), l + 1)
                dA = dts["dtA"]
                for a in range(3):
                    mm(bank[7][:, 128 + NH * a:128 + NH * a + NH], tri if a < 2 else tri2, dA[:, a, :])
                    mm(bank[7][:, 256 + NH * a:256 + NH * a + NH], ones if a < 2 else blk2, dA[:, a, :])
                    n = P if a < 2 else NS
                    last = mm(bank[6][0:NH, P * a:P * a + n], dA[:, a, :], (tri if a < 2 else tri2)[:, 0:n])
                last.then_inc(sem("cum_mm"), 1)
                for j in range(3):
                    columns(Unit(b + 15 + j), 2 * j,
                            lambda: pe.wait_ge(sem("tile_out"), tile_out(l, 30 + 2 * j - 4)))
                    if j:
                        pe.wait_ge(sem("pdiff_done"), N_GRP * (l + 1))
                        pe.wait_ge(sem("cumh"), l + 1)
                        pe.wait_ge(sem("cuml"), l + 1)
                        if l:
                            pe.wait_ge(sem("plw_in"), 16)
                        if j == 2:
                            pe.wait_ge(sem("plo_done"), N_GRP * l + 2)
                        for g in (2 * j - 2, 2 * j - 1):
                            mm(bank[6 + g % 2][:, 0:T], plw[:, g, :], pdiff[:, g, :]).then_inc(sem("pool_mm"), 1)
                pe.wait_ge(sem("tile_out"), tile_out(l, 2 * U_WIN))
                for c in range(XT):
                    last = turn(bank[c // 4][0:27, P * (c % 4):P * (c % 4) + P], ctail[:, c, :])
                    if c % 4 == 3:
                        last.then_inc(sem("tail_turned"), 1)
                pe.wait_ge(sem("tails_packed"), 18 * (l + 1))
                for g in range(N_GRP):
                    last = turn(bank[5][0:NB * PB, P * g:P * g + P], utail[:, g, PB:PB * (NB + 1)])
                last.then_inc(sem("tail_turned"), 1)
                pe.wait_ge(sem("plo_done"), N_GRP * (l + 1))
                for g in range(N_GRP):
                    last = turn(bank[6][0:PB, P * g:P * g + P], utail[:, g, 0:PB])
                last.then_inc(sem("tail_turned"), 1)
                pe.wait_ge(sem("xact_done"), XT * (l + 1))
                pe.wait_ge(sem("cuml"), l + 1)
                pe.wait_ge(sem("tail_out"), 7 * (l + 1))
                for bl in range(3):
                    n = P if bl < 2 else NS
                    q = 3 * l + bl
                    w = slice(P * bl, P * bl + n)
                    if bl:
                        pe.wait_ge(sem("y_diag"), 4 * q)
                        pe.wait_ge(sem("ecp_done"), N_GRP * (l + 1))
                    if bl == 2:
                        pe.wait_ge(sem("yoff1_done"), N_GRP * (l + 1))
                    for t in range(ST):
                        last = turn(bank[4 + t // 4][0:n, P * (t % 4):P * (t % 4) + P], xact[:, t, w])
                        if t % 4 == 3:
                            last.then_inc(sem("x_turned"), 1)
                    for g in range(N_GRP):
                        last = turn(bank[7][0:n, P * g:P * g + P], xact[:, ST + g, w])
                    last.then_inc(sem("b_turned"), 1)
                    if bl == 1:
                        pe.wait_ge(sem("h1_done"), 4 * (l + 1))
                    if bl == 2:
                        pe.wait_ge(sem("h2_done"), 4 * (l + 1))
                    def sums(g):
                        if g >= 2:
                            pe.wait_ge(sem("seg_ready"), 4 * q + g - 1)
                        for x in range(HG):
                            o = bank[2 * (g % 2) + x // 4][:, n * (x % 4):n * (x % 4) + n]
                            s_ = selc[:, HG * g + x:HG * g + x + 1].to_broadcast([P, P])
                            mm(o, s_, cumTh[:, w], True, False)
                            last = mm(o, s_, cumTl[:, w], False, True)
                        last.then_inc(sem("bc_mm"), 1)

                    def inside(g):
                        k = 4 * q + g
                        pe.wait_ge(sem("decay_masked"), k + 1)
                        pe.wait_ge(sem("y_diag"), k)
                        for x in range(HG):
                            h = HG * g + x
                            last = mm(bank[5][HD * (x % 2):HD * (x % 2) + HD, n * (x // 2):n * (x // 2) + n],
                                      xdt[0:n, HD * h:HD * h + HD], dec[g % 2][0:n, x, 0:n])
                        last.then_inc(sem("ydiag_mm"), 1)

                    def decays(g):
                        if g:
                            pe.wait_ge(sem("ecp_done"), N_GRP * l + g)
                        for t in range(GT * g, GT * g + GT):
                            for h in range(2):
                                last = mm(bank[7][HD * h:HD * h + HD, (P + NS) * (t % GT):(P + NS) * (t % GT + 1)],
                                          cst[:, C_ID + 2 * t + h:C_ID + 2 * t + h + 1].to_broadcast([P, HD]),
                                          cumT[:, P:T])
                        last.then_inc(sem("ecp_mm"), 1)

                    sums(0)
                    pe.wait_ge(sem("xdt_ready"), 3 * q + 1)
                    for g in range(N_GRP):
                        last = mm(bank[4][0:n, n * g:n * g + n], xact[:, ST + g, w], xact[:, ST + N_GRP + g, w])
                    last.then_inc(sem("cb_mm"), 1)
                    sums(1)
                    pe.wait_ge(sem("xdt_ready"), 3 * (q + 1))
                    pe.wait_ge(sem("btok_ready"), q + 1)
                    for g in range(N_GRP):
                        if 1 < g + 1 < N_GRP:
                            sums(g + 1)
                        inside(g)
                        if bl == 0:
                            decays(g)
                    if bl == 1:
                        for g in range(N_GRP):
                            if g >= 2:
                                pe.wait_ge(sem("yoff1_done"), N_GRP * l + g - 1)
                            for t in range(GT):
                                last = mm(bank[(6, 4)[g % 2]][:, P * t:P * t + P],
                                          hT[:, P * (GT * g + t):P * (GT * g + t) + P],
                                          xact[:, ST + N_GRP + g, w])
                            last.then_inc(sem("yoff1_mm"), 1)
                    if bl < 2:
                        pe.wait_ge(sem("wx_ready"), q + 1)
                        pe.wait_ge(sem("seg_ready"), 4 * q + 4)
                        for g in range(N_GRP):
                            mm(bank[g][:, 0:384], btok[:, g, :], wx[:, 384 * g:384 * g + 384])\
                                .then_inc(sem("state_mm"), 1)
                pe.wait_ge(sem("y_diag"), 12 * (l + 1))
                for t in range(ST):
                    last = turn(bank[4 + t // 4][:, P * (t % 4):P * (t % 4) + P], hT[:, P * t:P * t + P])
                    if t % 4 == 3:
                        last.then_inc(sem("h_turned"), 1)
                pe.wait_ge(sem("seg_ready"), 12 * (l + 1))
                pe.wait_ge(sem("wx_ready"), 3 * (l + 1))

                def state_turned(t):
                    pe.wait_ge(sem(f"state_in{t % 3}"), 16 * (4 * l + t // 3 + 1))
                    if t >= 2:
                        pe.wait_ge(sem("h0T_ready"), ST * l + t - 1)
                    for i in range(NB):
                        last = turn(bank[2 * (t % 2) + i // 4][:, P * (i % 4):P * (i % 4) + P], h0[t % 3][:, i, :])
                    last.then_inc(sem("h0_turned"), 1)

                def outputs_turned(g):
                    pe.wait_ge(sem("yst_ready"), N_GRP * l + g + 1)
                    for t in range(GT * g, GT * g + GT):
                        last = turn(bank[7][:, NS * t:NS * t + NS], yst[g % 2][:, P * (t % GT):P * (t % GT) + P], NS)
                    last.then_inc(sem("yst_turned"), 1)

                state_turned(0)
                pe.wait_ge(sem("hout_ready"), 3 * (l + 1))
                pe.wait_ge(sem("wx_padded"), 2 * (l + 1))
                for t in range(ST):
                    pe.wait_ge(sem("bblk_ready"), N_GRP * l + t // GT + 1)
                    if t:
                        pe.wait_ge(sem("state_new"), ST * l + t)
                    for h in range(2):
                        last = mm(bank[4 + h][:, :], wx[:, P * t:P * t + P], bblk[:, 4 * h:4 * h + 4, :])
                    last.then_inc(sem("update_mm"), 1)
                    if t + 1 < ST:
                        state_turned(t + 1)
                    pe.wait_ge(sem("h0T_ready"), ST * l + t + 1)
                    pe.wait_ge(sem("calone_ready"), N_GRP * l + t // GT + 1)
                    if t % GT == 0 and t:
                        pe.wait_ge(sem("yst_ready"), N_GRP * l + t // GT)
                    for i in range(NB):
                        last = mm(bank[6][0:NS, P * (t % GT):P * (t % GT) + P], calone[:, NS * i:NS * i + NS],
                                  h0T[t % 2][:, i, :], i == 0, i == NB - 1)
                    last.then_inc(sem("yoff_mm"), 1)
                    if t % GT == 0 and t:
                        outputs_turned(t // GT - 1)
                outputs_turned(N_GRP - 1)
                pe.wait_ge(sem("sq_summed"), N_GRP * (l + 1))
                pe.wait_ge(sem("sq_summed_s"), l + 1)
                for g in range(N_GRP):
                    mm(bank[g][:, 0:T], ones, sq[:, GT * g, :]).then_inc(sem("rms_mm"), 1)
                b += U_WIN

                def rows(u, mh, ml, k0, start, stop):
                    pe.wait_ge(split_done, u.n + RING + 1)
                    for kk in range(2):
                        for d in range(KD):
                            wh = view(hi[u.slot], D)[:, kk, P * d:P * d + P]
                            wl = view(lo[u.slot], D)[:, kk, P * d:P * d + P]
                            kx = bass.ds(k0 + kk, 1) if not isinstance(k0, int) else slice(k0 + kk, k0 + kk + 1)
                            last = three(bank[d][:, 0:T], wh, wl, mh[:, kx, :], ml[:, kx, :],
                                         start and kk == 0, stop and kk == 1)
                            if stop and kk == 1 and d < KD - 1:
                                last.then_inc(sem("row_done"), 1)
                    last.then_inc(used, 1)

                pe.wait_ge(sem("rms_in"), N_GRP * (l + 1))
                for j in range(U_WOUT):
                    group = 0 if 2 * j + 1 < N_GRP else 1 + (2 * j + 1 - N_GRP) // GT
                    pe.wait_ge(sem("mix_ready"), 5 * l + group + 1)
                    rows(Unit(b + j), mixh, mixl, 2 * j, j == 0, j == U_WOUT - 1)
                b += U_WOUT

                def norm(v):
                    for d in range(KD):
                        pe.wait_ge(sem("ln_res"), KD * v + d + 1)
                        last = mm(bank[0][:, 0:T], ones, res[:, d, :], d == 0, d == KD - 1)
                    last.then_inc(sem("ln_mean"), 1)
                    for d in range(KD):
                        pe.wait_ge(sem("ln_sq"), 2 * v + d // 4 + 1)
                        last = mm(bank[1][:, 0:T], ones, lsq[:, d, :], d == 0, d == KD - 1)
                    last.then_inc(sem("ln_varmm"), 1)
                    pe.wait_ge(sem("ln_scaled"), KD * v + 1)

                norm(2 * l)
                if l == 0:
                    def pair(un, s, need):
                        pe.wait_ge(sem("hf_done"), need)
                        for x in range(2):
                            columns(un(x), 4 * s + 2 * x, lambda: None, KD)

                    with pe.Fori(0, 3) as i:
                        for j in range(3):
                            pair(lambda x: Unit(b + 2 * j + x, i, 6), FFN_SET[j], 3 * i + (1, 0, 2)[j])
                    for j in range(9, 11):
                        pair(lambda x: Unit(b + 2 * j + x), FFN_SET[j], j)
                    b += U_GU
                    pe.wait_ge(sem("hf_done"), 12)
                    pe.wait_ge(sem("hl_done"), 10)
                    for d in range(KD):
                        zero(bank[d][:, 0:T], T)
                    with pe.Fori(0, 3) as i:
                        for j in range(3):
                            rows(Unit(b + j, i, 3), hh, hl, 6 * i + 2 * j, False, False)
                    for j in range(9, U_DN):
                        pe.wait_ge(sem("hl_done"), j + 2)
                        rows(Unit(b + j), hh, hl, 2 * j, False, j == U_DN - 1)
                    norm(1)

            zero(bank[6][:, 0:3 * NE], 3 * NE)
            for k in range(KD):
                pe.wait_ge(sem("x_done"), 3 * KD + k + 1)
                for a in range(3):
                    n = P if a < 2 else NS
                    last = turn(bank[2 * a + k // 4][0:n, P * (k % 4):P * (k % 4) + P], xT[:, k, P * a:P * a + n])
                    if k % 4 == 3:
                        last.then_inc(sem("tok_turned"), 1)
                for a in range(3):
                    n = P if a < 2 else NS
                    last = add(bank[6][0:n, NE * a:NE * a + NE], xT[:, k, P * a:P * a + n], rw[:, k, :],
                               stop=(a == 2 and k == KD - 1))
            last.then_inc(sem("logit_mm"), 1)
            pe.wait_ge(sem("marks_ready"), 1)
            Mk = rt["M"]
            zero(bank[7][:, 0:64 + NE], 64 + NE)
            for a in range(3):
                for b_ in range(a):
                    add(bank[7][:, NE * a:NE * a + NE], ones, Mk[:, b_, :])
                add(bank[7][:, NE * a:NE * a + NE], stri, Mk[:, a, :])
                last = add(bank[7][:, 64:64 + NE], ones, Mk[:, a, :], stop=(a == 2))
            last.then_inc(sem("pos_mm"), 1)
            pe.wait_ge(sem("xtokl_done"), 7)
            pe.wait_ge(sem("acc_begun"), 6)
            pe.wait_ge(sem("count_ready"), 1)

            def gather(it, quarter):
                pe.wait_ge(sem("pick_ready"), 3 * it + 3)
                for k in (2 * quarter, 2 * quarter + 1):
                    for a in range(3):
                        n = P if a < 2 else NS
                        for x in (xtokh, xtokl):
                            last = mm(bank[XG[k // 4]][:, P * (k % 4):P * (k % 4) + P],
                                      x[0:n, a, P * k:P * k + P], pick[0:n, a, :],
                                      a == 0 and x is xtokh, a == 2 and x is xtokl)
                if quarter % 2:
                    last.then_inc(sem("xg_mm"), 1)

            def scatter(s, r, o):
                a, h = r // 2, r % 2
                w = slice(512 * h, 512 * h + 512)
                mm(o[:, :], back[:, P * a:P * a + P], yh[:, w], True, False)
                mm(o[:, :], back[:, P * a:P * a + P], yl[:, w], False, True).then_inc(sem("scat_mm"), 1)

            def clear_outputs():
                for h in range(2):
                    for w in range(2):
                        mm(bank[5 + h][:, 256 * w:256 * w + 256], zer[:, 0:P], zer[:, 0:1].to_broadcast([P, 256]))

            def item(it, s, b, e, per):
                def unit(j):
                    return Unit(b + j, e, per)

                pe.wait_ge(sem("xgh_done"), 2 * it + 2)
                pe.wait_ge(sem("xgl_done"), 2 * it + 2)

                def turns(c):
                    pe.wait_ge(sem("h_ready"), 6 * it + c + 1)
                    if c:
                        pe.wait_ge(sem("hTl_done"), 6 * it + c)
                    for f in range(FCH[c][1] // P):
                        last = turn(bank[4][:, P * f:P * f + P], hex_[c % 2][:, P * f:P * f + P])
                    last.then_inc(sem("hT_mm"), 1)

                for j in range(U_EXP):
                    u = unit(j)
                    kind, c, h = EXPERT[j]
                    pe.wait_ge(split_done, u.n + RING + 1)
                    w = FCH[c][1]
                    if kind in "gu":
                        if kind == "g" and c >= 2 and h != 1:
                            pe.wait_ge(sem("h_ready"), 6 * it + c - 1)
                        o = bank[c % 2 + (0 if kind == "g" else 2)][:, 0:w]
                        ks = range(4 * h, 4 * h + 4) if h < 2 else range(KD)
                        for i, k in enumerate(ks):
                            last = three_t(o, xgh[:, k, :], xgl[:, k, :], view(hi[u.slot], w)[:, i, :],
                                           view(lo[u.slot], w)[:, i, :], k == 0, k == KD - 1)
                    else:
                        if h != 1:
                            pe.wait_ge(sem("hTl_done"), 6 * it + c + 1)
                        nf = w // P
                        for y_ in ((h,) if h < 2 else (0, 1)):
                            vw = 512 if h < 2 else D
                            x0 = 0 if h < 2 else 512 * y_
                            for f in range(nf):
                                last = three_t(bank[5 + y_][:, :], hTh[c % 2][:, f, :], hTl[c % 2][:, f, :],
                                               view(hi[u.slot], vw)[:, f, x0:x0 + 512],
                                               view(lo[u.slot], vw)[:, f, x0:x0 + 512],
                                               c == 0 and f == 0, c == 5 and f == nf - 1)
                    last.then_inc(used, 1)
                    if kind == "g" and h and c:
                        turns(c - 1)
                    if (kind, c, h) == ("d", 4, 0):
                        turns(5)
                    if j in J_SCATTER:
                        r = J_SCATTER.index(j)
                        if r == 0:
                            pe.wait_ge(sem("yl_done"), 2 * s + 2)
                        pe.wait_ge(sem("acc_added"), 6 * s + r + 1)
                        scatter(s, r, bank[7])
                    if j == J_BACK:
                        pe.wait_ge(sem("acc_added"), 6 * s + 7)
                        for a in range(3):
                            n = P if a < 2 else NS
                            turn(bank[7][:, P * a:P * a + n], pick[0:n, a, :].bitcast(F32), n)
                        for a in range(3):
                            last = mm(bank[7][:, T:T + 1], pick[:, a, :].bitcast(F32), rt["G"][:, a, bass.ds(e, 1)],
                                      a == 0, a == 2)
                        last.then_inc(sem("back_mm"), 1)
                    if j in J_GATHER:
                        if j >= J_COPY - 2:
                            pe.wait_ge(sem("h_ready"), 6 * it + 5)
                        else:
                            pe.wait_ge(sem("back_done"), 2 * it + 2)
                        gather(it + 1, J_GATHER.index(j))

            def items(base, r):
                with pe.Fori(0, NE) as e:
                    item(e + base, e + base + r, U_MOE + base * U_EXP, e, U_EXP)
                s = base + NE + r
                pe.wait_ge(sem("yl_done"), 2 * s + 2)
                for k in range(6):
                    pe.wait_ge(sem("acc_added"), 6 * s + max(k - 4, -1) + 2)
                    scatter(s, k, bank[TAIL[k]])

            for quarter in range(4):
                gather(0, quarter)
            clear_outputs()
            items(0, 0)
            over = pe.value_load(cnti[0:1, 0:1], min_val=0, max_val=T)
            with pe.If(over > P):
                for r in range(2):
                    clear_outputs()
                    items(NE * (r + 1), r + 1)


_INS = ['x_prompt', 'x_sample', 'state_pool', 'state_conv', 'state_ssm', 'w_in', 'conv_w', 'conv_b', 'dt_bias',
        'A_log', 'D_skip', 'ssm_norm_w', 'pool_w', 'pool_scale', 'w_out', 'ln1_g', 'ln1_b', 'ln2_g', 'ln2_b',
        'ffn_w_gate', 'ffn_w_up', 'ffn_w_down', 'router_w', 'router_b', 'moe_w_gate', 'moe_w_up', 'moe_w_down']
_OUTS = [(1, SEQ, D), (NB, DL, D), (DEPTH, 1, PB, D_POOL), (DEPTH, 1, HIST, D_XBC), (DEPTH, 1, NH, HD, N_STATE),
         (DEPTH, NB, PB, D_POOL), (DEPTH, NB, HIST, D_XBC), (DEPTH, NB, NH, HD, N_STATE)]


def kernel(**inputs):
    import concourse.bacc as _bacc
    from concourse.bass_utils import run_bass_kernel_spmd as _run

    nc = _bacc.Bacc("TRN2", target_bir_lowering=False, num_devices=1)
    arrays, args = {}, []
    for name in _INS + ["consts"]:
        a = shape_constants() if name == "consts" else np.ascontiguousarray(inputs[name])
        arrays[f"in_{name}_dram"] = a
        args.append(nc.dram_tensor(f"in_{name}_dram", a.shape, mybir.dt.from_np(a.dtype), kind="ExternalInput").ap())
    for i, shape in enumerate(_OUTS):
        args.append(nc.dram_tensor(f"out_{i}_dram", shape, F32, kind="ExternalOutput").ap())
    trunk(nc, *args)
    r = _run(nc, [arrays], core_ids=[0])
    return tuple(r.results[0][f"out_{i}_dram"] for i in range(len(_OUTS)))
```
